# Optimizing a Trainium2 kernel written in Bass

```python
import math
import jax, jax.numpy as jnp
from jax import lax
import numpy as np

D_MODEL = 1024
BATCH = 1
SEQ = 512
DEPTH = 1
DEC_BATCH = 1
DEC_SEQ = 64
PAST_LEN = 256

EPS = 1e-6
F32 = jnp.float32

CHUNK = 64
N_PAST_CHUNKS = 8
BAND = (N_PAST_CHUNKS + 1) * CHUNK
WINDOW = N_PAST_CHUNKS * CHUNK

H_A = 8
DH_A = 64
WIDTH_A = H_A * DH_A
REL_CLIP = 128

H_B = 4
DK_B = 32
DV_B = 64
WIDTH_B = H_B * DV_B
GATE_RANK = 16
GATE_TAU = 16.0

H_C = 4
P_C = 64
WIDTH_C = H_C * P_C
N_GROUPS_C = 2
D_STATE = 64
CONV_W = 4
CONV_CH = WIDTH_C + 2 * N_GROUPS_C * D_STATE

D_MIX = WIDTH_A + WIDTH_B + WIDTH_C
IN_SPLIT = (WIDTH_A, WIDTH_A, WIDTH_A,
            H_B * DK_B, H_B * DK_B, WIDTH_B, GATE_RANK, WIDTH_B,
            WIDTH_C, CONV_CH, H_C)
IN_COLS = sum(IN_SPLIT)

N_EXPERT_GROUPS = 4
EXPERTS_PER_GROUP = 4
N_EXPERTS = N_EXPERT_GROUPS * EXPERTS_PER_GROUP
TOP_K_IN_GROUP = 2
D_EXPERT = 256

kernel_name = 'hybrid_streaming_encoder_step'

def rms_norm(x, w):
    xf = x.astype(F32)
    y = xf * lax.rsqrt(jnp.mean(xf * xf, axis=-1, keepdims=True) + EPS) * w.astype(F32)
    return y.astype(x.dtype)

def chunked_scan(step, s0, xs):
    L = xs[0].shape[1]
    blk = min(CHUNK, L)
    n = L // blk

    def to_blocks(t):
        return jnp.moveaxis(t.reshape(t.shape[0], n, blk, *t.shape[2:]), 1, 0)

    s, ys = lax.scan(step, s0, tuple(to_blocks(t) for t in xs))
    ys = jnp.moveaxis(ys, 0, 1)
    return s, ys.reshape(ys.shape[0], L, *ys.shape[3:])

def rel_bias(table, rel):
    return table[:, jnp.clip(rel, -REL_CLIP, REL_CLIP) + REL_CLIP].astype(F32)

def band_attention(q, k, v, bias, valid):
    s = jnp.einsum('bnqhd,bnkhd->bnhqk', q, k).astype(F32) * (DH_A ** -0.5) + bias
    s = jnp.where(valid[None, :, None], s, -1e30)
    p = jax.nn.softmax(s, axis=-1).astype(v.dtype)
    return jnp.einsum('bnhqk,bnkhd->bnqhd', p, v)

def band_attention_prompt(q, k, v, table):
    bsz, S = q.shape[:2]
    nc = S // CHUNK

    def band(t):
        tc = t.reshape(bsz, nc, CHUNK, H_A, DH_A)
        tp = jnp.pad(tc, ((0, 0), (N_PAST_CHUNKS, 0), (0, 0), (0, 0), (0, 0)))
        return jnp.concatenate([tp[:, j:j + nc] for j in range(N_PAST_CHUNKS + 1)], axis=2)

    qi = jnp.arange(CHUNK)
    kj = jnp.arange(BAND)
    rel = qi[:, None] + WINDOW - kj[None, :]
    k_pos = (jnp.arange(nc)[:, None] - N_PAST_CHUNKS) * CHUNK + kj[None, :]
    valid = jnp.broadcast_to((k_pos >= 0)[:, None, :], (nc, CHUNK, BAND))
    out = band_attention(q.reshape(bsz, nc, CHUNK, H_A, DH_A), band(k), band(v),
                         rel_bias(table, rel), valid)
    return out.reshape(bsz, S, WIDTH_A)

def band_attention_sample(q, k, v, ck, cv, table):
    bsz, L = q.shape[:2]
    lc = ck.shape[1]
    kk = jnp.concatenate([ck.astype(k.dtype), k], axis=1)[:, None]
    vv = jnp.concatenate([cv.astype(v.dtype), v], axis=1)[:, None]
    q_pos = lc + jnp.arange(L)
    k_pos = jnp.arange(lc + L)
    valid = jnp.ones((1, L, lc + L), bool)
    out = band_attention(q[:, None], kk, vv, rel_bias(table, q_pos[:, None] - k_pos[None, :]), valid)
    return out.reshape(bsz, L, WIDTH_A)

def gla_block(s, blk):
    q, k, v, g = blk
    L = q.shape[1]
    b = jnp.cumsum(g, axis=1)
    causal = jnp.tril(jnp.ones((L, L), bool))[None, :, :, None, None]
    decay = jnp.exp(jnp.where(causal, b[:, :, None] - b[:, None, :], -jnp.inf))
    att = jnp.einsum('bthk,bshk,btshk->bhts', q, k, decay)
    o = jnp.einsum('bhts,bshv->bthv', att, v) + jnp.einsum('bthk,bhkv->bthv', q * jnp.exp(b), s)
    b_last = b[:, -1]
    s_new = jnp.exp(b_last)[..., None] * s + jnp.einsum('bshk,bshv->bhkv', k * jnp.exp(b_last[:, None] - b), v)
    return s_new, o

def ssd_block(h, blk):
    x, dt, a, bm, cm = blk
    L = x.shape[1]
    bh = jnp.repeat(bm, H_C // N_GROUPS_C, axis=2)
    ch = jnp.repeat(cm, H_C // N_GROUPS_C, axis=2)
    cs = jnp.cumsum(a, axis=1)
    causal = jnp.tril(jnp.ones((L, L), bool))[None, :, :, None]
    decay = jnp.exp(jnp.where(causal, cs[:, :, None] - cs[:, None, :], -jnp.inf))
    scores = jnp.einsum('bthn,bshn->btsh', ch, bh) * decay
    y = (jnp.einsum('btsh,bshp->bthp', scores, x * dt[..., None])
         + jnp.einsum('bthn,bhpn->bthp', ch, h) * jnp.exp(cs)[..., None])
    cs_last = cs[:, -1]
    w = jnp.exp(cs_last[:, None] - cs) * dt
    h_new = jnp.exp(cs_last)[:, :, None, None] * h + jnp.einsum('bsh,bshp,bshn->bhpn', w, x, bh)
    return h_new, y

def mixer_block(h, w_in, rel_table, gla_w_gate_up, gla_b_gate, gla_norm_w, conv_w, conv_b,
                dt_bias, a_log, d_skip, ssm_norm_w, w_out, cache_k, cache_v, gla_s0, conv_s0, ssm_s0):
    bsz, L, _ = h.shape
    proj = h @ w_in
    offsets = np.cumsum(IN_SPLIT)[:-1].tolist()
    aq, ak, av, bq, bk, bv, bglr, bog, cz, cxbc, cdt = jnp.split(proj, offsets, axis=-1)

    def heads(t, n):
        return t.reshape(bsz, L, n, -1)

    q, k, v = heads(aq, H_A), heads(ak, H_A), heads(av, H_A)
    if cache_k is None:
        att = band_attention_prompt(q, k, v, rel_table)
        keep = min(WINDOW, L)
        k_keep, v_keep = k[:, L - keep:], v[:, L - keep:]
    else:
        att = band_attention_sample(q, k, v, cache_k, cache_v, rel_table)
        k_keep, v_keep = k, v

    gq = heads(bq, H_B).astype(F32) * (DK_B ** -0.5)
    gk = heads(bk, H_B).astype(F32)
    gv = heads(bv, H_B).astype(F32)
    glog = jax.nn.log_sigmoid((bglr @ gla_w_gate_up + gla_b_gate).astype(F32)) / GATE_TAU
    gla_s, go = chunked_scan(gla_block, gla_s0.astype(F32), (gq, gk, gv, heads(glog, H_B)))
    go = rms_norm(go, gla_norm_w) * jax.nn.silu(heads(bog, H_B).astype(F32))
    gla_out = go.reshape(bsz, L, WIDTH_B)

    xpad = jnp.concatenate([conv_s0.astype(cxbc.dtype), cxbc], axis=1)
    conv = conv_b + sum(xpad[:, i:i + L] * conv_w[i] for i in range(CONV_W))
    conv = jax.nn.silu(conv.astype(F32))
    conv_s = xpad[:, L:]
    sx, sb, sc = jnp.split(conv, [WIDTH_C, WIDTH_C + N_GROUPS_C * D_STATE], axis=-1)
    sx = sx.reshape(bsz, L, H_C, P_C)
    sb = sb.reshape(bsz, L, N_GROUPS_C, D_STATE)
    sc = sc.reshape(bsz, L, N_GROUPS_C, D_STATE)
    dt = jax.nn.softplus(cdt.astype(F32) + dt_bias.astype(F32))
    a = -jnp.exp(a_log.astype(F32)) * dt
    ssm_s, sy = chunked_scan(ssd_block, ssm_s0.astype(F32), (sx, dt, a, sb, sc))
    sy = sy + d_skip.astype(F32)[:, None] * sx
    sy = sy.reshape(bsz, L, WIDTH_C) * jax.nn.silu(cz.astype(F32))
    gsz = WIDTH_C // N_GROUPS_C
    sy = rms_norm(sy.reshape(bsz, L, N_GROUPS_C, gsz), ssm_norm_w.reshape(N_GROUPS_C, gsz))
    ssm_out = sy.reshape(bsz, L, WIDTH_C)

    mixed = jnp.concatenate([att.astype(h.dtype), gla_out.astype(h.dtype), ssm_out.astype(h.dtype)], axis=-1)
    return mixed @ w_out, k_keep, v_keep, gla_s, conv_s, ssm_s

def hier_moe(h, w_rg, b_rg, w_re, b_re, w_gate, w_up, w_down):
    bsz, L, _ = h.shape
    hf = h.astype(F32)
    lg = hf @ w_rg.astype(F32) + b_rg.astype(F32)
    g_idx = jnp.argmax(lg, axis=-1)
    p_grp = jnp.take_along_axis(jax.nn.softmax(lg, axis=-1), g_idx[..., None], axis=-1)
    le = (hf @ w_re.astype(F32) + b_re.astype(F32)).reshape(bsz, L, N_EXPERT_GROUPS, EXPERTS_PER_GROUP)
    le = jnp.take_along_axis(le, g_idx[..., None, None], axis=2)[:, :, 0]
    top_v, top_i = lax.top_k(le, TOP_K_IN_GROUP)
    w_sel = jax.nn.softmax(top_v, axis=-1) * p_grp
    e_id = g_idx[..., None] * EXPERTS_PER_GROUP + top_i
    gate = jnp.sum(jax.nn.one_hot(e_id, N_EXPERTS, dtype=F32) * w_sel[..., None], axis=-2)
    hid = jax.nn.silu(jnp.einsum('bld,edf->blef', h, w_gate)) * jnp.einsum('bld,edf->blef', h, w_up)
    hid = hid * gate.astype(h.dtype)[..., None]
    return jnp.einsum('blef,efd->bld', hid, w_down)

def setup_inputs(seed: int = 0) -> dict:
    key = jax.random.key(seed)
    ks = iter(jax.random.split(key, 40))

    def nrm(shape, scale):
        return jax.random.normal(next(ks), shape, F32) * scale

    att_len = min(WINDOW, PAST_LEN)
    dt0 = jnp.exp(jax.random.uniform(next(ks), (DEPTH, H_C), F32, math.log(1e-3), math.log(1e-1)))
    dt_bias = dt0 + jnp.log(-jnp.expm1(-dt0))
    a_log = jnp.log(jax.random.uniform(next(ks), (DEPTH, H_C), F32, 1.0, 16.0))
    return {
        'x_prompt': nrm((BATCH, SEQ, D_MODEL), 1.0),
        'x_sample': nrm((DEC_BATCH, DEC_SEQ, D_MODEL), 1.0),
        'cache_k_a': nrm((DEPTH, DEC_BATCH, att_len, H_A, DH_A), 1.0),
        'cache_v_a': nrm((DEPTH, DEC_BATCH, att_len, H_A, DH_A), 1.0),
        'state_gla': nrm((DEPTH, DEC_BATCH, H_B, DK_B, DV_B), 0.5),
        'state_conv': nrm((DEPTH, DEC_BATCH, CONV_W - 1, CONV_CH), 1.0),
        'state_ssm': nrm((DEPTH, DEC_BATCH, H_C, P_C, D_STATE), 0.5),
        'norm1_w': 1.0 + nrm((DEPTH, D_MODEL), 0.02),
        'w_in': nrm((DEPTH, D_MODEL, IN_COLS), D_MODEL ** -0.5),
        'rel_bias_table': nrm((DEPTH, H_A, 2 * REL_CLIP + 1), 0.5),
        'gla_w_gate_up': nrm((DEPTH, GATE_RANK, H_B * DK_B), GATE_RANK ** -0.5),
        'gla_b_gate': nrm((DEPTH, H_B * DK_B), 0.1),
        'gla_norm_w': 1.0 + nrm((DEPTH, DV_B), 0.02),
        'ssm_conv_w': nrm((DEPTH, CONV_W, CONV_CH), CONV_W ** -0.5),
        'ssm_conv_b': nrm((DEPTH, CONV_CH), 0.02),
        'ssm_dt_bias': dt_bias,
        'ssm_a_log': a_log,
        'ssm_d': 1.0 + nrm((DEPTH, H_C), 0.02),
        'ssm_norm_w': 1.0 + nrm((DEPTH, WIDTH_C), 0.02),
        'w_out': nrm((DEPTH, D_MIX, D_MODEL), D_MIX ** -0.5),
        'norm2_w': 1.0 + nrm((DEPTH, D_MODEL), 0.02),
        'router_group_w': nrm((DEPTH, D_MODEL, N_EXPERT_GROUPS), D_MODEL ** -0.5),
        'router_group_b': nrm((DEPTH, N_EXPERT_GROUPS), 0.01),
        'router_expert_w': nrm((DEPTH, D_MODEL, N_EXPERTS), D_MODEL ** -0.5),
        'router_expert_b': nrm((DEPTH, N_EXPERTS), 0.01),
        'exp_w_gate': nrm((DEPTH, N_EXPERTS, D_MODEL, D_EXPERT), D_MODEL ** -0.5),
        'exp_w_up': nrm((DEPTH, N_EXPERTS, D_MODEL, D_EXPERT), D_MODEL ** -0.5),
        'exp_w_down': nrm((DEPTH, N_EXPERTS, D_EXPERT, D_MODEL), D_EXPERT ** -0.5),
        'final_norm_w': 1.0 + nrm((D_MODEL,), 0.02),
    }

def reference(x_prompt, x_sample, cache_k_a, cache_v_a, state_gla, state_conv, state_ssm,
              norm1_w, w_in, rel_bias_table, gla_w_gate_up, gla_b_gate, gla_norm_w,
              ssm_conv_w, ssm_conv_b, ssm_dt_bias, ssm_a_log, ssm_d, ssm_norm_w, w_out,
              norm2_w, router_group_w, router_group_b, router_expert_w, router_expert_b,
              exp_w_gate, exp_w_up, exp_w_down, final_norm_w):
    xp, xs = x_prompt, x_sample
    bp = xp.shape[0]
    pk, pv, pg, pc, ps = [], [], [], [], []
    sk, sv, sg, sc, ss = [], [], [], [], []
    for i in range(DEPTH):
        mix_w = (w_in[i], rel_bias_table[i], gla_w_gate_up[i], gla_b_gate[i], gla_norm_w[i],
                 ssm_conv_w[i], ssm_conv_b[i], ssm_dt_bias[i], ssm_a_log[i], ssm_d[i],
                 ssm_norm_w[i], w_out[i])
        moe_w = (router_group_w[i], router_group_b[i], router_expert_w[i], router_expert_b[i],
                 exp_w_gate[i], exp_w_up[i], exp_w_down[i])
        mo, k_new, v_new, g_s, c_s, s_s = mixer_block(
            rms_norm(xp, norm1_w[i]), *mix_w, None, None,
            jnp.zeros((bp, H_B, DK_B, DV_B), F32),
            jnp.zeros((bp, CONV_W - 1, CONV_CH), xp.dtype),
            jnp.zeros((bp, H_C, P_C, D_STATE), F32))
        xp = xp + mo
        xp = xp + hier_moe(rms_norm(xp, norm2_w[i]), *moe_w)
        pk.append(k_new); pv.append(v_new); pg.append(g_s); pc.append(c_s); ps.append(s_s)
        mo, k_new, v_new, g_s, c_s, s_s = mixer_block(
            rms_norm(xs, norm1_w[i]), *mix_w, cache_k_a[i], cache_v_a[i],
            state_gla[i], state_conv[i], state_ssm[i])
        xs = xs + mo
        xs = xs + hier_moe(rms_norm(xs, norm2_w[i]), *moe_w)
        sk.append(k_new); sv.append(v_new); sg.append(g_s); sc.append(c_s); ss.append(s_s)
    y_prompt = rms_norm(xp, final_norm_w)
    y_sample = rms_norm(xs, final_norm_w)
    return (y_prompt, y_sample,
            jnp.stack(pk), jnp.stack(pv), jnp.stack(pg), jnp.stack(pc), jnp.stack(ps),
            jnp.stack(sk), jnp.stack(sv), jnp.stack(sg), jnp.stack(sc), jnp.stack(ss))


_drawn_inputs = setup_inputs


def setup_inputs(seed=0):
    import zlib

    import numpy as np

    out = dict(_drawn_inputs(seed))
    spreads = {}
    factors = {'gla_norm_w': 11.53,
     'ssm_d': 42.354,
     'router_group_b': 4.165,
     'router_expert_b': 17.199,
     'final_norm_w': 7.468,
     'ssm_norm_w': 5.52,
     'norm2_w': 3.282}
    for name, (base, spread) in spreads.items():
        noise = np.random.default_rng([zlib.crc32(name.encode()), seed]).standard_normal(out[name].shape)
        drawn = base * np.exp(spread * noise) if base else spread * noise
        out[name] = __import__('jax').numpy.asarray(drawn.astype(out[name].dtype))
    for name, factor in factors.items():
        out[name] = (out[name] * factor).astype(out[name].dtype)
    return out
```

```python
from contextlib import ExitStack

import concourse.bass as bass
import numpy as np
from concourse import mybir
from concourse.alu_op_type import AluOpType as ALU

ACT = mybir.ActivationFunctionType
AX = mybir.AxisListType
F32 = mybir.dt.float32
I32 = mybir.dt.int32
U32 = mybir.dt.uint32
P = 128


def encoder_layer(nc, ins, outs):
    (x_prompt, x_sample, cache_k, cache_v, state_gla, state_conv, state_ssm, norm1_w, w_in, rel_table,
     gate_up, b_gate, gla_norm_w, conv_w, conv_b, dt_bias, a_log, d_skip, ssm_norm_w, w_out, norm2_w,
     rg_w, rg_b, re_w, re_b, exp_gate, exp_up, exp_down, final_w) = ins
    (y_prompt, y_sample, o_pk, o_pv, o_pg, o_pc, o_ps, o_sk, o_sv, o_sg, o_sc, o_ss) = outs

    D = x_prompt.shape[2]
    SEQ, DEC = x_prompt.shape[1], x_sample.shape[1]
    KD = D // P
    NT = SEQ // P + 1
    TOK = SEQ + DEC
    ROWS = [P] * (NT - 1) + [DEC]
    T0 = [P * i for i in range(NT)]
    HA, DH = cache_k.shape[3], cache_k.shape[4]
    WA = HA * DH
    PAST = cache_k.shape[2]
    HB, DK, DV = state_gla.shape[2:]
    HC, PC, NS = state_ssm.shape[2:]
    TAPS, CH = conv_w.shape[1:]
    NE, _, FE = exp_gate.shape[1:]
    NG = rg_w.shape[2]
    EG = NE // NG
    RANK = gate_up.shape[1]
    EPS = 1e-6
    NEG = -1e30
    CLIP = (rel_table.shape[2] - 1) // 2
    CAP = P
    ROUNDS = -(-TOK // CAP)
    MORE = (ROUNDS - 1) * NE
    SPAN = NE * CAP
    assert (D, SEQ, DEC, PAST, CLIP) == (1024, 512, 64, 256, 128) and WA == 512 and CH == 512

    C_Q, C_K, C_V = 0, WA, 2 * WA
    C_BQ = 3 * WA
    C_BK = C_BQ + HB * DK
    C_BV = C_BK + HB * DK
    C_LR = C_BV + HB * DV
    C_OG = C_LR + RANK
    C_Z = C_OG + HB * DV
    C_XBC = C_Z + HC * PC
    C_DT = C_XBC + CH
    COLS = C_DT + HC

    with ExitStack() as ctx:
        sems = {}

        def S(name):
            if name not in sems:
                sems[name] = ctx.enter_context(nc.semaphore(name))
            return sems[name]

        place = [0]

        def sb(name, shape, dt=F32, at=None):
            size = int(np.prod(shape[1:])) * 4
            if at is None:
                at = place[0]
                place[0] += -(-size // 32) * 32
            return nc.alloc_sbuf_tensor_at(name, shape, dt, offset=base + at), at, at + size

        base = -(-nc.sbuf_base // 32) * 32

        SLOT_W = 528
        NSLOT = 3
        wring, _, _ = sb("weight_ring", [P, NSLOT, KD * SLOT_W])
        down, down_at, down_end = sb("down_ring", [P, 2, FE // P * D])
        ident, _, _ = sb("ident", [P, P])
        triu, _, _ = sb("triu", [P, P])
        striu, _, _ = sb("striu", [P, P])
        ones, _, _ = sb("ones", [P, P])
        par, _, _ = sb("params_T", [P, 64])
        small, _, _ = sb("small", [P, 256])
        hT, hT_at, hT_end = sb("hT", [P, KD, TOK])
        mixT, mixT_at, e = sb("mixT", [P, KD, TOK])
        cso, _, e = sb("conv_state_out", [4, 2, CH], at=mixT_at)
        sto, _, e = sb("ssd_state_out", [PC, 2, 2 * P], at=e)
        assert e <= mixT_at + 4 * WA // P * TOK
        iot, _, e = sb("iota", [P, 2, P], I32, at=mixT_at + 4 * WA // P * TOK)
        lvf, _, e = sb("level_compare", [P, 3, P], at=e)
        prow, _, e = sb("params_rows", [64, P], at=e)
        gth, _, e = sb("gates_tanh", [P, 2, 512], at=e)
        assert e <= mixT_at + 4 * KD * TOK
        stage, stage_at, _ = sb("stage", [P, 2, D])
        mixer_at = place[0]
        kB, _, _ = sb("gla_kT", [P, TOK])
        qB, _, _ = sb("gla_qT", [P, TOK])
        bcum, _, _ = sb("gla_b", [P, TOK])
        wup, _, _ = sb("gla_w_up", [RANK, HB * DK])
        qbd, _, _ = sb("gla_q_blocks", [P, HB, P])
        qE, _, _ = sb("gla_q_decayed", [P, 2, HB, P])
        kE, _, _ = sb("gla_k_decayed", [P, 2, P])
        dif, _, _ = sb("gla_exponents", [P, 2, P])
        att, _, _ = sb("gla_scores", [P, HB, P])
        qs, _, _ = sb("gla_q_from_start", [P, P])
        kd, _, _ = sb("gla_k_to_end", [P, P])
        kdn, _, _ = sb("gla_k_to_end_nat", [P, P])
        Sg, _, _ = sb("gla_state", [P, 2, HB, DV])
        bv, _, _ = sb("gla_v", [P, NT, HB * DV])
        ogz, _, _ = sb("gates", [P, NT, HB * DV + HC * PC])
        lmask, _, _ = sb("level_masks", [P, 8, P], mybir.dt.uint8)
        gv, _, _ = sb("gla_o", [P, HB * DV])
        gt, _, _ = sb("gla_o_tmp", [P, HB * DV])
        xpre, _, e = sb("conv_in", [P, CH // P, TOK + 6], at=down_at)
        ctmp, _, e = sb("conv_sum", [P, 2, TOK + 4], at=e + (-e) % 32)
        thx, _, e = sb("conv_tanh", [P, TOK + 4], at=e + (-e) % 32)
        assert e <= down_end
        xnat, _, _ = sb("xB_nat", [P, 3 * P])
        dec, _, _ = sb("ssd_decay", [P, HC, P])
        cbm, _, _ = sb("ssd_cb", [P, 2, P])
        xdt, _, _ = sb("ssd_x_dt", [P, HC, PC])
        xw, _, _ = sb("ssd_x_w", [P, HC, PC])
        xD, _, _ = sb("ssd_x_skip", [P, HC, PC])
        hst, _, _ = sb("ssd_state", [P, 2, 2, PC])
        yv, _, _ = sb("ssd_y", [P, HC * PC])
        yt, _, _ = sb("ssd_tmp", [P, HC * PC])
        xc, xc_at, xc_end = sb("conv_out", [P, CH // P, TOK + 4])
        ckT, _, e = sb("att_cached_kT", [P, WA // P, PAST], at=xc_at)
        cv, _, e = sb("att_cached_v", [P, PAST // P, WA], at=e)
        assert e <= xc_end
        qT, qT_at, _ = sb("att_qT", [P, WA // P, TOK])
        kT, kT_at, kT_end = sb("att_kT", [P, WA // P, TOK])
        V, _, _ = sb("att_v", [P, NT, WA])
        mixer_end = place[0]
        rtab, _, _ = sb("bias_table", [HA, 2 * CLIP + 1], at=qT_at)
        xrel, _, e = sb("bias_table_long", [HA, 384], at=qT_at + 1056)
        gtmp, _, e = sb("gla_tmp", [P, 2, TOK], at=kT_at)
        lrT, _, e = sb("gla_lowrank", [RANK, TOK], at=e)
        assert e <= kT_end
        bias, _, e = sb("att_bias", [P, HA, 2 * P], at=hT_at)
        Pm, _, e = sb("att_p", [P, 2, 512], at=e)
        PT, _, e = sb("att_pT", [P, 2, 512], at=e)
        assert e <= hT_end
        x1, _, e = sb("x1", [P, NT, D], at=mixer_at)
        h2, _, e = sb("h2", [P, 2, D], at=e)
        w2b, _, e = sb("norm2_b", [P, D], at=e)
        wfb, _, e = sb("final_b", [P, D], at=e)
        assert e <= xc_at, (e, xc_at)
        xg, _, e = sb("expert_x", [P, 2, D], at=e)
        xgT, _, e = sb("expert_xT", [P, 2, KD, CAP], at=e)
        sg, _, e = sb("expert_silu", [P, 2, FE], at=e)
        hid, _, e = sb("expert_hidden", [P, 2, FE], at=e)
        hidT, _, e = sb("expert_hiddenT", [P, 2, FE // P, CAP], at=e)
        ye, _, e = sb("expert_y", [P, 2, D], at=e)
        rt, _, e = sb("router", [P, 20, NT, NE], at=e)
        lgt, _, e = sb("router_logits", [P, NT, NG + NE], at=e)
        moe_end = e
        rw, _, _ = sb("router_w", [P, KD, NG + NE])
        rb, _, _ = sb("router_b", [P, NG + NE])
        desc, _, _ = sb("router_order", [P, 4])
        ebase, _, _ = sb("expert_base", [P, NE])
        ri, _, _ = sb("router_index", [P, 64], I32)
        idi, _, _ = sb("ids_rows", [NE, CAP], I32)
        idf, _, _ = sb("ids_rows_f", [NE, CAP])
        zmap, _, _ = sb("zero_map", [P, ROUNDS * SPAN // P], I32)
        dtw, _, _ = sb("dt_work", [P, 10, NT * HC])
        assert moe_end <= mixer_end, (moe_end, mixer_end)
        assert base + place[0] <= nc.sbuf_usable_end

        A_SSQ, A_MS, A_RS, A_MH = 0, 8, 16, 24
        A_NA, A_DTB, A_D, A_AL = 44, 48, 52, 56
        A_A, A_CS, A_DT = 60, 80, 100
        A_CSL, A_ECL, A_W, A_ECS = 120, 124, 128, 132
        A_NM, A_SUM, A_RSUM = 136, 140, 156
        A_GS, A_GR, A_YS, A_YR, A_EBL = 172, 176, 180, 182, 184
        A_MAX = 186
        A_SLOT1, A_SLOT2 = 192, 200
        (R_EQ, R_OHG, R_SUB, R_TMP, R_SEL, R_K1, R_K2, R_L2, R_A1, R_A2, R_A, R_POS, R_V, R_X, R_SLOT) = range(15)

        bank = [ctx.enter_context(nc.psum_tensor(f"bank{b}", [P, 512], F32)) for b in range(8)]

        relpos_d = nc.dram_tensor("relative_bias", [HA, 384], F32, kind="Internal").ap()
        h2_d = nc.dram_tensor("h2_rows", [TOK, D], F32, kind="Internal").ap()
        map_d = nc.dram_tensor("slot_tokens", [ROUNDS * SPAN, 1], I32, kind="Internal").ap()
        y_d = nc.dram_tensor("slot_outputs", [ROUNDS * SPAN, D], F32, kind="Internal").ap()

        G1, G2, GCW, GCB, GBG, GGN, GSN, GCS = 0, 8, 16, 32, 36, 37, 38, 40
        NPAR = 52

        block = ctx.enter_context(nc.Block())

        fills, count, full_count = {}, [0] * 8, [0] * 8

        def tile_x(i, lo=0, hi=None):
            hi = D if hi is None else hi
            return x_prompt[0, T0[i]:T0[i] + P, lo:hi] if i < NT - 1 else x_sample[0, :, lo:hi]

        groups = [(C_BQ, 512), (C_LR, RANK + 512), (C_XBC, CH + HC), (C_Q, WA), (C_K, WA), (C_V, WA)]
        G_B, G_LR, G_XBC, G_Q, G_K, G_V, G_WO0, G_WO1, G_EXP = range(9)

        def ring(g, width):
            return wring[:, g % NSLOT, 0:KD * width].rearrange("p (k c) -> p k c", k=KD)

        def w_done(g):
            return sum(16 if k < G_EXP else 32 for k in range(g % NSLOT, g + 1, NSLOT))

        LEV = [64, 32, 16, 8, 4, 2, 1]

        def levels(i):
            return [m for m in LEV if 2 * m <= ROWS[i]] + [0]

        def seq(i):
            return i // (NT - 1)

        def nkeys(i):
            return T0[i] + P if i < NT - 1 else PAST + DEC

        def cols(i):
            c = T0[i] + (3 if i == NT - 1 else 0)
            return slice(c, c + ROWS[i])

        lev_key = [("lev", i, n) for i in range(NT) for n in range(len(levels(i)) - 1)]
        n_lev = [sum(len(levels(j)) for j in range(i)) for i in range(NT + 1)]

        def full(eng, key):
            b, n, _ = fills[key]
            eng.wait_ge(S(f"bank{b}_full"), n)
            return bank[b]

        def filled(eng, key):
            full(eng, key)

        def drained(eng, key):
            b, _, n = fills[key]
            eng.wait_ge(S(f"bank{b}_free"), n)

        def free(ins, key):
            ins.then_inc(S(f"bank{fills[key][0]}_free"), 1)

        @block.tensor
        def _(pe):
            mm, tr = nc.tensor.matmul, nc.tensor.transpose

            def fill(key, b):
                if count[b] > 0:
                    pe.wait_ge(S(f"bank{b}_free"), count[b])
                count[b] += 1
                full_count[b] += 1
                fills[key] = (b, full_count[b], count[b])
                return bank[b]

            def done(ins, key):
                ins.then_inc(S(f"bank{fills[key][0]}_full"), 1)

            pe.wait_ge(S("consts"), 1)
            pe.wait_ge(S("params_in"), 16 * 9)
            o = fill("par", 4)
            done(tr(o[:, 0:NPAR], prow[0:NPAR, :], ident[0:NPAR, 0:NPAR]), "par")
            for i in range(NT):
                r = ROWS[i]
                pe.wait_ge(S("x_normed"), i + 1)
                for hf in range(2):
                    o = fill(("xT", i, hf), 2 + hf)
                    for k in range(4):
                        last = tr(o[:, k * r:k * r + r], stage[0:r, i % 2, (4 * hf + k) * P:(4 * hf + k + 1) * P], ident[0:r, 0:r])
                    done(last, ("xT", i, hf))
            pe.wait_ge(S("state_in"), 16 * HC)
            o = fill("s0T", 4)
            for j in range(2):
                last = tr(o[:, j * PC:(j + 1) * PC], yt[0:PC, j * P:(j + 1) * P], ident[0:PC, 0:PC])
            done(last, "s0T")
            drained(pe, ("xT", NT - 1, 0))
            drained(pe, ("xT", NT - 1, 1))

            def proj_T(key, w, c0, m, toks, b, first_col=0):
                for k in range(KD):
                    last = mm(bank[b][0:m, first_col:first_col + toks.stop - toks.start], w[:, k, c0:c0 + m],
                              hT[:, k, toks], start=(k == 0), stop=(k == KD - 1))
                return last

            def proj_nat(w, c0, n, i, b, col=0):
                for k in range(KD):
                    last = mm(bank[b][0:ROWS[i], col:col + n], hT[:, k, T0[i]:T0[i] + ROWS[i]], w[:, k, c0:c0 + n],
                              start=(k == 0), stop=(k == KD - 1))
                return last

            PR, SA = slice(0, SEQ), slice(SEQ, TOK)

            def landed(g):
                pe.wait_ge(S(f"w{g % NSLOT}_in"), w_done(g))

            landed(G_B)
            w = ring(G_B, 512)
            for j, nm in enumerate(("bq", "bk")):
                fill(nm, j)
                done(proj_T(nm, w, j * P, P, PR, j), nm)
            fill("bqk_s", 2)
            proj_T("bqk_s", w, 0, P, SA, 2, 0)
            done(proj_T("bqk_s", w, P, P, SA, 2, DEC), "bqk_s")
            for i in range(NT):
                fill(("bv", i), i % 2)
                last = proj_nat(w, 2 * P, HB * DV, i, i % 2)
                done(last, ("bv", i))
            landed(G_LR)
            w = ring(G_LR, RANK + 512)
            fill("lr", 2)
            done(proj_T("lr", w, 0, RANK, PR, 2), "lr")
            fill("lr_s", 3)
            done(proj_T("lr_s", w, 0, RANK, SA, 3), "lr_s")
            for i in range(NT):
                fill(("ogz", i), i % 2)
                done(proj_nat(w, RANK, 512, i, i % 2), ("ogz", i))
            landed(G_XBC)
            w = ring(G_XBC, CH + HC)
            for j in range(4):
                fill(("xbc", j), j % 2)
                done(proj_T("", w, j * P, P, PR, j % 2), ("xbc", j))
            fill("xbc_s", 0)
            for j in range(4):
                last = proj_T("", w, j * P, P, SA, 0, j * DEC)
            done(last, "xbc_s")
            fill("dt", 2)
            for i in range(NT):
                last = proj_nat(w, CH, HC, i, 2, i * HC)
            done(last, "dt")

            def gla_gate():
                drained(pe, "lr")
                drained(pe, "lr_s")
                pe.wait_ge(S("wup_in"), 16)
                o = fill("gate", 2)
                done(mm(o[:, 0:SEQ], wup[:, :], lrT[:, 0:SEQ], start=True, stop=True), "gate")
                o = fill("gate_s", 3)
                done(mm(o[:, 0:DEC], wup[:, :], lrT[:, SEQ:TOK], start=True, stop=True), "gate_s")

            def ssd_cums():
                pe.wait_ge(S("a_ready"), 1)
                o = fill("cs", 2)
                for i in range(NT):
                    r = ROWS[i]
                    last = mm(o[0:r, i * HC:(i + 1) * HC], triu[0:r, 0:r], small[0:r, A_A + i * HC:A_A + (i + 1) * HC],
                              start=True, stop=True)
                done(last, "cs")

            def conv_state():
                drained(pe, "xbc_s")
                drained(pe, ("xbc", 3))
                pe.wait_ge(S("conv_state_placed"), 1)
                for s, c in ((0, SEQ), (1, TOK + 3)):
                    o = fill(("cst", s), 3)
                    for j in range(4):
                        last = tr(o[0:3, j * P:(j + 1) * P], xpre[:, j, c:c + 3], ident[:, :])
                    done(last, ("cst", s))

            def gla_levels(i):
                r = ROWS[i]
                for n, m in enumerate(levels(i)):
                    b = 4 + n % 2
                    o = fill(("lev", i, n), b)
                    if m:
                        c = n_lev[i] - i + n
                        pe.wait_ge(S("k_decayed"), c + 1)
                        pe.wait_ge(S("q_decayed"), c + 1)
                        last = mm(o[0:r, 0:HB * r], kE[:, c % 2, 0:r], qE[:, c % 2, :, 0:r], start=True, stop=True)
                    else:
                        pe.wait_ge(S("q_blocks"), i + 1)
                        last = mm(o[0:r, 0:HB * r], kB[:, T0[i]:T0[i] + r], qbd[:, :, 0:r], start=True, stop=True)
                    done(last, ("lev", i, n))

            def gla_out(i):
                r = ROWS[i]
                pe.wait_ge(S("k_to_end"), i + 1)
                o = fill(("kdT", i), 6)
                done(tr(o[0:r, 0:P], kd[:, 0:r], ident[:, :]), ("kdT", i))
                pe.wait_ge(S("q_from_start"), i + 1)
                if i:
                    drained(pe, ("gkv", i - 1))
                if i == NT - 1:
                    pe.wait_ge(S("gla_state_in"), 16 * HB)
                drained(pe, ("lev", i, len(levels(i)) - 1))
                o = fill(("go", i), 7)
                for h in range(HB):
                    mm(o[0:r, h * DV:(h + 1) * DV], qs[:, 0:r], Sg[:, seq(i), h, :], start=True, stop=False)
                    last = mm(o[0:r, h * DV:(h + 1) * DV], att[0:r, h, 0:r], bv[0:r, i, h * DV:(h + 1) * DV],
                              start=False, stop=True)
                done(last, ("go", i))
                drained(pe, ("kdT", i))
                o = fill(("gkv", i), 6)
                done(mm(o[:, 0:HB * DV], kdn[0:r, :], bv[0:r, i, :], start=True, stop=True), ("gkv", i))

            def gla_mixT(i):
                r = ROWS[i]
                pe.wait_ge(S("gla_gated"), i + 1)
                o = fill(("goT", i), 7)
                for j in range(2):
                    last = tr(o[:, j * r:(j + 1) * r], gv[0:r, j * P:(j + 1) * P], ident[0:r, 0:r])
                done(last, ("goT", i))

            def ssd(i):
                r = ROWS[i]
                o = fill(("xn", i), 2)
                for j in range(3):
                    last = tr(o[0:r, j * P:(j + 1) * P], xc[:, j, cols(i)], ident[:, :])
                done(last, ("xn", i))
                o = fill(("csrow", i), 3)
                for h in range(HC):
                    a = small[0:r, A_A + i * HC + h:A_A + i * HC + h + 1].broadcast_to([r, P])
                    last = mm(o[:, h * P:h * P + r], a, triu[0:r, 0:r], start=True, stop=True)
                done(last, ("csrow", i))
                for g in range(2):
                    o = fill(("cb", i, g), g)
                    done(mm(o[0:r, 0:r], xc[g * NS:(g + 1) * NS, 2, cols(i)], xc[g * NS:(g + 1) * NS, 3, cols(i)],
                            start=True, stop=True), ("cb", i, g))
                if i:
                    drained(pe, ("st", i - 1))
                for g in range(2):
                    o = fill(("yi", i, g), g)
                    done(mm(o[0:r, 0:2 * PC], xc[g * NS:(g + 1) * NS, 3, cols(i)], hst[g * NS:(g + 1) * NS, seq(i), :, :],
                            start=True, stop=True), ("yi", i, g))
                pe.wait_ge(S("x_w"), i + 1)
                o = fill(("st", i), 2)
                done(mm(o[:, 0:HC * PC], xnat[0:r, 2 * P:3 * P], xw[0:r, :, :], start=True, stop=True), ("st", i))
                pe.wait_ge(S("ssd_scores"), i + 1)
                pe.wait_ge(S("x_dt"), i + 1)
                o = fill(("ya", i), 3)
                for h in range(HC):
                    last = mm(o[0:r, h * PC:(h + 1) * PC], dec[0:r, h, 0:r], xdt[0:r, h, :], start=True, stop=True)
                done(last, ("ya", i))

            def ssd_mixT(i):
                r = ROWS[i]
                pe.wait_ge(S("ssd_gated"), i + 1)
                o = fill(("syT", i), 2)
                for j in range(2):
                    last = tr(o[:, j * r:(j + 1) * r], yv[0:r, j * P:(j + 1) * P], ident[0:r, 0:r])
                done(last, ("syT", i))

            gla_gate()
            ssd_cums()
            conv_state()
            pe.wait_ge(S("conv_out"), 4)
            pe.wait_ge(S("zeroed"), 1)
            drained(pe, "s0T")
            drained(pe, ("bv", NT - 1))
            drained(pe, ("bv", NT - 2))
            drained(pe, "bk")
            drained(pe, "bqk_s")
            for i in range(NT):
                gla_levels(i)
                ssd(i)
                gla_out(i)
                gla_mixT(i)
                ssd_mixT(i)
            for s in range(2):
                drained(pe, ("st", NT - 2 + s))
                o = fill(("stT", s), 2)
                for j in range(2):
                    last = tr(o[0:PC, j * P:(j + 1) * P], hst[:, s, j, :], ident[:, :])
                done(last, ("stT", s))

            for g, nm in ((G_Q, "q"), (G_K, "k")):
                landed(g)
                w = ring(g, WA)
                for j in range(4):
                    fill((nm, j), j % 2)
                    done(proj_T("", w, j * P, P, PR, j % 2), (nm, j))
                fill((nm, 4), 2)
                for j in range(4):
                    last = proj_T("", w, j * P, P, SA, 2, j * DEC)
                done(last, (nm, 4))
            landed(G_V)
            w = ring(G_V, WA)
            for i in range(NT):
                fill(("v", i), i % 2)
                done(proj_nat(w, 0, WA, i, i % 2), ("v", i))
            for key in (("k", 2), ("k", 3), ("k", 4)):
                drained(pe, key)
            for i in range(NT):
                r = ROWS[i]
                o = fill(("kn", i), 2 + i % 2)
                for j in range(4):
                    last = tr(o[0:r, j * P:(j + 1) * P], kT[:, j, T0[i]:T0[i] + r], ident[:, :])
                done(last, ("kn", i))
            pe.wait_ge(S("cached_k_in"), 16)
            for c in range(PAST // P):
                o = fill(("ckT", c), 6 + c)
                for j in range(4):
                    last = tr(o[:, j * P:(j + 1) * P], stage[:, c, j * P:(j + 1) * P], ident[:, :])
                done(last, ("ckT", c))
            for key in (("q", 2), ("q", 3), ("q", 4), ("ckT", 0), ("ckT", 1), ("v", 3), ("v", 4)):
                drained(pe, key)
            pe.wait_ge(S("cached_v_in"), 16)

            def scores(n):
                i, h = divmod(n, HA)
                r, j, p0 = ROWS[i], h // 2, (h % 2) * DH
                q = qT[p0:p0 + DH, j, T0[i]:T0[i] + r]
                o = fill(("S", n), 4 + h % 2)
                if i < NT - 1:
                    last = mm(o[0:r, 0:nkeys(i)], q, kT[p0:p0 + DH, j, 0:nkeys(i)], start=True, stop=True)
                else:
                    mm(o[0:r, 0:PAST], q, ckT[p0:p0 + DH, j, :], start=True, stop=True)
                    last = mm(o[0:r, PAST:PAST + DEC], q, kT[p0:p0 + DH, j, SEQ:TOK], start=True, stop=True)
                done(last, ("S", n))

            def weigh(n):
                i, h = divmod(n, HA)
                r = ROWS[i]
                nk = nkeys(i)
                blocks = [(c, min(P, nk - c)) for c in range(0, nk, P)]
                drained(pe, ("S", n))
                o = fill(("PT", n), 6 + n % 2)
                for c, w_ in blocks:
                    last = tr(o[0:w_, (c // P) * r:(c // P) * r + r], Pm[0:r, n % 2, c:c + w_], ident[0:r, 0:r])
                done(last, ("PT", n))

            def values(n):
                i, h = divmod(n, HA)
                r = ROWS[i]
                nk = nkeys(i)
                blocks = [(c, min(P, nk - c)) for c in range(0, nk, P)]
                if h == 0:
                    fill(("ao", i), i % 2)
                    full_count[i % 2] -= 1
                drained(pe, ("PT", n))
                for c, w_ in blocks:
                    b = c // P
                    if i < NT - 1:
                        v = V[0:w_, b, h * DH:(h + 1) * DH]
                    else:
                        v = cv[0:w_, b, h * DH:(h + 1) * DH] if c < PAST else V[0:w_, NT - 1, h * DH:(h + 1) * DH]
                    last = mm(bank[i % 2][0:r, h * DH:(h + 1) * DH], PT[0:w_, n % 2, b * r:(b + 1) * r], v,
                              start=(b == 0), stop=(b == len(blocks) - 1))
                last.then_inc(S("pv"), 1)

            def att_mixT(i):
                r = ROWS[i]
                drained(pe, ("ao", i))
                o = fill(("aoT", i), 2 + i % 2)
                for j in range(4):
                    last = tr(o[:, j * r:(j + 1) * r], stage[0:r, i % 2, j * P:(j + 1) * P], ident[0:r, 0:r])
                done(last, ("aoT", i))

            NA = NT * HA
            for n in range(NA + 3):
                if n < NA:
                    scores(n)
                if 1 <= n <= NA:
                    weigh(n - 1)
                if 2 <= n <= NA + 1:
                    values(n - 2)
                if n >= 10 and (n - 10) % HA == 0 and (n - 10) // HA < NT - 1:
                    att_mixT((n - 10) // HA)
            att_mixT(NT - 1)

            landed(G_WO0)
            landed(G_WO1)

            def out_proj(i):
                if i == 0:
                    drained(pe, ("goT", NT - 1))
                    drained(pe, ("syT", NT - 1))
                drained(pe, ("aoT", i))
                for hf in range(2):
                    w = ring(G_WO0 + hf, 512)
                    fill(("wo", i, hf), hf)
                    for k in range(KD):
                        last = mm(bank[hf][0:ROWS[i], 0:512], mixT[:, k, T0[i]:T0[i] + ROWS[i]], w[:, k, :],
                                  start=(k == 0), stop=(k == KD - 1))
                    done(last, ("wo", i, hf))

            def router(i):
                r = ROWS[i]
                pe.wait_ge(S("h2"), i + 1)
                for hf in range(2):
                    o = fill(("h2T", i, hf), 2 + hf)
                    for k in range(4):
                        last = tr(o[:, k * r:k * r + r], h2[0:r, i % 2, (4 * hf + k) * P:(4 * hf + k + 1) * P], ident[0:r, 0:r])
                    done(last, ("h2T", i, hf))
                drained(pe, ("h2T", i, 0))
                drained(pe, ("h2T", i, 1))
                if i == 0:
                    pe.wait_ge(S("router_w_in"), 32)
                o = fill(("lg", i), 4)
                for k in range(KD):
                    last = mm(o[0:r, 0:NG + NE], hT[:, k, T0[i]:T0[i] + r], rw[:, k, :], start=(k == 0), stop=(k == KD - 1))
                done(last, ("lg", i))

            for i in range(NT + 1):
                if i < NT:
                    out_proj(i)
                if i >= 1:
                    router(i - 1)
            pe.wait_ge(S("picks"), 1)
            o = fill("pos", 5)
            for i in range(NT):
                r = ROWS[i]
                for j in range(i):
                    mm(o[0:r, i * NE:(i + 1) * NE], ones[:, 0:r], rt[:, R_A, j, :], start=(j == 0), stop=False)
                last = mm(o[0:r, i * NE:(i + 1) * NE], striu[0:r, 0:r], rt[0:r, R_A, i, :], start=(i == 0), stop=True)
            done(last, "pos")

            o = fill("tot", 5)
            for i in range(NT):
                r = ROWS[i]
                last = mm(o[:, 0:NE], ones[0:r, :], rt[0:r, R_A, i, :], start=(i == 0), stop=(i == NT - 1))
            done(last, "tot")

            pe.wait_ge(S("ids_f"), 1)
            o = fill("ids", 4)
            done(tr(o[:, 0:NE], idf[:, :], ident[0:NE, 0:NE]), "ids")

            def expert_in(e):
                pe.wait_ge(S(f"xg{e % 2}_in"), 16 * (e // 2 + 1))
                for hf in range(2):
                    o = fill(("xgT", e, hf), hf)
                    for k in range(4):
                        last = tr(o[:, k * CAP:(k + 1) * CAP], xg[:, e % 2, (4 * hf + k) * P:(4 * hf + k + 1) * P], ident[:, :])
                    done(last, ("xgT", e, hf))

            def expert_up(e):
                g = G_EXP + e
                pe.wait_ge(S(f"w{g % NSLOT}_in"), w_done(g))
                drained(pe, ("xgT", e, 0))
                drained(pe, ("xgT", e, 1))
                w = wring[:, g % NSLOT, 0:2 * KD * FE].rearrange("p (u k f) -> p k u f", u=2, k=KD)
                o = fill(("gu", e), 2 + e % 2)
                for k in range(KD):
                    last = mm(o[:, :], xgT[:, e % 2, k, :], w[:, k], start=(k == 0), stop=(k == KD - 1))
                done(last, ("gu", e))

            def expert_down(e):
                drained(pe, ("gu", e))
                o = fill(("hT", e), 4 + e % 2)
                for j in range(FE // P):
                    last = tr(o[:, j * CAP:(j + 1) * CAP], hid[:, e % 2, j * P:(j + 1) * P], ident[:, :])
                done(last, ("hT", e))
                drained(pe, ("hT", e))
                pe.wait_ge(S(f"down{e % 2}_in"), 16 * (e // 2 + 1))
                for hf in range(2):
                    o = fill(("ye", e, hf), 6 + hf)
                    for j in range(FE // P):
                        last = mm(o[:, :], hidT[:, e % 2, j, :], down[:, e % 2, j * D + hf * 512:j * D + (hf + 1) * 512],
                                  start=(j == 0), stop=(j == FE // P - 1))
                    done(last, ("ye", e, hf))

            for e in range(NE + 1):
                if e == 0:
                    expert_in(0)
                if e < NE:
                    expert_up(e)
                    if e + 1 < NE:
                        expert_in(e + 1)
                if e >= 1:
                    expert_down(e - 1)
            pe.wait_ge(S("max_count"), 1)
            fullest = pe.value_load(ri[0:1, 60:61], min_val=0, max_val=TOK)
            for key in [("xgT", NE - 1, 0), ("xgT", NE - 1, 1), ("gu", NE - 2), ("hT", NE - 2), ("hT", NE - 1),
                        ("ye", NE - 1, 0), ("ye", NE - 1, 1)]:
                drained(pe, key)
            with pe.If(fullest > CAP):
                with pe.Fori(0, MORE) as t:
                    pe.wait_ge(S("more_x"), (t + 1) * 16)
                    for k in range(KD):
                        last = tr(bank[k // 4][:, k % 4 * CAP:(k % 4 + 1) * CAP], xg[:, 0, k * P:(k + 1) * P], ident[:, :])
                    last.then_inc(S("more_turned"), 1)
                    pe.wait_ge(S("more_xT"), t + 1)
                    pe.wait_ge(S("more_w"), (t + 1) * 48)
                    w = wring[:, 0, 0:2 * KD * FE].rearrange("p (u k f) -> p k u f", u=2, k=KD)
                    for k in range(KD):
                        last = mm(bank[2][:, :], xgT[:, 0, k, :], w[:, k], start=(k == 0), stop=(k == KD - 1))
                    last.then_inc(S("more_up"), 1)
                    pe.wait_ge(S("more_hidden"), t + 1)
                    for j in range(FE // P):
                        last = tr(bank[4][:, j * CAP:(j + 1) * CAP], hid[:, 0, j * P:(j + 1) * P], ident[:, :])
                    last.then_inc(S("more_hidden_turned"), 1)
                    pe.wait_ge(S("more_hiddenT"), t + 1)
                    for hf in range(2):
                        for j in range(FE // P):
                            last = mm(bank[6 + hf][:, :], hidT[:, 0, j, :],
                                      down[:, 0, j * D + hf * 512:j * D + (hf + 1) * 512],
                                      start=(j == 0), stop=(j == FE // P - 1))
                    last.then_inc(S("more_down"), 1)
            pe.nop()

        @block.sync
        def _(sp):
            def load(dst, src, sem):
                sp.dma_start(dst, src).then_inc(S(sem), 16)

            rows = lambda a: a.rearrange("(k p) -> k p", p=P)
            load(stage[:, 0, :], tile_x(0), "x0_in")
            load(prow[G1:G1 + 8, :], rows(norm1_w[0]), "params_in")
            load(prow[G2:G2 + 8, :], rows(norm2_w[0]), "params_in")
            load(prow[GCW:GCW + 16, :], conv_w[0].rearrange("t (j p) -> (t j) p", p=P), "params_in")
            load(prow[GCB:GCB + 4, :], rows(conv_b[0]), "params_in")
            load(prow[GBG:GBG + 1, :], rows(b_gate[0]), "params_in")
            load(prow[GGN:GGN + 1, 0:DV], gla_norm_w, "params_in")
            load(prow[GGN:GGN + 1, DV:2 * DV], gla_norm_w, "params_in")
            load(prow[GSN:GSN + 2, :], rows(ssm_norm_w[0]), "params_in")
            load(prow[GCS:GCS + 12, :], state_conv[0, 0].rearrange("t (j p) -> (t j) p", p=P), "params_in")
            load(stage[:, 1, :], tile_x(1), "x1_in")
            load(wring[:, 0, 0:KD * 512].rearrange("p (k c) -> p k c", k=KD),
                 w_in[0, :, C_BQ:C_BQ + 512].rearrange("(k p) c -> p k c", p=P), "w0_in")
            for i in range(2, NT):
                filled(sp, ("xT", i - 2, 1))
                load(stage[0:ROWS[i], i % 2, :], tile_x(i), f"x{i % 2}_in")
            load(rtab[:, :], rel_table[0], "table_in")
            bc = lambda a, r: a.broadcast_to([P, r])
            load(small[:, A_AL:A_AL + HC], bc(a_log, HC), "ssd_params_in")
            load(small[:, A_DTB:A_DTB + HC], bc(dt_bias, HC), "ssd_params_in")
            load(small[:, A_D:A_D + HC], bc(d_skip, HC), "ssd_params_in")
            load(wup[:, :], gate_up[0], "wup_in")
            for h in range(HC):
                at = (2 * (h % 2) + h // 2) * NS
                load(yt[0:PC, at:at + NS], state_ssm[0, 0, h], "state_in")
            for g in (1, 2):
                c, w = groups[g]
                load(ring(g, w), w_in[0, :, c:c + w].rearrange("(k p) c -> p k c", p=P), f"w{g}_in")
            sp.wait_ge(S("zeroed"), 1)
            for h in range(HB):
                load(Sg[h * DK:(h + 1) * DK, 1, h, :], state_gla[0, 0, h], "gla_state_in")
            load(map_d.rearrange("(p c) one -> p (c one)", p=P), zmap[:, :], "map_zero")
            load(rw[:, :, 0:NG], rg_w[0].rearrange("(k p) c -> p k c", p=P), "router_w_in")
            load(rw[:, :, NG:NG + NE], re_w[0].rearrange("(k p) c -> p k c", p=P), "router_w_in")
            load(rb[:, 0:NG], bc(rg_b, NG), "router_b_in")
            load(rb[:, NG:NG + NE], bc(re_b, NE), "router_b_in")
            filled(sp, ("xT", NT - 1, 1))
            load(stage[:, :, 0:WA], cache_k[0, 0].rearrange("(c p) h d -> p c (h d)", p=P), "cached_k_in")
            last_use = {G_B: ("bv", NT - 1), G_LR: ("ogz", NT - 1), G_XBC: "dt", G_Q: ("q", 4), G_K: ("k", 4),
                        G_V: ("v", NT - 1), G_WO0: ("wo", NT - 1, 0), G_WO1: ("wo", NT - 1, 1)}
            for g in (G_Q, G_K, G_V, G_WO0, G_WO1):
                filled(sp, last_use[g - NSLOT])
                src = (w_in[0, :, groups[g][0]:groups[g][0] + WA] if g <= G_V
                       else w_out[0, :, (g - G_WO0) * 512:(g - G_WO0 + 1) * 512])
                load(ring(g, 512), src.rearrange("(k p) c -> p k c", p=P), f"w{g % NSLOT}_in")
                if g == G_V:
                    drained(sp, ("goT", NT - 1))
                    drained(sp, ("syT", NT - 1))
                    drained(sp, ("stT", 1))
                    sp.wait_ge(S("states_out"), 16 * (2 * HB + 4 + 2))
                    for i in range(NT):
                        load(x1[0:ROWS[i], i, :], tile_x(i), "x1_in_residual")
                    load(w2b[:, :], bc(norm2_w, D), "norm_rows_in")
                    load(wfb[:, :], final_w.rearrange("(o d) -> o d", o=1).broadcast_to([P, D]), "norm_rows_in")
            for e in range(NE):
                g = G_EXP + e
                filled(sp, last_use[g - NSLOT] if g - NSLOT in last_use else ("gu", e - NSLOT))
                dst = wring[:, g % NSLOT, 0:2 * KD * FE].rearrange("p (u k f) -> p u k f", u=2, k=KD)
                load(dst[:, 0], exp_gate[0, e].rearrange("(k p) f -> p k f", p=P), f"w{g % NSLOT}_in")
                load(dst[:, 1], exp_up[0, e].rearrange("(k p) f -> p k f", p=P), f"w{g % NSLOT}_in")
                if e >= 2:
                    filled(sp, ("ye", e - 2, 1))
                else:
                    sp.wait_ge(S("conv_out"), 4)
                load(down[:, e % 2, :].rearrange("p (j d) -> p j d", j=FE // P),
                     exp_down[0, e].rearrange("(j p) d -> p j d", p=P), f"down{e % 2}_in")
            sp.wait_ge(S("max_count"), 1)
            fullest = sp.value_load(ri[0:1, 60:61], min_val=0, max_val=TOK)
            drained(sp, ("ye", NE - 1, 1))
            with sp.If(fullest > CAP):
                with sp.Fori(0, MORE) as t:
                    dst = wring[:, 0, 0:2 * KD * FE].rearrange("p (u k f) -> p u k f", u=2, k=KD)
                    e = t % NE
                    for u, w in ((0, exp_gate), (1, exp_up)):
                        sp.dma_start(dst[:, u], w[0, bass.ds(e, 1)].rearrange("o (k p) f -> p (o k) f", p=P)
                                     ).then_inc(S("more_w"), 16)
                    sp.dma_start(down[:, 0, :].rearrange("p (j d) -> p j d", j=FE // P),
                                 exp_down[0, bass.ds(e, 1)].rearrange("o (j p) d -> p (o j) d", p=P)
                                 ).then_inc(S("more_w"), 16)
                    sp.wait_ge(S("more_y"), t + 1)
                    sp.sem_inc(S("more_y_seen"), 1)
            sp.nop()

        @block.gpsimd
        def _(pool):
            chain = [0]

            def link(ins):
                chain[0] += 1
                ins.then_inc(S("pool_chain"), 1)
                pool.wait_ge(S("pool_chain"), chain[0])

            g = nc.gpsimd
            link(g.memset(ones[:, :], 1.0))
            link(g.affine_select(out=triu[:, :], in_=ones[:, :], pattern=[[1, P]], compare_op=ALU.is_ge, fill=0.0,
                                 base=0, channel_multiplier=-1))
            link(g.affine_select(out=striu[:, :], in_=ones[:, :], pattern=[[1, P]], compare_op=ALU.is_gt, fill=0.0,
                                 base=0, channel_multiplier=-1))
            g.tensor_tensor(ident[:, :], triu[:, :], striu[:, :], ALU.subtract).then_inc(S("consts"), 1)
            g.iota(iot[:, 0, :], pattern=[[0, P]], base=0, channel_multiplier=1)
            g.iota(iot[:, 1, :], pattern=[[1, P]], base=0, channel_multiplier=0).then_inc(S("iotas"), 1)
            g.memset(small[:, A_MH:A_MH + 20], -0.5).then_inc(S("half"), 1)
            g.memset(qbd[:, :, :], 0.0)
            g.memset(qE[:, :, :, :], 0.0)
            g.memset(att[:, :, :], 0.0)
            g.memset(Sg[:, :, :, :], 0.0)
            g.memset(hst[:, 0, :, :], 0.0)
            g.memset(dtw[:, :, :], 0.0)
            g.memset(xpre[:, :, 0:3], 0.0)
            link(g.memset(zmap[:, :], 0))
            g.iota(ri[:, 32:32 + NT], pattern=[[P, NT]], base=0, channel_multiplier=1)
            g.iota(ri[:, 48:48 + NE], pattern=[[CAP, NE]], base=0, channel_multiplier=0)
            g.iota(ri[:, 40:44], pattern=[[-1, 4]], base=4, channel_multiplier=0).then_inc(S("zeroed"), 1)
            pool.wait_ge(S("zeroed"), 1)

            def inv_rms(col, out, n, rows, need, count, sem):
                pool.wait_ge(S(need), count)
                g.tensor_tensor(small[0:rows, out:out + n], small[0:rows, col:col + n],
                                small[0:rows, A_MH:A_MH + n], ALU.pow).then_inc(S(sem), 1)

            pool.wait_ge(S("half"), 1)
            for i in range(NT):
                inv_rms(A_MS + i, A_RS + i, 1, ROWS[i], "norm1_mean", i + 1, "norm1_rms")

            pool.wait_ge(S("rev_ready"), 1)
            g.dma_start(relpos_d[:, 0:383], xrel[:, 0:383]).then_inc(S("rev_out"), 16)
            pool.wait_ge(S("rev_out"), 16)

            for i in range(NT):
                r = ROWS[i]
                pool.wait_ge(S("q_blocks"), i + 1)
                for n, m in enumerate(levels(i)[:-1]):
                    c = n_lev[i] - i + n
                    pool.wait_ge(S("E"), c + 1)
                    if c >= 2:
                        filled(pool, lev_key[c - 2])
                    g.tensor_tensor(qE[:, c % 2, :, 0:r], qbd[:, :, 0:r],
                                    dif[:, c % 2, 0:r].unsqueeze(1).broadcast_to([P, HB, r]),
                                    ALU.mult).then_inc(S("q_decayed"), 1)
                drained(pool, ("xn", i))
                x = xnat[0:r, 0:2 * P].rearrange("p (h c) -> p h c", h=HC)

                def scaled(dst, col):
                    return g.tensor_tensor(dst[0:r, :, :], x,
                                           small[0:r, col:col + HC].unsqueeze(2).broadcast_to([r, HC, PC]), ALU.mult)

                if i:
                    filled(pool, ("ya", i - 1))
                scaled(xdt, A_DT + i * HC).then_inc(S("x_dt"), 1)
                if i:
                    pool.wait_ge(S("ssd_sum"), i)
                scaled(xD, A_D).then_inc(S("x_skip"), 1)
                pool.wait_ge(S("ssd_w"), i + 1)
                scaled(xw, A_W).then_inc(S("x_w"), 1)
                inv_rms(A_GS, A_GR, HB, r, "gla_mean", i + 1, "gla_rms")
                inv_rms(A_YS, A_YR, 2, r, "ssd_mean", i + 1, "ssd_rms")
            filled(pool, ("v", NT - 1))
            src = bass.AP(tensor=relpos_d.tensor, offset=0, ap=[[1, P], [384, HA], [1, 2 * P]])
            g.dma_start(bias[:, :, :], src).then_inc(S("bias_in"), 16)
            for i in range(NT):
                inv_rms(A_MS + i, A_RS + i, 1, ROWS[i], "norm2_mean", i + 1, "norm2_rms")

            pool.wait_ge(S("slots"), 1)
            pool.wait_ge(S("map_zero"), 16)
            for k in range(2):
                for i in range(NT):
                    r = ROWS[i]
                    g.indirect_dma_start(out=map_d, out_offset=bass.IndirectOffsetOnAxis(ap=ri[0:r, k * NT + i:k * NT + i + 1].bitcast(U32), axis=0),
                                         in_=ri[0:r, 32 + i:33 + i], in_offset=None).then_inc(S("map_written"), 16)
            pool.wait_ge(S("map_written"), 16 * 2 * NT)
            g.dma_start(idi[:, :], map_d[0:SPAN].rearrange("(e s) one -> e (s one)", e=NE)).then_inc(S("ids_in"), 16)
            drained(pool, "ids")
            pool.wait_ge(S("h2_out0"), 16 * ((NT + 1) // 2))
            pool.wait_ge(S("h2_out1"), 16 * (NT // 2))
            for e in range(NE):
                if e >= 2:
                    filled(pool, ("xgT", e - 2, 1))
                g.indirect_dma_start(out=xg[:, e % 2, :], out_offset=None, in_=h2_d,
                                     in_offset=bass.IndirectOffsetOnAxis(ap=ri[:, 16 + e:17 + e].bitcast(U32), axis=0)
                                     ).then_inc(S(f"xg{e % 2}_in"), 16)
            def combine(slots):
                for i in range(NT):
                    r = ROWS[i]
                    if i >= 2:
                        pool.wait_ge(S("combined"), i - 1)
                    for k, dst in ((0, xg[0:r, i % 2, :]), (1, xgT[0:r, i % 2, :, :].rearrange("p k c -> p (k c)"))):
                        index = ri[0:r, k * NT + i:k * NT + i + 1].bitcast(U32)
                        g.indirect_dma_start(out=dst, out_offset=None, in_=slots,
                                             in_offset=bass.IndirectOffsetOnAxis(ap=index, axis=0)
                                             ).then_inc(S(f"yg{i % 2}_in"), 16)
                    if i >= 1:
                        inv_rms(A_MS + i - 1, A_RS + i - 1, 1, ROWS[i - 1], "final_mean", i, "final_rms")
                inv_rms(A_MS + NT - 1, A_RS + NT - 1, 1, ROWS[NT - 1], "final_mean", NT, "final_rms")

            pool.wait_ge(S("max_count"), 1)
            fullest = pool.value_load(ri[0:1, 60:61], min_val=0, max_val=TOK)
            filled(pool, ("ye", NE - 1, 1))
            pool.wait_ge(S("y_out0"), 16 * (NE // 2))
            pool.wait_ge(S("y_out1"), 16 * (NE // 2))
            with pool.If(fullest > CAP):
                with pool.Fori(0, MORE) as t:
                    g.dma_start(ri[:, 61:62], map_d[bass.ds(t * CAP + SPAN, CAP), :]).then_inc(S("more_ids"), 16)
                    pool.wait_ge(S("more_ids"), (t + 1) * 16)
                    pool.sem_inc(S("more_ids_seen"), 1)
                    g.indirect_dma_start(out=xg[:, 0, :], out_offset=None, in_=h2_d,
                                         in_offset=bass.IndirectOffsetOnAxis(ap=ri[:, 61:62].bitcast(U32), axis=0)
                                         ).then_inc(S("more_x"), 16)
                    pool.wait_ge(S("more_turned"), t + 1)
                pool.wait_ge(S("more_out"), 16 * MORE)
                combine(y_d)
            with pool.Else():
                combine(y_d[0:SPAN, :])
            pool.nop()

        @block.scalar
        def _(act):
            a = nc.scalar.activation
            own = [0]

            def link(ins):
                own[0] += 1
                ins.then_inc(S("act_chain"), 1)
                act.wait_ge(S("act_chain"), own[0])

            def store(dst, src, sem):
                act.dma_start(dst, src).then_inc(S(sem), 16)

            def squares(i, rows, src, dump, sem):
                if i:
                    act.wait_ge(S(sem), i)
                a(dump, src, ACT.Square, accum_out=small[0:rows, A_SSQ + i:A_SSQ + i + 1]).then_inc(S(sem), 1)

            full(act, "par")
            free(a(par[:, 0:NPAR], bank[4][:, 0:NPAR], ACT.Copy), "par")
            for i in range(NT):
                r = ROWS[i]
                act.wait_ge(S(f"x{i % 2}_in"), 16 * (i // 2 + 1))
                squares(i, r, stage[0:r, i % 2, :].rearrange("p (a b) -> p a b", a=2), mixT[0:r, 0:2, 0:512], "norm1_sq")
            act.wait_ge(S("ssd_params_in"), 48)
            a(small[:, A_NA:A_NA + HC], small[:, A_AL:A_AL + HC], ACT.Exp).then_inc(S("a_exp"), 1)
            full(act, "s0T")
            free(a(hst[:, 1, :, :], bank[4][:, 0:2 * PC].rearrange("p (j c) -> p j c", j=2), ACT.Copy), "s0T")
            full(act, "bq")
            free(a(qB[:, 0:SEQ], bank[0][:, :], ACT.Copy, scale=DK ** -0.5), "bq")
            full(act, "bqk_s")
            a(qB[:, SEQ:TOK], bank[2][:, 0:DEC], ACT.Copy, scale=DK ** -0.5)
            free(a(kB[:, SEQ:TOK], bank[2][:, DEC:2 * DEC], ACT.Copy), "bqk_s")
            for i in range(NT):
                r = ROWS[i]
                full(act, ("bv", i))
                free(a(bv[0:r, i, :], bank[i % 2][0:r, 0:HB * DV], ACT.Copy), ("bv", i))
            full(act, "lr")
            free(a(lrT[:, 0:SEQ], bank[2][0:RANK, :], ACT.Copy), "lr")
            full(act, "lr_s")
            free(a(lrT[:, SEQ:TOK], bank[3][0:RANK, 0:DEC], ACT.Copy), "lr_s")
            for i in range(NT):
                r = ROWS[i]
                full(act, ("ogz", i))
                free(a(ogz[0:r, i, :], bank[i % 2][0:r, :], ACT.Copy, scale=0.5), ("ogz", i))
                drained(act, ("ogz", i))
                if i >= 2:
                    act.wait_ge(S("gates"), i - 1)
                a(gth[0:r, i % 2, :], ogz[0:r, i, :], ACT.Tanh).then_inc(S("gates_tanh"), 1)
            drained(act, "par")
            a(xpre[:, :, SEQ + 3:SEQ + 6], par[:, GCS:GCS + 12].rearrange("p (t j) -> p j t", j=4),
              ACT.Copy).then_inc(S("conv_state_placed"), 1)
            for j in range(4):
                full(act, ("xbc", j))
                free(a(xpre[:, j, 3:SEQ + 3], bank[j % 2][:, :], ACT.Copy), ("xbc", j))
            full(act, "xbc_s")
            free(a(xpre[:, :, SEQ + 6:TOK + 6], bank[0][:, 0:4 * DEC].rearrange("p (j t) -> p j t", j=4), ACT.Copy),
                 "xbc_s")
            drained(act, "gate")
            drained(act, "gate_s")
            link(a(gtmp[:, 1, :], gtmp[:, 0, :], ACT.Abs))
            link(a(gtmp[:, 1, :], gtmp[:, 1, :], ACT.Exp, scale=-1.0))
            a(gtmp[:, 1, :], gtmp[:, 1, :], ACT.Ln, bias=1.0).then_inc(S("gate_log"), 1)
            act.wait_ge(S("dt_u"), 1)
            link(a(dtw[:, 1, :], dtw[:, 0, :], ACT.Abs))
            a(dtw[:, 2, :], dtw[:, 1, :], ACT.Exp, scale=-1.0).then_inc(S("dt_e"), 1)
            act.wait_ge(S("dt_w"), 1)
            a(dtw[:, 4, :], dtw[:, 3, :], ACT.Ln).then_inc(S("dt_ln"), 1)
            for s, dst in ((0, o_pc), (1, o_sc)):
                full(act, ("cst", s))
                free(a(cso[0:3, s, :], bank[3][0:3, :], ACT.Copy), ("cst", s))
                drained(act, ("cst", s))
                store(dst[0, 0], cso[0:3, s, :], "states_out")
            for j in range(4):
                act.wait_ge(S("conv_sum"), j + 1)
                if j:
                    act.wait_ge(S("conv_out"), j)
                a(thx[:, 0:TOK + 3], ctmp[:, j % 2, 0:TOK + 3], ACT.Tanh).then_inc(S("conv_tanh"), 1)

            for i in range(NT):
                r = ROWS[i]
                t0, t1 = T0[i], T0[i] + r
                if i == 0:
                    act.wait_ge(S("zeroed"), 1)
                    drained(act, "bq")
                    drained(act, "bqk_s")
                else:
                    filled(act, ("lev", i - 1, len(levels(i - 1)) - 1))
                for h in range(HB):
                    last = a(qbd[h * DK:(h + 1) * DK, h, 0:r], qB[h * DK:(h + 1) * DK, t0:t1], ACT.Copy)
                last.then_inc(S("q_blocks"), 1)
                act.wait_ge(S("gla_b"), i + 1)
                a(qs[:, 0:r], bcum[:, t0:t1], ACT.Exp).then_inc(S("gla_exps"), 1)
                a(kd[:, 0:r], bcum[:, t0:t1], ACT.Exp, scale=-1.0, bias=bcum[:, t1 - 1:t1]).then_inc(S("gla_exps"), 1)
                a(small[:, A_EBL:A_EBL + 1], bcum[:, t1 - 1:t1], ACT.Exp).then_inc(S("gla_exps"), 1)
                for n, m in enumerate(levels(i)[:-1]):
                    c = n_lev[i] - i + n
                    act.wait_ge(S("dif"), c + 1)
                    a(dif[:, c % 2, 0:r], dif[:, c % 2, 0:r], ACT.Exp).then_inc(S("E"), 1)
                full(act, ("xn", i))
                free(a(xnat[0:r, :], bank[2][0:r, 0:3 * P], ACT.Copy), ("xn", i))
                act.wait_ge(S("cs_last"), i + 1)
                a(small[0:r, A_W:A_W + HC], small[0:r, A_W:A_W + HC], ACT.Exp)
                a(small[:, A_ECL:A_ECL + HC], small[:, A_CSL:A_CSL + HC], ACT.Exp)
                a(small[0:r, A_ECS:A_ECS + HC], small[0:r, A_CS + i * HC:A_CS + (i + 1) * HC],
                  ACT.Exp).then_inc(S("ssd_exps"), 1)
                drained(act, ("csrow", i))
                a(dec[0:r, :, 0:r], dec[0:r, :, 0:r], ACT.Exp).then_inc(S("decay"), 1)
                full(act, ("kdT", i))
                free(a(kdn[0:r, :], bank[6][0:r, 0:P], ACT.Copy), ("kdT", i))
                full(act, ("go", i))
                free(a(gv[0:r, :], bank[7][0:r, 0:HB * DV], ACT.Copy), ("go", i))
                for key, b, c, kt in ((("goT", i), 7, (GGN, GGN), WA // P), (("syT", i), 2, (GSN, GSN + 1), WA // P + 2)):
                    full(act, key)
                    a(mixT[:, kt, t0:t1], bank[b][:, 0:r], ACT.Copy, scale=par[:, c[0]:c[0] + 1])
                    free(a(mixT[:, kt + 1, t0:t1], bank[b][:, r:2 * r], ACT.Copy, scale=par[:, c[1]:c[1] + 1]), key)
                if i >= NT - 2:
                    s = seq(i)
                    drained(act, ("gkv", i))
                    for h in range(HB):
                        store((o_pg, o_sg)[s][0, 0, h], Sg[h * DK:(h + 1) * DK, s, h, :], "states_out")
            for s in range(2):
                full(act, ("stT", s))
                free(a(sto[:, s, :], bank[2][0:PC, 0:2 * P], ACT.Copy), ("stT", s))
                drained(act, ("stT", s))
                o = (o_ps, o_ss)[s][0, 0].rearrange("(g j) p n -> j p g n", j=2)
                for j in range(2):
                    store(o[j], sto[:, s, j * P:(j + 1) * P].rearrange("p (g n) -> p g n", g=2), "states_out")
            filled(act, ("stT", 1))
            act.dma_start(cv[:, :, :], cache_v[0, 0].rearrange("(c p) h d -> p c (h d)", p=P)).then_inc(S("cached_v_in"), 16)
            for j in range(5):
                full(act, ("q", j))
                if j < 4:
                    free(a(qT[:, j, 0:SEQ], bank[j % 2][:, :], ACT.Copy, scale=DH ** -0.5), ("q", j))
                else:
                    free(a(qT[:, :, SEQ:TOK], bank[2][:, 0:4 * DEC].rearrange("p (j t) -> p j t", j=4), ACT.Copy,
                           scale=DH ** -0.5), ("q", j))
            for i in range(NT):
                r = ROWS[i]
                full(act, ("v", i))
                free(a(V[0:r, i, :], bank[i % 2][0:r, :], ACT.Copy), ("v", i))
                drained(act, ("v", i))
                dst = o_pv[0, 0, T0[i]:T0[i] + r] if i < NT - 1 else o_sv[0, 0]
                store(dst.rearrange("t h d -> t (h d)"), V[0:r, i, :], "v_out")
            for i in range(NT):
                r = ROWS[i]
                drained(act, ("kn", i))
                dst = o_pk[0, 0, T0[i]:T0[i] + r] if i < NT - 1 else o_sk[0, 0]
                store(dst.rearrange("t h d -> t (h d)"), stage[0:r, i % 2, WA:2 * WA], f"k_out{i % 2}")
            for c in range(PAST // P):
                full(act, ("ckT", c))
                free(a(ckT[:, :, c * P:(c + 1) * P], bank[6 + c][:, :].rearrange("p (j t) -> p j t", j=4), ACT.Copy),
                     ("ckT", c))
            NA = NT * HA
            for n in range(NA + 1):
                if n < NA:
                    i, h = divmod(n, HA)
                    r, nk = ROWS[i], nkeys(i)
                    act.wait_ge(S("negmax"), n + 1)
                    if n >= 2:
                        filled(act, ("PT", n - 2))
                    c = A_SUM + (i % 2) * HA + h
                    free(a(Pm[0:r, n % 2, 0:nk], bank[4 + h % 2][0:r, 0:nk], ACT.Exp,
                           bias=small[0:r, A_NM + n % 4:A_NM + n % 4 + 1], accum_out=small[0:r, c:c + 1]), ("S", n))
                if n >= 1:
                    m = n - 1
                    i, h = divmod(m, HA)
                    r, nk = ROWS[i], nkeys(i)
                    full(act, ("PT", m))
                    if m >= 2:
                        act.wait_ge(S("pv"), m - 1)
                    src, nb, rest = bank[6 + m % 2], nk // P, nk % P
                    if rest:
                        a(PT[0:rest, m % 2, nb * r:(nb + 1) * r], src[0:rest, nb * r:(nb + 1) * r], ACT.Copy)
                    free(a(PT[:, m % 2, 0:nb * r], src[:, 0:nb * r], ACT.Copy), ("PT", m))
            for i in range(NT):
                r = ROWS[i]
                drained(act, ("wo", i, 0))
                drained(act, ("wo", i, 1))
                squares(i, r, x1[0:r, i, :], xgT[0:r, 1, :, :].rearrange("p k c -> p (k c)"), "norm2_sq")
                act.wait_ge(S("h2"), i + 1)
                store(h2_d[T0[i]:T0[i] + r, :], h2[0:r, i % 2, :], f"h2_out{i % 2}")
                full(act, ("h2T", i, 0))
                free(a(hT[:, 0:4, T0[i]:T0[i] + r], bank[2][:, 0:4 * r].rearrange("p (k t) -> p k t", k=4), ACT.Copy),
                     ("h2T", i, 0))
            act.wait_ge(S("router_sub"), 1)
            a(rt[:, R_SUB, :, 0:4], rt[:, R_SUB, :, 0:4], ACT.Exp).then_inc(S("router_exp"), 1)
            act.wait_ge(S("router_sub"), 2)
            a(rt[:, R_V, :, 0:1], rt[:, R_V, :, 0:1], ACT.Exp).then_inc(S("router_exp"), 1)
            for e in range(-1, NE + 1):
                if e + 1 < NE:
                    full(act, ("xgT", e + 1, 0))
                    free(a(xgT[:, (e + 1) % 2, 0:4, :], bank[0][:, :].rearrange("p (k c) -> p k c", k=4), ACT.Copy),
                         ("xgT", e + 1, 0))
                if 0 <= e < NE:
                    full(act, ("gu", e))
                    if e >= 2:
                        drained(act, ("gu", e - 2))
                    a(sg[:, e % 2, :], bank[2 + e % 2][:, 0:FE], ACT.Silu).then_inc(S("silu"), 1)
                if e >= 1:
                    d = e - 1
                    full(act, ("hT", d))
                    free(a(hidT[:, d % 2, :, :],
                           bank[4 + d % 2][:, 0:FE // P * CAP].rearrange("p (j c) -> p j c", j=FE // P), ACT.Copy),
                         ("hT", d))
                    if d >= 2:
                        act.wait_ge(S(f"y_out{d % 2}"), 16 * (d // 2))
                    full(act, ("ye", d, 0))
                    free(a(ye[:, d % 2, 0:512], bank[6][:, :], ACT.Copy), ("ye", d, 0))
                    drained(act, ("ye", d, 0))
                    drained(act, ("ye", d, 1))
                    store(y_d[d * CAP:(d + 1) * CAP, :], ye[:, d % 2, :], f"y_out{d % 2}")
            act.wait_ge(S("max_count"), 1)
            fullest = act.value_load(ri[0:1, 60:61], min_val=0, max_val=TOK)
            act.wait_ge(S("y_out0"), 16 * (NE // 2))
            act.wait_ge(S("y_out1"), 16 * (NE // 2))
            with act.If(fullest > CAP):
                with act.Fori(0, MORE) as t:
                    act.wait_ge(S("more_turned"), t + 1)
                    a(xgT[:, 0, 0:4, :], bank[0][:, :].rearrange("p (k c) -> p k c", k=4), ACT.Copy)
                    a(xgT[:, 0, 4:8, :], bank[1][:, :].rearrange("p (k c) -> p k c", k=4), ACT.Copy).then_inc(S("more_xT"), 1)
                    act.wait_ge(S("more_up"), t + 1)
                    a(sg[:, 0, :], bank[2][:, 0:FE], ACT.Silu).then_inc(S("more_silu"), 1)
                    act.wait_ge(S("more_hidden_turned"), t + 1)
                    a(hidT[:, 0, :, :], bank[4][:, 0:FE // P * CAP].rearrange("p (j c) -> p j c", j=FE // P),
                      ACT.Copy).then_inc(S("more_hiddenT"), 1)
                    act.wait_ge(S("more_down"), t + 1)
                    a(ye[:, 0, 0:512], bank[6][:, :], ACT.Copy)
                    a(ye[:, 0, 512:1024], bank[7][:, :], ACT.Copy).then_inc(S("more_y"), 1)
                    act.wait_ge(S("more_y"), t + 1)
                    act.dma_start(y_d[bass.ds(t * CAP + SPAN, CAP), :], ye[:, 0, :]).then_inc(S("more_out"), 16)
                    act.wait_ge(S("more_out"), (t + 1) * 16)
            act.nop()
            for i in range(NT + 1):
                if i < NT:
                    r = ROWS[i]
                    act.wait_ge(S("combined"), i + 1)
                    squares(i, r, x1[0:r, i, :].rearrange("p (a b) -> p a b", a=2), mixT[0:r, 0:2, 0:512], "final_sq")
                if i >= 1:
                    n = i - 1
                    r = ROWS[n]
                    act.wait_ge(S("y_normed"), n + 1)
                    dst = y_prompt[0, T0[n]:T0[n] + r, :] if n < NT - 1 else y_sample[0]
                    store(dst, ye[0:r, n % 2, :], f"y_final{n % 2}")
            act.wait_ge(S("states_out"), 16 * (2 + 2 * HB + 4))
            act.wait_ge(S("v_out"), 16 * NT)
            for i in range(2):
                n = (NT + 1 - i) // 2
                act.wait_ge(S(f"k_out{i}"), 16 * n)
                act.wait_ge(S(f"y_final{i}"), 16 * n)

        @block.vector
        def _(dve):
            v = nc.vector
            chain = [0]

            def link(ins):
                chain[0] += 1
                ins.then_inc(S("dve_chain"), 1)
                dve.wait_ge(S("dve_chain"), chain[0])

            def col(c, n=1, rows=P):
                return small[0:rows, c:c + n]

            def mean(ssq, ms, n, rows, over, sem):
                v.tensor_scalar(col(ms, n, rows), col(ssq, n, rows), 1.0 / over, EPS, ALU.mult, ALU.add).then_inc(S(sem), 1)

            dve.wait_ge(S("iotas"), 1)
            dve.wait_ge(S("consts"), 1)
            link(v.tensor_tensor(iot[:, 0, :], iot[:, 0, :], iot[:, 1, :], ALU.bitwise_xor))
            link(v.tensor_copy(lvf[:, 0, :], iot[:, 0, :]))
            link(v.tensor_tensor(lvf[:, 0, :], lvf[:, 0, :], striu[:, :], ALU.mult))
            for n, m in enumerate(LEV):
                link(v.tensor_scalar(lvf[:, 1 + n % 2, :], lvf[:, 0, :], float(m), None, ALU.is_ge))
                if n:
                    link(v.tensor_tensor(lmask[:, n, :], lvf[:, 1 + n % 2, :], lvf[:, 2 - n % 2, :], ALU.subtract))
                else:
                    link(v.tensor_copy(lmask[:, n, :], lvf[:, 1, :]))
            link(v.tensor_copy(lmask[:, 7, :], ident[:, :]))
            for i in range(NT):
                r = ROWS[i]
                dve.wait_ge(S("norm1_sq"), i + 1)
                mean(A_SSQ + i, A_MS + i, 1, r, D, "norm1_mean")
                dve.wait_ge(S("norm1_rms"), i + 1)
                v.tensor_scalar(stage[0:r, i % 2, :], stage[0:r, i % 2, :], col(A_RS + i, 1, r), None,
                                ALU.mult).then_inc(S("x_normed"), 1)
                if i == 0:
                    drained(dve, "par")
                for hf in range(2):
                    o = full(dve, ("xT", i, hf))
                    free(v.tensor_tensor(hT[:, 4 * hf:4 * hf + 4, T0[i]:T0[i] + r],
                                         o[:, 0:4 * r].rearrange("p (k t) -> p k t", k=4),
                                         par[:, G1 + 4 * hf:G1 + 4 * hf + 4].unsqueeze(2).broadcast_to([P, 4, r]),
                                         ALU.mult), ("xT", i, hf))
            dve.wait_ge(S("table_in"), 16)
            link(v.tensor_copy(xrel[:, 0:2 * CLIP], rtab[:, 1:2 * CLIP + 1]))
            link(v.tensor_copy(xrel[:, 2 * CLIP:383], rtab[:, 2 * CLIP:2 * CLIP + 1].broadcast_to([HA, 127])))
            v.tensor_scalar(xrel[:, 0:383], xrel[:, 0:383], rtab[:, 2 * CLIP:2 * CLIP + 1], None,
                            ALU.subtract).then_inc(S("rev_ready"), 1)
            dve.wait_ge(S("a_exp"), 1)
            link(v.tensor_scalar(col(A_NA, HC), col(A_NA, HC), -1.0, None, ALU.mult))
            link(v.tensor_scalar(par[:, GCW:GCW + 20], par[:, GCW:GCW + 20], 0.5, None, ALU.mult))
            full(dve, "bk")
            free(v.tensor_copy(kB[:, 0:SEQ], bank[1][:, :]), "bk")
            for i in range(NT):
                r = ROWS[i]
                dve.wait_ge(S("gates_tanh"), i + 1)
                v.scalar_tensor_tensor(out=ogz[0:r, i, :], in0=gth[0:r, i % 2, :], scalar=1.0, in1=ogz[0:r, i, :],
                                       op0=ALU.add, op1=ALU.mult).then_inc(S("gates"), 1)
            o = full(dve, "dt")
            dve.wait_ge(S("zeroed"), 1)
            nb = NT - 1
            v.tensor_tensor(dtw[:, 0, 0:nb * HC].rearrange("p (i h) -> p i h", i=nb),
                            o[:, 0:nb * HC].rearrange("p (i h) -> p i h", i=nb),
                            col(A_DTB, HC).unsqueeze(1).broadcast_to([P, nb, HC]), ALU.add)
            free(v.tensor_tensor(dtw[0:DEC, 0, nb * HC:NT * HC], o[0:DEC, nb * HC:NT * HC],
                                 col(A_DTB, HC, DEC), ALU.add), "dt")
            drained(dve, "dt")
            v.tensor_scalar(dtw[:, 8, :], dtw[:, 0, :], 0.0, None, ALU.max).then_inc(S("dt_u"), 1)
            o = full(dve, "gate")
            free(v.tensor_scalar(gtmp[:, 0, 0:SEQ], o[:, :], par[:, GBG:GBG + 1], None, ALU.add), "gate")
            o = full(dve, "gate_s")
            free(v.tensor_scalar(gtmp[:, 0, SEQ:TOK], o[:, 0:DEC], par[:, GBG:GBG + 1], None, ALU.add), "gate_s")
            dve.wait_ge(S("gate_log"), 1)
            link(v.scalar_tensor_tensor(out=gtmp[:, 0, :], in0=gtmp[:, 0, :], scalar=0.0, in1=gtmp[:, 1, :],
                                        op0=ALU.min, op1=ALU.subtract))
            link(v.tensor_scalar(gtmp[:, 0, :], gtmp[:, 0, :], 1.0 / 16.0, None, ALU.mult))
            for i in range(NT):
                r = ROWS[i]
                v.tensor_tensor_scan(bcum[:, T0[i]:T0[i] + r], ones[:, 0:r], gtmp[:, 0, T0[i]:T0[i] + r], 0.0,
                                     ALU.mult, ALU.add).then_inc(S("gla_b"), 1)
            dve.wait_ge(S("dt_e"), 1)
            v.tensor_scalar(dtw[:, 3, :], dtw[:, 2, :], 1.0, None, ALU.add).then_inc(S("dt_w"), 1)
            dve.wait_ge(S("dt_w"), 1)
            link(v.tensor_scalar(dtw[:, 5, :], dtw[:, 3, :], -1.0, None, ALU.add))
            link(v.tensor_scalar(dtw[:, 6, :], dtw[:, 5, :], 0.0, None, ALU.is_equal))
            link(v.tensor_tensor(dtw[:, 5, :], dtw[:, 5, :], dtw[:, 6, :], ALU.add))
            link(v.reciprocal(dtw[:, 7, :], dtw[:, 5, :]))
            link(v.tensor_tensor(dtw[:, 7, :], dtw[:, 7, :], dtw[:, 2, :], ALU.mult))
            link(v.tensor_tensor(dtw[:, 6, :], dtw[:, 6, :], dtw[:, 2, :], ALU.mult))
            dve.wait_ge(S("dt_ln"), 1)
            link(v.tensor_tensor(dtw[:, 7, :], dtw[:, 7, :], dtw[:, 4, :], ALU.mult))
            link(v.tensor_tensor(dtw[:, 7, :], dtw[:, 7, :], dtw[:, 6, :], ALU.add))
            link(v.tensor_tensor(col(A_DT, NT * HC), dtw[:, 7, :], dtw[:, 8, :], ALU.add))
            v.tensor_tensor(col(A_A, NT * HC).rearrange("p (i h) -> p i h", i=NT),
                            col(A_DT, NT * HC).rearrange("p (i h) -> p i h", i=NT),
                            col(A_NA, HC).unsqueeze(1).broadcast_to([P, NT, HC]), ALU.mult).then_inc(S("a_ready"), 1)
            o = full(dve, "cs")
            v.tensor_copy(col(A_CS, nb * HC), o[:, 0:nb * HC])
            free(v.tensor_copy(col(A_CS + nb * HC, HC, DEC), o[0:DEC, nb * HC:NT * HC]), "cs")
            for key in (("xbc", 3), "xbc_s"):
                drained(dve, key)
            dve.wait_ge(S("conv_state_placed"), 1)
            L = TOK + 3

            def conv_silu(j):
                dve.wait_ge(S("conv_tanh"), j + 1)
                v.scalar_tensor_tensor(out=xc[:, j, 0:L], in0=thx[:, 0:L], scalar=1.0, in1=ctmp[:, j % 2, 0:L],
                                       op0=ALU.add, op1=ALU.mult).then_inc(S("conv_out"), 1)

            for j in range(4):
                acc = ctmp[:, j % 2, 0:L]

                def tap(t):
                    return par[:, GCW + 4 * t + j:GCW + 4 * t + j + 1]

                if j >= 2:
                    dve.wait_ge(S("conv_out"), j - 1)
                link(v.tensor_scalar(acc, xpre[:, j, 0:L], tap(0), par[:, GCB + j:GCB + j + 1], ALU.mult, ALU.add))
                for t in range(1, TAPS):
                    ins = v.scalar_tensor_tensor(out=acc, in0=xpre[:, j, t:t + L], scalar=tap(t), in1=acc,
                                                 op0=ALU.mult, op1=ALU.add)
                    if t < TAPS - 1:
                        link(ins)
                ins.then_inc(S("conv_sum"), 1)
                if j:
                    conv_silu(j - 1)
            conv_silu(3)
            drained(dve, "cs")

            for i in range(NT):
                r = ROWS[i]
                t0 = T0[i]
                base_c = n_lev[i] - i
                lev = levels(i)
                first = LEV.index(lev[0])
                dve.wait_ge(S("gla_exps"), 3 * (i + 1))
                drained(dve, "bq")
                drained(dve, "bqk_s")
                v.tensor_tensor(qs[:, 0:r], qs[:, 0:r], qB[:, t0:t0 + r], ALU.mult).then_inc(S("q_from_start"), 1)
                v.tensor_tensor(kd[:, 0:r], kd[:, 0:r], kB[:, t0:t0 + r], ALU.mult).then_inc(S("k_to_end"), 1)

                def exponents(n):
                    m, c = lev[n], base_c + n
                    if c >= 2:
                        dve.wait_ge(S("q_decayed"), c - 1)
                        dve.wait_ge(S("k_decayed"), c - 1)
                    b = bcum[:, t0:t0 + r].rearrange("p (n two m) -> p n two m", two=2, m=m)
                    d = dif[:, c % 2, 0:r].rearrange("p (n two m) -> p n two m", two=2, m=m)
                    ref = b[:, :, 0, m - 1:m].broadcast_to([P, r // (2 * m), m])
                    v.tensor_tensor(d[:, :, 1, :], b[:, :, 1, :], ref, ALU.subtract)
                    v.tensor_tensor(d[:, :, 0, :], ref, b[:, :, 0, :], ALU.subtract).then_inc(S("dif"), 1)

                def decay_k(n):
                    c = base_c + n
                    dve.wait_ge(S("E"), c + 1)
                    if c >= 2:
                        filled(dve, lev_key[c - 2])
                    v.tensor_tensor(kE[:, c % 2, 0:r], kB[:, t0:t0 + r], dif[:, c % 2, 0:r],
                                    ALU.mult).then_inc(S("k_decayed"), 1)

                def select(n):
                    o = full(dve, ("lev", i, n))
                    if n:
                        drained(dve, ("lev", i, n - 1))
                    which = 7 if lev[n] == 0 else first + n
                    free(v.copy_predicated(att[0:r, :, 0:r],
                                           lmask[0:r, which, 0:r].unsqueeze(1).broadcast_to([r, HB, r]),
                                           o[0:r, 0:HB * r].rearrange("p (h t) -> p h t", h=HB)), ("lev", i, n))

                for n in range(len(lev) + 1):
                    if n < len(lev) - 1:
                        exponents(n)
                    if 1 <= n < len(lev):
                        decay_k(n - 1)
                    if n >= 2:
                        select(n - 2)
                select(len(lev) - 1)
                o = full(dve, ("csrow", i))
                link(v.tensor_copy(col(A_CSL, HC), o[:, :].rearrange("p (h t) -> p h t", h=HC)[:, :, r - 1]))
                v.tensor_tensor(col(A_W, HC, r), col(A_CSL, HC, r), col(A_CS + i * HC, HC, r),
                                ALU.subtract).then_inc(S("cs_last"), 1)
                for h in range(HC):
                    ins = v.tensor_scalar(dec[0:r, h, 0:r], o[0:r, h * P:h * P + r], col(A_CS + i * HC + h, 1, r), 0.0,
                                          ALU.subtract, ALU.min)
                free(ins, ("csrow", i))
                if i:
                    dve.wait_ge(S("ssd_scores"), i)
                for g in range(2):
                    o = full(dve, ("cb", i, g))
                    free(v.tensor_tensor(cbm[0:r, g, 0:r], o[0:r, 0:r], triu[0:r, 0:r], ALU.mult), ("cb", i, g))
                dve.wait_ge(S("ssd_exps"), i + 1)
                v.tensor_tensor(col(A_W, HC, r), col(A_W, HC, r), col(A_DT + i * HC, HC, r), ALU.mult).then_inc(S("ssd_w"), 1)
                dve.wait_ge(S("decay"), i + 1)
                drained(dve, ("cb", i, 1))
                for g in range(2):
                    ins = v.tensor_tensor(dec[0:r, 2 * g:2 * g + 2, 0:r], dec[0:r, 2 * g:2 * g + 2, 0:r],
                                          cbm[0:r, g, 0:r].unsqueeze(1).broadcast_to([r, 2, r]), ALU.mult)
                ins.then_inc(S("ssd_scores"), 1)
                for g in range(2):
                    o = full(dve, ("yi", i, g))
                    free(v.tensor_tensor(yt[0:r, g * 2 * PC:(g + 1) * 2 * PC].rearrange("p (j c) -> p j c", j=2),
                                         o[0:r, 0:2 * PC].rearrange("p (j c) -> p j c", j=2),
                                         col(A_ECS + 2 * g, 2, r).unsqueeze(2).broadcast_to([r, 2, PC]), ALU.mult),
                         ("yi", i, g))
                o = full(dve, ("st", i))
                for h in range(HC):
                    g, j = divmod(h, 2)
                    new, old = hst[g * NS:(g + 1) * NS, seq(i), j, :], hst[g * NS:(g + 1) * NS, seq(i), j, :]
                    ins = v.scalar_tensor_tensor(out=new, in0=old, scalar=small[g * NS:(g + 1) * NS, A_ECL + h:A_ECL + h + 1],
                                                 in1=o[g * NS:(g + 1) * NS, h * PC:(h + 1) * PC], op0=ALU.mult, op1=ALU.add)
                free(ins, ("st", i))
                drained(dve, ("st", i))
                drained(dve, ("yi", i, 1))
                dve.wait_ge(S("x_skip"), i + 1)
                v.tensor_tensor(yt[0:r, :], yt[0:r, :], xD[0:r, :, :].rearrange("p h c -> p (h c)"),
                                ALU.add).then_inc(S("ssd_sum"), 1)
                o = full(dve, ("ya", i))
                dve.wait_ge(S("ssd_sum"), i + 1)
                free(v.tensor_tensor(yv[0:r, :], o[0:r, 0:HC * PC], yt[0:r, :], ALU.add), ("ya", i))
                drained(dve, ("ya", i))
                link(v.tensor_tensor(yv[0:r, :], yv[0:r, :], ogz[0:r, i, HB * DV:], ALU.mult))
                link(v.tensor_tensor(yt[0:r, :], yv[0:r, :], yv[0:r, :], ALU.mult))
                link(v.tensor_reduce(col(A_YS, 2, r), yt[0:r, :].rearrange("p (g c) -> p g c", g=2), AX.X, ALU.add))
                mean(A_YS, A_YS, 2, r, HC * PC // 2, "ssd_mean")
                drained(dve, ("go", i))
                link(v.tensor_tensor(gt[0:r, :], gv[0:r, :], gv[0:r, :], ALU.mult))
                link(v.tensor_reduce(col(A_GS, HB, r), gt[0:r, :].rearrange("p (h c) -> p h c", h=HB), AX.X, ALU.add))
                mean(A_GS, A_GS, HB, r, DV, "gla_mean")
                o = full(dve, ("gkv", i))
                for h in range(HB):
                    p0, p1 = h * DK, (h + 1) * DK
                    ins = v.scalar_tensor_tensor(out=Sg[p0:p1, seq(i), h, :], in0=Sg[p0:p1, seq(i), h, :],
                                                 scalar=small[p0:p1, A_EBL:A_EBL + 1], in1=o[p0:p1, h * DV:(h + 1) * DV],
                                                 op0=ALU.mult, op1=ALU.add)
                free(ins, ("gkv", i))
                dve.wait_ge(S("gla_rms"), i + 1)
                link(v.tensor_tensor(gv[0:r, :].rearrange("p (h c) -> p h c", h=HB),
                                     gv[0:r, :].rearrange("p (h c) -> p h c", h=HB),
                                     col(A_GR, HB, r).unsqueeze(2).broadcast_to([r, HB, DV]), ALU.mult))
                v.tensor_tensor(gv[0:r, :], gv[0:r, :], ogz[0:r, i, 0:HB * DV], ALU.mult).then_inc(S("gla_gated"), 1)
                dve.wait_ge(S("ssd_rms"), i + 1)
                v.tensor_tensor(yv[0:r, :].rearrange("p (g c) -> p g c", g=2),
                                yv[0:r, :].rearrange("p (g c) -> p g c", g=2),
                                col(A_YR, 2, r).unsqueeze(2).broadcast_to([r, 2, HC * PC // 2]),
                                ALU.mult).then_inc(S("ssd_gated"), 1)

            for j in range(5):
                o = full(dve, ("k", j))
                if j < 4:
                    free(v.tensor_copy(kT[:, j, 0:SEQ], o[:, :]), ("k", j))
                else:
                    free(v.tensor_copy(kT[:, :, SEQ:TOK], o[:, 0:4 * DEC].rearrange("p (j t) -> p j t", j=4)), ("k", j))
            for i in range(NT):
                r = ROWS[i]
                o = full(dve, ("kn", i))
                if i >= 2:
                    dve.wait_ge(S(f"k_out{i % 2}"), 16 * (i // 2))
                free(v.tensor_copy(stage[0:r, i % 2, WA:2 * WA], o[0:r, :]), ("kn", i))
            dve.wait_ge(S("bias_in"), 16)
            link(v.memset(bias[0:P // 2, :, 0:P // 2], NEG))

            def att_norm(i):
                r = ROWS[i]
                dve.wait_ge(S("pv"), HA * (i + 1))
                c = A_SUM + (i % 2) * HA
                link(v.reciprocal(col(A_RSUM + (i % 2) * HA, HA, r), col(c, HA, r)))
                o = bank[i % 2]
                free(v.tensor_tensor(stage[0:r, i % 2, 0:WA].rearrange("p (h d) -> p h d", h=HA),
                                     o[0:r, :].rearrange("p (h d) -> p h d", h=HA),
                                     col(A_RSUM + (i % 2) * HA, HA, r).unsqueeze(2).broadcast_to([r, HA, DH]), ALU.mult),
                     ("ao", i))

            def att_out(i):
                r = ROWS[i]
                if i == 0:
                    dve.wait_ge(S("states_out"), 16 * (2 + 2 * HB + 4))
                o = full(dve, ("aoT", i))
                free(v.tensor_copy(mixT[:, 0:4, T0[i]:T0[i] + r], o[:, 0:4 * r].rearrange("p (k t) -> p k t", k=4)),
                     ("aoT", i))

            for n in range(NT * HA + 3):
                if n < NT * HA:
                    i, h = divmod(n, HA)
                    r, nk = ROWS[i], nkeys(i)
                    o = full(dve, ("S", n))
                    if i == NT - 1:
                        link(v.tensor_tensor(o[0:r, P:nk], o[0:r, P:nk], bias[0:r, h, 2 * P - 1:P // 2 - 1:-1], ALU.add))
                    else:
                        w = min(nk, 2 * P)
                        link(v.tensor_tensor(o[0:r, nk - w:nk], o[0:r, nk - w:nk], bias[:, h, w - 1::-1], ALU.add))
                    v.tensor_reduce(col(A_NM + n % 4, 1, r), o[0:r, 0:nk], AX.X, ALU.max, negate=True).then_inc(S("negmax"), 1)
                if n >= 10 and (n - 10) % HA == 0 and (n - 10) // HA < NT - 1:
                    att_norm((n - 10) // HA)
                    att_out((n - 10) // HA)
            att_norm(NT - 1)
            att_out(NT - 1)

            dve.wait_ge(S("x1_in_residual"), 16 * NT)
            dve.wait_ge(S("norm_rows_in"), 32)
            dve.wait_ge(S("router_b_in"), 32)
            link(v.memset(lgt[:, :, :], 0.0))
            for i in range(NT):
                r = ROWS[i]
                for hf in range(2):
                    o = full(dve, ("wo", i, hf))
                    x = x1[0:r, i, hf * 512:(hf + 1) * 512]
                    free(v.tensor_tensor(x, x, o[0:r, :], ALU.add), ("wo", i, hf))
                dve.wait_ge(S("norm2_sq"), i + 1)
                mean(A_SSQ + i, A_MS + i, 1, r, D, "norm2_mean")
                dve.wait_ge(S("norm2_rms"), i + 1)
                if i >= 2:
                    dve.wait_ge(S(f"h2_out{i % 2}"), 16 * (i // 2))
                v.scalar_tensor_tensor(out=h2[0:r, i % 2, :], in0=x1[0:r, i, :], scalar=col(A_RS + i, 1, r),
                                       in1=w2b[0:r, :], op0=ALU.mult, op1=ALU.mult).then_inc(S("h2"), 1)
                o = full(dve, ("h2T", i, 1))
                free(v.tensor_copy(hT[:, 4:8, T0[i]:T0[i] + r], o[:, 0:4 * r].rearrange("p (k t) -> p k t", k=4)),
                     ("h2T", i, 1))
                o = full(dve, ("lg", i))
                free(v.tensor_tensor(lgt[0:r, i, :], o[0:r, 0:NG + NE], rb[0:r, :], ALU.add), ("lg", i))
            drained(dve, ("lg", NT - 1))

            def R(k, n=4):
                return rt[:, k, :, 0:n]

            def over(x, n):
                return x.broadcast_to([P, NT, n])

            dve.wait_ge(S("zeroed"), 1)
            link(v.tensor_copy(desc[:, :], ri[:, 40:44]))
            link(v.tensor_copy(ebase[:, :], ri[:, 48:48 + NE]))

            def first_max(x, m, one_hot):
                link(v.tensor_reduce(m, x, AX.X, ALU.max))
                link(v.tensor_tensor(R(R_EQ), x, over(m, 4), ALU.is_equal))
                link(v.tensor_tensor(R(R_EQ), R(R_EQ), desc[:, :].unsqueeze(1).broadcast_to([P, NT, 4]), ALU.mult))
                link(v.tensor_reduce(rt[:, R_X, :, 0:1], R(R_EQ), AX.X, ALU.max))
                link(v.tensor_tensor(one_hot, R(R_EQ), over(rt[:, R_X, :, 0:1], 4), ALU.is_equal))

            G = lgt[:, :, 0:NG]
            VMG, VS, VP, VM1, VM2 = (rt[:, R_X, :, c:c + 1] for c in (1, 2, 3, 4, 5))
            VE, VD, VW1, VW2 = (rt[:, R_V, :, c:c + 1] for c in (0, 1, 2, 3))
            first_max(G, VMG, R(R_OHG))
            v.tensor_tensor(R(R_SUB), G, over(VMG, 4), ALU.subtract).then_inc(S("router_sub"), 1)
            link(v.tensor_tensor(rt[:, R_TMP, :, :].rearrange("p i (g j) -> p i g j", g=NG),
                                 lgt[:, :, NG:].rearrange("p i (g j) -> p i g j", g=NG),
                                 R(R_OHG).unsqueeze(3).broadcast_to([P, NT, NG, EG]), ALU.mult))
            for i in range(NT):
                ins = v.tensor_reduce(rt[:, R_SEL, i, 0:4], rt[:, R_TMP, i, :].rearrange("p (g j) -> p j g", g=NG), AX.X, ALU.add)
            link(ins)
            first_max(R(R_SEL), VM1, R(R_K1))
            link(v.scalar_tensor_tensor(out=R(R_L2), in0=R(R_K1), scalar=NEG, in1=R(R_SEL), op0=ALU.mult, op1=ALU.add))
            first_max(R(R_L2), VM2, R(R_K2))
            dve.wait_ge(S("router_exp"), 1)
            v.tensor_tensor(VE, VM2, VM1, ALU.subtract).then_inc(S("router_sub"), 1)
            for k, a_ in ((R_K1, R_A1), (R_K2, R_A2)):
                for i in range(NT):
                    ins = v.tensor_tensor(rt[:, a_, i, :].rearrange("p (g j) -> p g j", g=NG),
                                          rt[:, R_OHG, i, 0:4].unsqueeze(2).broadcast_to([P, NG, EG]),
                                          rt[:, k, i, 0:4].unsqueeze(1).broadcast_to([P, NG, EG]), ALU.mult)
            link(ins)
            v.tensor_tensor(R(R_A, NE), R(R_A1, NE), R(R_A2, NE), ALU.add).then_inc(S("picks"), 1)
            link(v.tensor_reduce(VS, R(R_SUB), AX.X, ALU.add))
            dve.wait_ge(S("router_exp"), 2)
            link(v.tensor_scalar(VD, VE, 1.0, None, ALU.add))
            link(v.tensor_tensor(VD, VD, VS, ALU.mult))
            link(v.reciprocal(VW1, VD))
            link(v.tensor_tensor(VW2, VW1, VE, ALU.mult))
            o = full(dve, "pos")
            link(v.memset(rt[:, R_POS, NT - 1, :], 0.0))
            v.tensor_copy(R(R_POS, NE)[:, 0:nb, :], o[:, 0:nb * NE].rearrange("p (i e) -> p i e", i=nb))
            free(v.tensor_copy(rt[0:DEC, R_POS, NT - 1, :], o[0:DEC, nb * NE:NT * NE]), "pos")
            drained(dve, "pos")
            link(v.tensor_tensor(R(R_SLOT, NE), R(R_POS, NE), ebase[:, :].unsqueeze(1).broadcast_to([P, NT, NE]), ALU.add))
            for k, a_ in ((0, R_A1), (1, R_A2)):
                for n, src in ((6, R_POS), (8, R_SLOT)):
                    link(v.tensor_tensor(R(R_TMP, NE), R(a_, NE), R(src, NE), ALU.mult))
                    link(v.tensor_reduce(rt[:, R_X, :, n + k:n + k + 1], R(R_TMP, NE), AX.X, ALU.add))
            place_, slot = rt[:, R_X, :, 6:8], rt[:, R_X, :, 8:10]
            for n in range(1, ROUNDS):
                link(v.tensor_scalar(rt[:, R_X, :, 10:12], place_, float(n * CAP), float(SPAN - CAP), ALU.is_ge, ALU.mult))
                link(v.tensor_tensor(slot, slot, rt[:, R_X, :, 10:12], ALU.add))
            for k in range(2):
                ins = v.tensor_copy(ri[:, k * NT:(k + 1) * NT], rt[:, R_X, :, 8 + k])
            ins.then_inc(S("slots"), 1)
            o = full(dve, "tot")
            free(v.tensor_reduce(col(A_MAX), o[:, 0:NE], AX.X, ALU.max), "tot")
            drained(dve, "tot")
            v.tensor_copy(ri[:, 60:61], col(A_MAX)).then_inc(S("max_count"), 1)

            dve.wait_ge(S("ids_in"), 16)
            v.tensor_copy(idf[:, :], idi[:, :]).then_inc(S("ids_f"), 1)
            o = full(dve, "ids")
            free(v.tensor_copy(ri[:, 16:16 + NE], o[:, 0:NE]), "ids")

            for e in range(-1, NE + 1):
                if e + 1 < NE:
                    o = full(dve, ("xgT", e + 1, 1))
                    free(v.tensor_copy(xgT[:, (e + 1) % 2, 4:8, :], o[:, :].rearrange("p (k c) -> p k c", k=4)),
                         ("xgT", e + 1, 1))
                if 0 <= e < NE:
                    dve.wait_ge(S("silu"), e + 1)
                    if e >= 2:
                        filled(dve, ("hT", e - 2))
                    free(v.tensor_tensor(hid[:, e % 2, :], bank[2 + e % 2][:, FE:2 * FE], sg[:, e % 2, :], ALU.mult),
                         ("gu", e))
                if e >= 1:
                    d = e - 1
                    if d >= 2:
                        dve.wait_ge(S(f"y_out{d % 2}"), 16 * (d // 2))
                    o = full(dve, ("ye", d, 1))
                    free(v.tensor_copy(ye[:, d % 2, 512:1024], o[:, :]), ("ye", d, 1))

            dve.wait_ge(S("max_count"), 1)
            fullest = dve.value_load(ri[0:1, 60:61], min_val=0, max_val=TOK)
            with dve.If(fullest > CAP):
                with dve.Fori(0, MORE) as t:
                    dve.wait_ge(S("more_silu"), t + 1)
                    v.tensor_tensor(hid[:, 0, :], bank[2][:, FE:2 * FE], sg[:, 0, :], ALU.mult).then_inc(S("more_hidden"), 1)
            dve.nop()

            def final(i):
                r = ROWS[i]
                dve.wait_ge(S("final_sq"), i + 1)
                mean(A_SSQ + i, A_MS + i, 1, r, D, "final_mean")
                dve.wait_ge(S("final_rms"), i + 1)
                if i >= 2:
                    dve.wait_ge(S(f"y_final{i % 2}"), 16 * (i // 2))
                v.scalar_tensor_tensor(out=ye[0:r, i % 2, :], in0=x1[0:r, i, :], scalar=col(A_RS + i, 1, r),
                                       in1=wfb[0:r, :], op0=ALU.mult, op1=ALU.mult).then_inc(S("y_normed"), 1)

            for i in range(NT):
                r = ROWS[i]
                dve.wait_ge(S(f"yg{i % 2}_in"), 32 * (i // 2 + 1))
                link(v.scalar_tensor_tensor(out=x1[0:r, i, :], in0=xg[0:r, i % 2, :], scalar=rt[0:r, R_V, i, 2:3],
                                            in1=x1[0:r, i, :], op0=ALU.mult, op1=ALU.add))
                v.scalar_tensor_tensor(out=x1[0:r, i, :], in0=xgT[0:r, i % 2, :, :].rearrange("p k c -> p (k c)"),
                                       scalar=rt[0:r, R_V, i, 3:4], in1=x1[0:r, i, :], op0=ALU.mult,
                                       op1=ALU.add).then_inc(S("combined"), 1)
                if i >= 1:
                    final(i - 1)
            final(NT - 1)


_INS = ['x_prompt', 'x_sample', 'cache_k_a', 'cache_v_a', 'state_gla', 'state_conv', 'state_ssm', 'norm1_w', 'w_in',
        'rel_bias_table', 'gla_w_gate_up', 'gla_b_gate', 'gla_norm_w', 'ssm_conv_w', 'ssm_conv_b', 'ssm_dt_bias',
        'ssm_a_log', 'ssm_d', 'ssm_norm_w', 'w_out', 'norm2_w', 'router_group_w', 'router_group_b',
        'router_expert_w', 'router_expert_b', 'exp_w_gate', 'exp_w_up', 'exp_w_down', 'final_norm_w']


def kernel(**inputs):
    import numpy as _np
    import concourse.bacc as _bacc
    from concourse import mybir as _mybir
    from concourse.bass_utils import run_bass_kernel_spmd as _run

    nc = _bacc.Bacc("TRN2", target_bir_lowering=False, num_devices=1)
    arrays, ins = {}, []
    for name in _INS:
        a = _np.ascontiguousarray(inputs[name])
        arrays[f"in_{name}"] = a
        ins.append(nc.dram_tensor(f"in_{name}", a.shape, _mybir.dt.from_np(a.dtype), kind="ExternalInput").ap())
    sh = {k: v.shape for k, v in inputs.items()}
    b, seq, d = sh['x_prompt']
    db, dec, _ = sh['x_sample']
    depth, _, _, ha, dh = sh['cache_k_a']
    window = 512
    shapes = [(b, seq, d), (db, dec, d),
              (depth, b, min(window, seq), ha, dh), (depth, b, min(window, seq), ha, dh),
              (depth, b) + sh['state_gla'][2:], (depth, b) + sh['state_conv'][2:], (depth, b) + sh['state_ssm'][2:],
              (depth, db, dec, ha, dh), (depth, db, dec, ha, dh),
              sh['state_gla'], sh['state_conv'], sh['state_ssm']]
    outs = [nc.dram_tensor(f"out_{i}", s, _mybir.dt.float32, kind="ExternalOutput").ap() for i, s in enumerate(shapes)]
    encoder_layer(nc, ins, outs)
    r = _run(nc, [arrays], core_ids=[0])
    return tuple(r.results[0][f"out_{i}"] for i in range(len(shapes)))
```

```python
from contextlib import ExitStack

import concourse.bass as bass
import numpy as np
from concourse import mybir
from concourse.alu_op_type import AluOpType as ALU

ACT = mybir.ActivationFunctionType
AX = mybir.AxisListType
F32 = mybir.dt.float32
I32 = mybir.dt.int32
U32 = mybir.dt.uint32
BF16 = mybir.dt.bfloat16
P = 128


def encoder_layer(nc, ins, outs):
    (x_prompt, x_sample, cache_k, cache_v, state_gla, state_conv, state_ssm, norm1_w, w_in, rel_table,
     gate_up, b_gate, gla_norm_w, conv_w, conv_b, dt_bias, a_log, d_skip, ssm_norm_w, w_out, norm2_w,
     rg_w, rg_b, re_w, re_b, exp_gate, exp_up, exp_down, final_w) = ins
    (y_prompt, y_sample, o_pk, o_pv, o_pg, o_pc, o_ps, o_sk, o_sv, o_sg, o_sc, o_ss) = outs

    D = x_prompt.shape[2]
    SEQ, DEC = x_prompt.shape[1], x_sample.shape[1]
    KD = D // P
    NT = SEQ // P + 1
    TOK = SEQ + DEC
    ROWS = [P] * (NT - 1) + [DEC]
    T0 = [P * i for i in range(NT)]
    HA, DH = cache_k.shape[3], cache_k.shape[4]
    WA = HA * DH
    PAST = cache_k.shape[2]
    HB, DK, DV = state_gla.shape[2:]
    HC, PC, NS = state_ssm.shape[2:]
    TAPS, CH = conv_w.shape[1:]
    NE, _, FE = exp_gate.shape[1:]
    NG = rg_w.shape[2]
    EG = NE // NG
    RANK = gate_up.shape[1]
    EPS = 1e-6
    NEG = -1e30
    CLIP = (rel_table.shape[2] - 1) // 2
    CAP = P
    ROUNDS = -(-TOK // CAP)
    MORE = (ROUNDS - 1) * NE
    SPAN = NE * CAP
    AHEAD = 3
    assert (D, SEQ, DEC, PAST, CLIP) == (1024, 512, 64, 256, 128) and WA == 512 and CH == 512

    C_Q, C_K, C_V = 0, WA, 2 * WA
    C_BQ = 3 * WA
    C_BK = C_BQ + HB * DK
    C_BV = C_BK + HB * DK
    C_LR = C_BV + HB * DV
    C_OG = C_LR + RANK
    C_Z = C_OG + HB * DV
    C_XBC = C_Z + HC * PC
    C_DT = C_XBC + CH
    COLS = C_DT + HC

    with ExitStack() as ctx:
        sems = {}

        def S(name):
            if name not in sems:
                sems[name] = ctx.enter_context(nc.semaphore(name))
            return sems[name]

        place = [0]

        def sb(name, shape, dt=F32, at=None):
            size = int(np.prod(shape[1:])) * mybir.dt.size(dt)
            size += (-size) % 32
            if at is None:
                at = place[0]
                place[0] += size
            return nc.alloc_sbuf_tensor_at(name, shape, dt, offset=base + at), at, at + size

        base = -(-nc.sbuf_base // 32) * 32

        SLOT_W = 528
        NSLOT = 3
        wring, _, _ = sb("weight_ring", [P, NSLOT, KD * SLOT_W])
        down, down_at, down_end = sb("down_ring", [P, 2, FE // P * D])
        ident, _, _ = sb("ident", [P, P])
        triu, _, _ = sb("triu", [P, P])
        striu, _, _ = sb("striu", [P, P])
        ones, _, _ = sb("ones", [P, P])
        par, _, _ = sb("params_T", [P, 64])
        small, _, _ = sb("small", [P, 256])
        hT, hT_at, hT_end = sb("hT", [P, KD, TOK])
        mixT, mixT_at, e = sb("mixT", [P, KD, TOK])
        cso, _, e = sb("conv_state_out", [4, 2, CH], at=mixT_at)
        sto, _, e = sb("ssd_state_out", [PC, 2, 2 * P], at=e)
        assert e <= mixT_at + 4 * WA // P * TOK
        iot, _, e = sb("iota", [P, 2, P], I32, at=mixT_at + 4 * WA // P * TOK)
        lvf, _, e = sb("level_compare", [P, 3, P], at=e)
        prow, _, e = sb("params_rows", [64, P], at=e)
        gth, _, e = sb("gates_tanh", [P, 2, 512], at=e)
        assert e <= mixT_at + 4 * KD * TOK
        stage, stage_at, _ = sb("stage", [P, 2, D])
        mixer_at = place[0]
        kB, _, _ = sb("gla_kT", [P, TOK])
        qB, _, _ = sb("gla_qT", [P, TOK])
        bcum, _, _ = sb("gla_b", [P, TOK])
        wup, _, _ = sb("gla_w_up", [RANK, HB * DK])
        qbd, _, _ = sb("gla_q_blocks", [P, HB, P])
        qE, _, _ = sb("gla_q_decayed", [P, 2, HB, P])
        kE, _, _ = sb("gla_k_decayed", [P, 2, P])
        dif, _, _ = sb("gla_exponents", [P, 2, P])
        att, _, _ = sb("gla_scores", [P, HB, P])
        qs, _, _ = sb("gla_q_from_start", [P, P])
        kd, _, _ = sb("gla_k_to_end", [P, P])
        kdn, _, _ = sb("gla_k_to_end_nat", [P, P])
        Sg, _, _ = sb("gla_state", [P, 2, HB, DV])
        bv, _, _ = sb("gla_v", [P, NT, HB * DV])
        ogz, _, _ = sb("gates", [P, NT, HB * DV + HC * PC])
        lmask, _, _ = sb("level_masks", [P, 8, P], mybir.dt.uint8)
        gv, _, _ = sb("gla_o", [P, HB * DV])
        gt, _, _ = sb("gla_o_tmp", [P, HB * DV])
        xpre, _, e = sb("conv_in", [P, CH // P, TOK + 6], at=down_at)
        ctmp, _, e = sb("conv_sum", [P, 2, TOK + 4], at=e + (-e) % 32)
        thx, _, e = sb("conv_tanh", [P, TOK + 4], at=e + (-e) % 32)
        assert e <= down_end
        h2T, _, e = sb("h2T", [P, 2, KD, P], at=down_at + 4 * (FE // P) * D)
        assert e <= down_end
        xnat, _, _ = sb("xB_nat", [P, 3 * P])
        dec, _, _ = sb("ssd_decay", [P, HC, P])
        cbm, _, _ = sb("ssd_cb", [P, 2, P])
        xdt, _, _ = sb("ssd_x_dt", [P, HC, PC])
        xw, _, _ = sb("ssd_x_w", [P, HC, PC])
        xD, _, _ = sb("ssd_x_skip", [P, HC, PC])
        hst, _, _ = sb("ssd_state", [P, 2, 2, PC])
        yv, _, _ = sb("ssd_y", [P, HC * PC])
        yt, _, _ = sb("ssd_tmp", [P, HC * PC])
        xc, xc_at, xc_end = sb("conv_out", [P, CH // P, TOK + 4])
        ckT, _, e = sb("att_cached_kT", [P, WA // P, PAST], at=xc_at)
        cv, _, e = sb("att_cached_v", [P, PAST // P, WA], at=e)
        assert e <= xc_end
        qT, qT_at, _ = sb("att_qT", [P, WA // P, TOK])
        kT, kT_at, kT_end = sb("att_kT", [P, WA // P, TOK])
        V, _, _ = sb("att_v", [P, NT, WA])
        mixer_end = place[0]
        rtab, _, _ = sb("bias_table", [HA, 2 * CLIP + 1], at=qT_at)
        xrel, _, e = sb("bias_table_long", [HA, 384], at=qT_at + 1056)
        xlast, _, e = sb("x_last_tile", [P, D], at=e)
        assert e <= kT_at
        gtmp, _, e = sb("gla_tmp", [P, 2, TOK], at=kT_at)
        lrT, _, e = sb("gla_lowrank", [RANK, TOK], at=e)
        assert e <= kT_end
        bias, _, e = sb("att_bias", [P, HA, 2 * P], at=hT_at)
        Pm, _, e = sb("att_p", [P, 2, 512], at=e)
        PT, _, e = sb("att_pT", [P, 2, 512], at=e)
        assert e <= hT_end
        x1, _, e = sb("x1", [P, NT, D], at=mixer_at)
        h2, _, e = sb("h2", [P, 2, D], at=e)
        w2b, _, e = sb("norm2_b", [P, D], at=e)
        wfb, _, e = sb("final_b", [P, D], at=e)
        attn, _, e2 = sb("att_out", [P, 2, WA], at=e)
        dump, _, e2 = sb("norm2_squares", [P, D], at=e2)
        xg, _, e = sb("expert_x", [P, 2, D], at=e)
        assert e2 <= e
        lgt, _, e = sb("router_logits", [P, NT, NG + NE], at=e)
        ones_b, _, e = sb("ones_bf16", [P, P], BF16, at=e)
        before_b, _, e = sb("earlier_bf16", [P, P], BF16, at=e)
        tokid, _, e = sb("token_parts", [P, NT, 2], BF16, at=e)
        assert e <= xc_at, (e, xc_at)
        xgT, _, e = sb("expert_xT", [P, 2, KD, CAP], at=e)
        sg, _, e = sb("expert_silu", [P, 2, FE], at=e)
        hid, _, e = sb("expert_hidden", [P, 2, FE], at=e)
        hidT, _, e = sb("expert_hiddenT", [P, 2, FE // P, CAP], at=e)
        ye, _, e = sb("expert_y", [P, 2, D], at=e)
        rt, _, e = sb("router", [P, 20, NT, NE], at=e)
        picked, _, e = sb("picked", [P, NT, NE], BF16, at=e)
        place_e, _, e = sb("place_or_none", [P, NT, NE], at=e)
        idp, _, e = sb("token_tile_start", [P, 2, 1], at=e)
        onehot, _, e = sb("slot_one_hot", [P, 2, NT, CAP], BF16, at=e)
        moe_end = e
        rw, _, _ = sb("router_w", [P, KD, NG + NE])
        rb, _, _ = sb("router_b", [P, NG + NE])
        desc, _, _ = sb("router_order", [P, 4])
        ebase, _, _ = sb("expert_base", [P, NE])
        ri, _, _ = sb("router_index", [P, 64], I32)
        slot_i, _, _ = sb("slot_iota_i", [P, CAP], I32)
        slot_f, _, _ = sb("slot_iota", [P, CAP])
        zmap, _, _ = sb("zero_map", [P, ROUNDS * SPAN // P], I32)
        dtw, _, _ = sb("dt_work", [P, 10, NT * HC])
        assert moe_end <= mixer_end, (moe_end, mixer_end)
        assert base + place[0] <= nc.sbuf_usable_end

        A_SSQ, A_MS, A_RS, A_MH = 0, 8, 16, 24
        A_NA, A_DTB, A_D, A_AL = 44, 48, 52, 56
        A_A, A_CS, A_DT = 60, 80, 100
        A_CSL, A_ECL, A_W, A_ECS = 120, 124, 128, 132
        A_NM, A_SUM, A_RSUM = 136, 140, 156
        A_GS, A_GR, A_YS, A_YR, A_EBL = 172, 176, 180, 182, 184
        A_MAX = 186
        A_SLOT1, A_SLOT2 = 192, 200
        (R_EQ, R_OHG, R_SUB, R_TMP, R_SEL, R_K1, R_K2, R_L2, R_A1, R_A2, R_A, R_POS, R_V, R_X, R_SLOT) = range(15)

        bank = [ctx.enter_context(nc.psum_tensor(f"bank{b}", [P, 512], F32)) for b in range(8)]

        relpos_d = nc.dram_tensor("relative_bias", [HA, 384], F32, kind="Internal").ap()
        h2_d = nc.dram_tensor("h2_rows", [TOK, D], F32, kind="Internal").ap()
        map_d = nc.dram_tensor("slot_tokens", [ROUNDS * SPAN, 1], I32, kind="Internal").ap()
        y_d = nc.dram_tensor("slot_outputs", [ROUNDS * SPAN, D], F32, kind="Internal").ap()

        G1, G2, GCW, GCB, GBG, GGN, GSN, GCS = 0, 8, 16, 32, 36, 37, 38, 40
        NPAR = 52

        block = ctx.enter_context(nc.Block())

        fills, count, full_count = {}, [0] * 8, [0] * 8
        behind = []

        def tile_x(i, lo=0, hi=None):
            hi = D if hi is None else hi
            return x_prompt[0, T0[i]:T0[i] + P, lo:hi] if i < NT - 1 else x_sample[0, :, lo:hi]

        def x_in(i):
            r = ROWS[i]
            if i < 2:
                return stage[0:r, i, :]
            if i < 4:
                return V[:, :, :].rearrange("p i c -> p (i c)")[0:r, (i - 2) * D:(i - 1) * D]
            return xlast[0:r, :]

        assert NT == 5
        groups = [(C_BQ, 512), (C_LR, RANK + 512), (C_XBC, CH), (C_Q, WA), (C_K, WA), (C_V, WA)]
        G_B, G_LR, G_XBC, G_Q, G_K, G_V, G_WO0, G_WO1, G_EXP = range(9)

        def ring(g, width):
            return wring[:, g % NSLOT, 0:KD * width].rearrange("p (k c) -> p k c", k=KD)

        def chosen(i, k):
            return wring[:, :, :].rearrange("p s c -> p (s c)")[0:ROWS[i], (2 * i + k) * D:(2 * i + k + 1) * D]

        def w_done(g):
            return sum(32 if k == G_B or k >= G_EXP else 16 for k in range(g % NSLOT, g + 1, NSLOT))

        HALF = TOK // 2
        HALVES = [slice(0, HALF), slice(HALF, TOK)]
        NA = NT * HA
        LAST_STEP = 17
        WO_PARTS = {2: 3, 3: 3, 4: 2, 6: 3, 7: 3, 8: 2}
        WO_ADD = {5: 0, 9: 1}

        def steps_behind(n):
            return [(i, n - 10 - HA * i) for i in reversed(range(NT)) if 0 <= n - 10 - HA * i <= LAST_STEP]

        HEADS = NA + 3 + LAST_STEP
        LEV = [64, 32, 16, 8, 4, 2, 1]

        def levels(i):
            return [m for m in LEV if 2 * m <= ROWS[i]] + [0]

        def seq(i):
            return i // (NT - 1)

        def nkeys(i):
            return T0[i] + P if i < NT - 1 else PAST + DEC

        def cols(i):
            c = T0[i] + (3 if i == NT - 1 else 0)
            return slice(c, c + ROWS[i])

        lev_key = [("lev", i, n) for i in range(NT) for n in range(len(levels(i)) - 1)]
        n_lev = [sum(len(levels(j)) for j in range(i)) for i in range(NT + 1)]

        def full(eng, key):
            b, n, _ = fills[key]
            eng.wait_ge(S(f"bank{b}_full"), n)
            return bank[b]

        def filled(eng, key):
            full(eng, key)

        def drained(eng, key):
            b, _, n = fills[key]
            eng.wait_ge(S(f"bank{b}_free"), n)

        def free(ins, key):
            ins.then_inc(S(f"bank{fills[key][0]}_free"), 1)

        @block.tensor
        def _(pe):
            mm, tr = nc.tensor.matmul, nc.tensor.transpose

            def fill(key, b):
                if count[b] > 0:
                    pe.wait_ge(S(f"bank{b}_free"), count[b])
                count[b] += 1
                full_count[b] += 1
                fills[key] = (b, full_count[b], count[b])
                return bank[b]

            def done(ins, key):
                ins.then_inc(S(f"bank{fills[key][0]}_full"), 1)

            pe.wait_ge(S("consts"), 1)
            pe.wait_ge(S("params_in"), 16 * 9)
            o = fill("par", 4)
            done(tr(o[:, 0:NPAR], prow[0:NPAR, :], ident[0:NPAR, 0:NPAR]), "par")
            for i in range(NT):
                r = ROWS[i]
                pe.wait_ge(S("x_normed"), i + 1)
                for hf in range(2):
                    o = fill(("xT", i, hf), 2 + hf)
                    for k in range(4):
                        last = tr(o[:, k * r:k * r + r], x_in(i)[:, (4 * hf + k) * P:(4 * hf + k + 1) * P], ident[0:r, 0:r])
                    done(last, ("xT", i, hf))
            pe.wait_ge(S("state_in"), 16 * HC)
            o = fill("s0T", 4)
            for j in range(2):
                last = tr(o[:, j * PC:(j + 1) * PC], yt[0:PC, j * P:(j + 1) * P], ident[0:PC, 0:PC])
            done(last, "s0T")
            drained(pe, ("xT", NT - 1, 0))
            drained(pe, ("xT", NT - 1, 1))

            def proj_T(w, c0, m, half, b):
                for k in range(KD):
                    last = mm(bank[b][0:m, 0:HALF], w[:, k, c0:c0 + m], hT[:, k, half], start=(k == 0), stop=(k == KD - 1))
                return last

            def proj_nat(w, c0, n, i, b):
                for k in range(KD):
                    last = mm(bank[b][0:ROWS[i], 0:n], hT[:, k, T0[i]:T0[i] + ROWS[i]], w[:, k, c0:c0 + n],
                              start=(k == 0), stop=(k == KD - 1))
                return last

            def landed(g):
                pe.wait_ge(S(f"w{g % NSLOT}_in"), w_done(g))

            landed(G_B)
            w = ring(G_B, 512 + HC)
            for j, nm in enumerate(("bq", "bk")):
                for n, half in enumerate(HALVES):
                    fill((nm, n), 2 * j + n)
                    done(proj_T(w, j * P, P, half, 2 * j + n), (nm, n))
            for i in range(NT):
                fill(("bv", i), i % 2)
                done(proj_nat(w, 2 * P, HB * DV + HC, i, i % 2), ("bv", i))
            def gla_gate():
                drained(pe, ("lr", 0))
                drained(pe, ("lr", 1))
                pe.wait_ge(S("wup_in"), 16)
                for n, half in enumerate(HALVES):
                    o = fill(("gate", n), 2 + n)
                    done(mm(o[:, 0:HALF], wup[:, :], lrT[:, half], start=True, stop=True), ("gate", n))

            landed(G_LR)
            w = ring(G_LR, RANK + 512)
            for n, half in enumerate(HALVES):
                fill(("lr", n), 2 + n)
                done(proj_T(w, 0, RANK, half, 2 + n), ("lr", n))
            for i in range(NT):
                fill(("ogz", i), i % 2)
                done(proj_nat(w, RANK, 512, i, i % 2), ("ogz", i))
            gla_gate()
            landed(G_XBC)
            w = ring(G_XBC, CH)
            for j in range(4):
                for n, half in enumerate(HALVES):
                    fill(("xbc", j, n), n)
                    done(proj_T(w, j * P, P, half, n), ("xbc", j, n))

            def attention_projections():
                turn = 0

                def result(key):
                    behind.append((key, len(fills)))

                for g, nm in ((G_Q, "q"), (G_K, "k")):
                    landed(g)
                    w = ring(g, WA)
                    for n in range(8):
                        j, half = n // 2, HALVES[n % 2]
                        o = fill((nm, n), (0, 6)[turn % 2])
                        for k in range(KD):
                            last = mm(o[:, 0:HALF], w[:, k, j * P:(j + 1) * P], hT[:, k, half], start=(k == 0), stop=(k == KD - 1))
                            if k == KD - 1:
                                done(last, (nm, n))
                                result((nm, n))
                            if k % 2:
                                yield
                        turn += 1
                landed(G_V)
                w = ring(G_V, WA)
                for i in range(NT):
                    o = fill(("v", i), (0, 6)[turn % 2])
                    for k in range(KD):
                        last = mm(o[0:ROWS[i], :], hT[:, k, T0[i]:T0[i] + ROWS[i]], w[:, k, :], start=(k == 0), stop=(k == KD - 1))
                        if k == KD - 1:
                            done(last, ("v", i))
                            result(("v", i))
                        yield
                    turn += 1
                drained(pe, ("k", 6))
                drained(pe, ("k", 7))
                for i in range(NT):
                    r = ROWS[i]
                    o = fill(("kn", i), (0, 6)[turn % 2])
                    for j in range(4):
                        last = tr(o[0:r, j * P:(j + 1) * P], kT[:, j, T0[i]:T0[i] + r], ident[:, :])
                    done(last, ("kn", i))
                    result(("kn", i))
                    turn += 1
                    yield

            projections = attention_projections()

            def meanwhile(n):
                for _ in range(n):
                    next(projections, None)

            def ssd_cums():
                pe.wait_ge(S("a_ready"), 1)
                o = fill("cs", 2)
                for i in range(NT):
                    r = ROWS[i]
                    last = mm(o[0:r, i * HC:(i + 1) * HC], triu[0:r, 0:r], small[0:r, A_A + i * HC:A_A + (i + 1) * HC],
                              start=True, stop=True)
                done(last, "cs")

            def conv_state():
                drained(pe, ("xbc", 3, 0))
                drained(pe, ("xbc", 3, 1))
                pe.wait_ge(S("conv_state_placed"), 1)
                for s, c in ((0, SEQ), (1, TOK + 3)):
                    o = fill(("cst", s), 3)
                    for j in range(4):
                        last = tr(o[0:3, j * P:(j + 1) * P], xpre[:, j, c:c + 3], ident[:, :])
                    done(last, ("cst", s))

            def gla_levels(i):
                r = ROWS[i]
                if i:
                    meanwhile(5)
                for n, m in enumerate(levels(i)):
                    b = 4 + n % 2
                    o = fill(("lev", i, n), b)
                    if m:
                        c = n_lev[i] - i + n
                        pe.wait_ge(S("k_decayed"), c + 1)
                        pe.wait_ge(S("q_decayed"), c + 1)
                        last = mm(o[0:r, 0:HB * r], kE[:, c % 2, 0:r], qE[:, c % 2, :, 0:r], start=True, stop=True)
                    else:
                        pe.wait_ge(S("q_blocks"), i + 1)
                        last = mm(o[0:r, 0:HB * r], kB[:, T0[i]:T0[i] + r], qbd[:, :, 0:r], start=True, stop=True)
                    done(last, ("lev", i, n))
                    meanwhile(1)

            def gla_out(i):
                r = ROWS[i]
                pe.wait_ge(S("k_to_end"), i + 1)
                o = fill(("kdT", i), 1)
                done(tr(o[0:r, 0:P], kd[:, 0:r], ident[:, :]), ("kdT", i))
                pe.wait_ge(S("q_from_start"), i + 1)
                if i:
                    drained(pe, ("gkv", i - 1))
                if i == NT - 1:
                    pe.wait_ge(S("gla_state_in"), 16 * HB)
                meanwhile(1)
                drained(pe, ("lev", i, len(levels(i)) - 1))
                o = fill(("go", i), 7)
                for h in range(HB):
                    mm(o[0:r, h * DV:(h + 1) * DV], qs[:, 0:r], Sg[:, seq(i), h, :], start=True, stop=False)
                    last = mm(o[0:r, h * DV:(h + 1) * DV], att[0:r, h, 0:r], bv[0:r, i, h * DV:(h + 1) * DV],
                              start=False, stop=True)
                done(last, ("go", i))
                drained(pe, ("kdT", i))
                o = fill(("gkv", i), 1)
                done(mm(o[:, 0:HB * DV], kdn[0:r, :], bv[0:r, i, :], start=True, stop=True), ("gkv", i))

            def gla_mixT(i):
                r = ROWS[i]
                meanwhile(3)
                pe.wait_ge(S("gla_gated"), i + 1)
                o = fill(("goT", i), 7)
                for j in range(2):
                    last = tr(o[:, j * r:(j + 1) * r], gv[0:r, j * P:(j + 1) * P], ident[0:r, 0:r])
                done(last, ("goT", i))

            def ssd(i):
                r = ROWS[i]
                o = fill(("xn", i), 2)
                for j in range(3):
                    last = tr(o[0:r, j * P:(j + 1) * P], xc[:, j, cols(i)], ident[:, :])
                done(last, ("xn", i))
                o = fill(("csrow", i), 3)
                for h in range(HC):
                    a = small[0:r, A_A + i * HC + h:A_A + i * HC + h + 1].broadcast_to([r, P])
                    last = mm(o[:, h * P:h * P + r], a, triu[0:r, 0:r], start=True, stop=True)
                done(last, ("csrow", i))
                meanwhile(1)
                if i:
                    drained(pe, ("st", i - 1))
                for g in range(2):
                    o = fill(("cby", i, g), (1, 3)[g])
                    b_, c_ = (xc[g * NS:(g + 1) * NS, j, cols(i)] for j in (2, 3))
                    mm(o[0:r, 0:r], b_, c_, start=True, stop=True)
                    done(mm(o[0:r, P:2 * P], c_, hst[g * NS:(g + 1) * NS, seq(i), :, :], start=True, stop=True),
                         ("cby", i, g))
                meanwhile(2)
                pe.wait_ge(S("x_w"), i + 1)
                o = fill(("st", i), 2)
                done(mm(o[:, 0:HC * PC], xnat[0:r, 2 * P:3 * P], xw[0:r, :, :], start=True, stop=True), ("st", i))
                meanwhile(2)
                pe.wait_ge(S("ssd_scores"), i + 1)
                pe.wait_ge(S("x_dt"), i + 1)
                o = fill(("ya", i), 3)
                for h in range(HC):
                    last = mm(o[0:r, h * PC:(h + 1) * PC], dec[0:r, h, 0:r], xdt[0:r, h, :], start=True, stop=True)
                done(last, ("ya", i))

            def ssd_mixT(i):
                r = ROWS[i]
                meanwhile(1)
                pe.wait_ge(S("ssd_gated"), i + 1)
                o = fill(("syT", i), 2)
                for j in range(2):
                    last = tr(o[:, j * r:(j + 1) * r], yv[0:r, j * P:(j + 1) * P], ident[0:r, 0:r])
                done(last, ("syT", i))

            meanwhile(3)
            ssd_cums()
            conv_state()
            meanwhile(6)
            pe.wait_ge(S("conv_out"), 4)
            pe.wait_ge(S("zeroed"), 1)
            drained(pe, "s0T")
            drained(pe, ("bv", NT - 1))
            drained(pe, ("bv", NT - 2))
            drained(pe, ("bk", 0))
            drained(pe, ("bk", 1))
            for i in range(NT):
                gla_levels(i)
                ssd(i)
                gla_out(i)
                gla_mixT(i)
                ssd_mixT(i)
            for s in range(2):
                drained(pe, ("st", NT - 2 + s))
                o = fill(("stT", s), 2)
                for j in range(2):
                    last = tr(o[0:PC, j * P:(j + 1) * P], hst[:, s, j, :], ident[:, :])
                done(last, ("stT", s))

            meanwhile(1000)
            pe.wait_ge(S("cached_k_in"), 16)
            for c in range(PAST // P):
                o = fill(("ckT", c), (0, 6)[c])
                for j in range(4):
                    last = tr(o[:, j * P:(j + 1) * P], stage[:, c, j * P:(j + 1) * P], ident[:, :])
                done(last, ("ckT", c))
            drained(pe, ("ckT", 0))
            drained(pe, ("ckT", 1))

            def scores(n):
                i, h = divmod(n, HA)
                r, j, p0 = ROWS[i], h // 2, (h % 2) * DH
                if n == (NT - 1) * HA:
                    pe.wait_ge(S("cached_v_in"), 16)
                q = qT[p0:p0 + DH, j, T0[i]:T0[i] + r]
                o = fill(("S", n), 4 + h % 2)
                if i < NT - 1:
                    last = mm(o[0:r, 0:nkeys(i)], q, kT[p0:p0 + DH, j, 0:nkeys(i)], start=True, stop=True)
                else:
                    mm(o[0:r, 0:PAST], q, ckT[p0:p0 + DH, j, :], start=True, stop=True)
                    last = mm(o[0:r, PAST:PAST + DEC], q, kT[p0:p0 + DH, j, SEQ:TOK], start=True, stop=True)
                done(last, ("S", n))

            def weigh(n):
                i, h = divmod(n, HA)
                r = ROWS[i]
                nk = nkeys(i)
                blocks = [(c, min(P, nk - c)) for c in range(0, nk, P)]
                drained(pe, ("S", n))
                o = fill(("PT", n), 6 + n % 2)
                for c, w_ in blocks:
                    last = tr(o[0:w_, (c // P) * r:(c // P) * r + r], Pm[0:r, n % 2, c:c + w_], ident[0:r, 0:r])
                done(last, ("PT", n))

            def values(n):
                i, h = divmod(n, HA)
                r = ROWS[i]
                nk = nkeys(i)
                blocks = [(c, min(P, nk - c)) for c in range(0, nk, P)]
                if h == 0:
                    fill(("ao", i), i % 2)
                    full_count[i % 2] -= 1
                drained(pe, ("PT", n))
                for c, w_ in blocks:
                    b = c // P
                    if i < NT - 1:
                        v = V[0:w_, b, h * DH:(h + 1) * DH]
                    else:
                        v = cv[0:w_, b, h * DH:(h + 1) * DH] if c < PAST else V[0:w_, NT - 1, h * DH:(h + 1) * DH]
                    last = mm(bank[i % 2][0:r, h * DH:(h + 1) * DH], PT[0:w_, n % 2, b * r:(b + 1) * r], v,
                              start=(b == 0), stop=(b == len(blocks) - 1))
                last.then_inc(S("pv"), 1)

            def att_mixT(i):
                r = ROWS[i]
                drained(pe, ("ao", i))
                o = fill(("aoT", i), 2)
                for j in range(4):
                    last = tr(o[:, j * r:(j + 1) * r], attn[0:r, i % 2, j * P:(j + 1) * P], ident[0:r, 0:r])
                done(last, ("aoT", i))

            landed(G_WO0)
            landed(G_WO1)
            drained(pe, ("goT", NT - 1))
            drained(pe, ("syT", NT - 1))
            wo_k = {}

            def out_proj(i, parts):
                for _ in range(parts):
                    hf, k = divmod(wo_k.get(i, 0), KD)
                    if k == 0:
                        fill(("wo", i, hf), 3)
                        if hf == 0:
                            drained(pe, ("aoT", i))
                    last = mm(bank[3][0:ROWS[i], 0:512], mixT[:, k, T0[i]:T0[i] + ROWS[i]], ring(G_WO0 + hf, 512)[:, k, :],
                              start=(k == 0), stop=(k == KD - 1))
                    if k == KD - 1:
                        done(last, ("wo", i, hf))
                    wo_k[i] = wo_k.get(i, 0) + 1

            def turn_h2(i, hf):
                r = ROWS[i]
                pe.wait_ge(S("h2"), i + 1)
                o = fill(("h2T", i, hf), 2)
                for k in range(4):
                    last = tr(o[:, k * r:k * r + r], h2[0:r, i % 2, (4 * hf + k) * P:(4 * hf + k + 1) * P], ident[0:r, 0:r])
                done(last, ("h2T", i, hf))

            def logits(i):
                r = ROWS[i]
                drained(pe, ("h2T", i, 0))
                drained(pe, ("h2T", i, 1))
                if i == 0:
                    pe.wait_ge(S("router_w_in"), 32)
                o = fill(("lg", i), 2)
                for k in range(KD):
                    last = mm(o[0:r, 0:NG + NE], h2T[:, i % 2, k, 0:r], rw[:, k, :], start=(k == 0), stop=(k == KD - 1))
                done(last, ("lg", i))

            for n in range(HEADS):
                if n < NA:
                    scores(n)
                if 1 <= n <= NA:
                    weigh(n - 1)
                if 2 <= n <= NA + 1:
                    values(n - 2)
                for i, step in steps_behind(n):
                    if step == 0:
                        att_mixT(i)
                    if step in WO_PARTS:
                        out_proj(i, WO_PARTS[step])
                    if step in (12, 14):
                        turn_h2(i, (step - 12) // 2)
                    if step == 16:
                        logits(i)
            pe.wait_ge(S("picks"), 1)
            o = fill("pos", 5)
            for i in range(NT):
                r = ROWS[i]
                for j in range(i):
                    mm(o[0:r, i * NE:(i + 1) * NE], ones_b[:, 0:r], picked[:, j, :], start=(j == 0), stop=False)
                last = mm(o[0:r, i * NE:(i + 1) * NE], before_b[0:r, 0:r], picked[0:r, i, :], start=(i == 0), stop=True)
            done(last, "pos")
            o = fill("tot", 2)
            for i in range(NT):
                r = ROWS[i]
                last = mm(o[:, 0:NE], ones_b[0:r, :], picked[0:r, i, :], start=(i == 0), stop=(i == NT - 1))
            done(last, "tot")

            def expert_ids(e):
                if e >= NE:
                    return
                pe.wait_ge(S("slot_one_hot"), e + 1)
                o = fill(("ids", e), 4 + e % 2)
                for i in range(NT):
                    r = ROWS[i]
                    last = mm(o[:, 0:2], onehot[0:r, e % 2, i, :], tokid[0:r, i, :], start=(i == 0), stop=(i == NT - 1))
                done(last, ("ids", e))

            def expert_in(e):
                pe.wait_ge(S(f"xg{e % 2}_in"), 16 * (e // 2 + 1))
                for hf in range(2):
                    o = fill(("xgT", e, hf), hf)
                    for k in range(4):
                        last = tr(o[:, k * CAP:(k + 1) * CAP], xg[:, e % 2, (4 * hf + k) * P:(4 * hf + k + 1) * P], ident[:, :])
                    done(last, ("xgT", e, hf))

            def expert_up(e):
                g = G_EXP + e
                pe.wait_ge(S(f"w{g % NSLOT}_in"), w_done(g))
                drained(pe, ("xgT", e, 0))
                drained(pe, ("xgT", e, 1))
                w = wring[:, g % NSLOT, 0:2 * KD * FE].rearrange("p (u k f) -> p k u f", u=2, k=KD)
                o = fill(("gu", e), 2 + e % 2)
                for k in range(KD):
                    last = mm(o[:, :], xgT[:, e % 2, k, :], w[:, k], start=(k == 0), stop=(k == KD - 1))
                done(last, ("gu", e))

            def expert_turn(e):
                drained(pe, ("gu", e))
                o = fill(("hT", e), 4 + e % 2)
                for j in range(FE // P):
                    last = tr(o[:, j * CAP:(j + 1) * CAP], hid[:, e % 2, j * P:(j + 1) * P], ident[:, :])
                done(last, ("hT", e))

            def expert_down(e):
                drained(pe, ("hT", e))
                pe.wait_ge(S(f"down{e % 2}_in"), 16 * (e // 2 + 1))
                for hf in range(2):
                    o = fill(("ye", e, hf), 6 + hf)
                    for j in range(FE // P):
                        last = mm(o[:, :], hidT[:, e % 2, j, :], down[:, e % 2, j * D + hf * 512:j * D + (hf + 1) * 512],
                                  start=(j == 0), stop=(j == FE // P - 1))
                    done(last, ("ye", e, hf))

            for e in range(NE + 1):
                if e == 0:
                    for n in range(AHEAD):
                        expert_ids(n)
                    expert_in(0)
                if e < NE:
                    expert_ids(e + AHEAD)
                    expert_up(e)
                if e >= 1:
                    expert_turn(e - 1)
                if e + 1 < NE:
                    expert_in(e + 1)
                if e >= 1:
                    expert_down(e - 1)
            pe.wait_ge(S("max_count"), 1)
            fullest = pe.value_load(ri[0:1, 60:61], min_val=0, max_val=TOK)
            for key in [("xgT", NE - 1, 0), ("xgT", NE - 1, 1), ("gu", NE - 2), ("hT", NE - 2), ("hT", NE - 1),
                        ("ye", NE - 1, 0), ("ye", NE - 1, 1)]:
                drained(pe, key)
            with pe.If(fullest > CAP):
                with pe.Fori(0, MORE) as t:
                    pe.wait_ge(S("more_x"), (t + 1) * 16)
                    for k in range(KD):
                        last = tr(bank[k // 4][:, k % 4 * CAP:(k % 4 + 1) * CAP], xg[:, 0, k * P:(k + 1) * P], ident[:, :])
                    last.then_inc(S("more_turned"), 1)
                    pe.wait_ge(S("more_xT"), t + 1)
                    pe.wait_ge(S("more_w"), (t + 1) * 48)
                    w = wring[:, 0, 0:2 * KD * FE].rearrange("p (u k f) -> p k u f", u=2, k=KD)
                    for k in range(KD):
                        last = mm(bank[2][:, :], xgT[:, 0, k, :], w[:, k], start=(k == 0), stop=(k == KD - 1))
                    last.then_inc(S("more_up"), 1)
                    pe.wait_ge(S("more_hidden"), t + 1)
                    for j in range(FE // P):
                        last = tr(bank[4][:, j * CAP:(j + 1) * CAP], hid[:, 0, j * P:(j + 1) * P], ident[:, :])
                    last.then_inc(S("more_hidden_turned"), 1)
                    pe.wait_ge(S("more_hiddenT"), t + 1)
                    for hf in range(2):
                        for j in range(FE // P):
                            last = mm(bank[6 + hf][:, :], hidT[:, 0, j, :],
                                      down[:, 0, j * D + hf * 512:j * D + (hf + 1) * 512],
                                      start=(j == 0), stop=(j == FE // P - 1))
                    last.then_inc(S("more_down"), 1)
            pe.nop()

        @block.sync
        def _(sp):
            def load(dst, src, sem):
                sp.dma_start(dst, src).then_inc(S(sem), 16)

            rows = lambda a: a.rearrange("(k p) -> k p", p=P)
            load(x_in(0), tile_x(0), "x0_in")
            load(prow[G1:G1 + 8, :], rows(norm1_w[0]), "params_in")
            load(prow[G2:G2 + 8, :], rows(norm2_w[0]), "params_in")
            load(prow[GCW:GCW + 16, :], conv_w[0].rearrange("t (j p) -> (t j) p", p=P), "params_in")
            load(prow[GCB:GCB + 4, :], rows(conv_b[0]), "params_in")
            load(prow[GBG:GBG + 1, :], rows(b_gate[0]), "params_in")
            load(prow[GGN:GGN + 1, 0:DV], gla_norm_w, "params_in")
            load(prow[GGN:GGN + 1, DV:2 * DV], gla_norm_w, "params_in")
            load(prow[GSN:GSN + 2, :], rows(ssm_norm_w[0]), "params_in")
            load(prow[GCS:GCS + 12, :], state_conv[0, 0].rearrange("t (j p) -> (t j) p", p=P), "params_in")
            for i in range(1, NT):
                load(x_in(i), tile_x(i), f"x{i}_in")
            for at, c, n in ((0, C_BQ, 512), (512, C_DT, HC)):
                load(ring(G_B, 512 + HC)[:, :, at:at + n], w_in[0, :, c:c + n].rearrange("(k p) c -> p k c", p=P), "w0_in")
            load(rtab[:, :], rel_table[0], "table_in")
            bc = lambda a, r: a.broadcast_to([P, r])
            load(small[:, A_AL:A_AL + HC], bc(a_log, HC), "ssd_params_in")
            load(small[:, A_DTB:A_DTB + HC], bc(dt_bias, HC), "ssd_params_in")
            load(small[:, A_D:A_D + HC], bc(d_skip, HC), "ssd_params_in")
            load(wup[:, :], gate_up[0], "wup_in")
            for h in range(HC):
                at = (2 * (h % 2) + h // 2) * NS
                load(yt[0:PC, at:at + NS], state_ssm[0, 0, h], "state_in")
            for g in (1, 2):
                c, w = groups[g]
                load(ring(g, w), w_in[0, :, c:c + w].rearrange("(k p) c -> p k c", p=P), f"w{g}_in")
            sp.wait_ge(S("zeroed"), 1)
            for h in range(HB):
                load(Sg[h * DK:(h + 1) * DK, 1, h, :], state_gla[0, 0, h], "gla_state_in")
            load(map_d.rearrange("(p c) one -> p (c one)", p=P), zmap[:, :], "map_zero")
            load(rw[:, :, 0:NG], rg_w[0].rearrange("(k p) c -> p k c", p=P), "router_w_in")
            load(rw[:, :, NG:NG + NE], re_w[0].rearrange("(k p) c -> p k c", p=P), "router_w_in")
            load(rb[:, 0:NG], bc(rg_b, NG), "router_b_in")
            load(rb[:, NG:NG + NE], bc(re_b, NE), "router_b_in")
            filled(sp, ("xT", NT - 1, 1))
            load(stage[:, :, 0:WA], cache_k[0, 0].rearrange("(c p) h d -> p c (h d)", p=P), "cached_k_in")
            last_use = {G_B: ("bv", NT - 1), G_LR: ("ogz", NT - 1), G_XBC: ("xbc", 3, 1), G_Q: ("q", 7), G_K: ("k", 7),
                        G_V: ("v", NT - 1), G_WO0: ("wo", NT - 1, 0), G_WO1: ("wo", NT - 1, 1)}
            for g in (G_Q, G_K, G_V, G_WO0, G_WO1):
                filled(sp, last_use[g - NSLOT])
                src = (w_in[0, :, groups[g][0]:groups[g][0] + WA] if g <= G_V
                       else w_out[0, :, (g - G_WO0) * 512:(g - G_WO0 + 1) * 512])
                load(ring(g, 512), src.rearrange("(k p) c -> p k c", p=P), f"w{g % NSLOT}_in")
            sp.wait_ge(S("bias_in"), 16)
            sp.wait_ge(S("cached_v_in"), 16)
            drained(sp, ("goT", NT - 1))
            drained(sp, ("syT", NT - 1))
            drained(sp, ("stT", 1))
            sp.wait_ge(S("states_out"), 16 * (2 * HB + 4 + 2))
            for i in range(NT):
                load(x1[0:ROWS[i], i, :], tile_x(i), "x1_in_residual")
            load(w2b[:, :], bc(norm2_w, D), "norm_rows_in")
            load(wfb[:, :], final_w.rearrange("(o d) -> o d", o=1).broadcast_to([P, D]), "norm_rows_in")

            def load_down(e):
                load(down[:, e % 2, :].rearrange("p (j d) -> p j d", j=FE // P),
                     exp_down[0, e].rearrange("(j p) d -> p j d", p=P), f"down{e % 2}_in")

            for e in range(NE):
                g = G_EXP + e
                filled(sp, last_use[g - NSLOT] if g - NSLOT in last_use else ("gu", e - NSLOT))
                dst = wring[:, g % NSLOT, 0:2 * KD * FE].rearrange("p (u k f) -> p u k f", u=2, k=KD)
                load(dst[:, 0], exp_gate[0, e].rearrange("(k p) f -> p k f", p=P), f"w{g % NSLOT}_in")
                load(dst[:, 1], exp_up[0, e].rearrange("(k p) f -> p k f", p=P), f"w{g % NSLOT}_in")
                if e == 0:
                    sp.wait_ge(S("conv_out"), 4)
                    load_down(0)
                if e >= 2:
                    if e == 2:
                        filled(sp, ("lg", NT - 1))
                        load_down(1)
                    filled(sp, ("ye", e - 2, 1))
                    load_down(e)
            sp.wait_ge(S("max_count"), 1)
            fullest = sp.value_load(ri[0:1, 60:61], min_val=0, max_val=TOK)
            drained(sp, ("ye", NE - 1, 1))
            with sp.If(fullest > CAP):
                with sp.Fori(0, MORE) as t:
                    dst = wring[:, 0, 0:2 * KD * FE].rearrange("p (u k f) -> p u k f", u=2, k=KD)
                    e = t % NE
                    for u, w in ((0, exp_gate), (1, exp_up)):
                        sp.dma_start(dst[:, u], w[0, bass.ds(e, 1)].rearrange("o (k p) f -> p (o k) f", p=P)
                                     ).then_inc(S("more_w"), 16)
                    sp.dma_start(down[:, 0, :].rearrange("p (j d) -> p j d", j=FE // P),
                                 exp_down[0, bass.ds(e, 1)].rearrange("o (j p) d -> p (o j) d", p=P)
                                 ).then_inc(S("more_w"), 16)
                    sp.wait_ge(S("more_y"), t + 1)
                    sp.sem_inc(S("more_y_seen"), 1)
            sp.nop()

        @block.gpsimd
        def _(pool):
            chain = [0]

            def link(ins):
                chain[0] += 1
                ins.then_inc(S("pool_chain"), 1)
                pool.wait_ge(S("pool_chain"), chain[0])

            g = nc.gpsimd
            link(g.memset(ones[:, :], 1.0))
            link(g.affine_select(out=triu[:, :], in_=ones[:, :], pattern=[[1, P]], compare_op=ALU.is_ge, fill=0.0,
                                 base=0, channel_multiplier=-1))
            link(g.affine_select(out=striu[:, :], in_=ones[:, :], pattern=[[1, P]], compare_op=ALU.is_gt, fill=0.0,
                                 base=0, channel_multiplier=-1))
            g.tensor_tensor(ident[:, :], triu[:, :], striu[:, :], ALU.subtract).then_inc(S("consts"), 1)
            g.iota(iot[:, 0, :], pattern=[[0, P]], base=0, channel_multiplier=1)
            g.iota(iot[:, 1, :], pattern=[[1, P]], base=0, channel_multiplier=0).then_inc(S("iotas"), 1)
            g.memset(small[:, A_MH:A_MH + 20], -0.5).then_inc(S("half"), 1)
            g.memset(qbd[:, :, :], 0.0)
            g.memset(qE[:, :, :, :], 0.0)
            g.memset(att[:, :, :], 0.0)
            g.memset(Sg[:, :, :, :], 0.0)
            g.memset(hst[:, 0, :, :], 0.0)
            g.memset(dtw[:, :, :], 0.0)
            g.memset(xpre[:, :, 0:3], 0.0)
            link(g.memset(zmap[:, :], 0))
            g.iota(ri[:, 32:32 + NT], pattern=[[P, NT]], base=0, channel_multiplier=1)
            g.iota(ri[:, 48:48 + NE], pattern=[[CAP, NE]], base=0, channel_multiplier=0)
            g.iota(slot_i[:, :], pattern=[[1, CAP]], base=0, channel_multiplier=0)
            g.iota(ri[:, 40:44], pattern=[[-1, 4]], base=4, channel_multiplier=0).then_inc(S("zeroed"), 1)
            pool.wait_ge(S("zeroed"), 1)

            def inv_rms(col, out, n, rows, need, count, sem):
                pool.wait_ge(S(need), count)
                g.tensor_tensor(small[0:rows, out:out + n], small[0:rows, col:col + n],
                                small[0:rows, A_MH:A_MH + n], ALU.pow).then_inc(S(sem), 1)

            pool.wait_ge(S("half"), 1)
            for i in range(NT):
                inv_rms(A_MS + i, A_RS + i, 1, ROWS[i], "norm1_mean", i + 1, "norm1_rms")

            pool.wait_ge(S("rev_ready"), 1)
            g.dma_start(relpos_d[:, 0:383], xrel[:, 0:383]).then_inc(S("rev_out"), 16)
            pool.wait_ge(S("rev_out"), 16)
            began = {key: n for n, key in enumerate(fills)}
            v_done = dict(behind)["v", NT - 1]
            bias_tile = min(i for i in range(NT) if began["ya", i] >= v_done)

            for i in range(NT):
                r = ROWS[i]
                pool.wait_ge(S("q_blocks"), i + 1)
                for n, m in enumerate(levels(i)[:-1]):
                    c = n_lev[i] - i + n
                    pool.wait_ge(S("E"), c + 1)
                    if c >= 2:
                        filled(pool, lev_key[c - 2])
                    g.tensor_tensor(qE[:, c % 2, :, 0:r], qbd[:, :, 0:r],
                                    dif[:, c % 2, 0:r].unsqueeze(1).broadcast_to([P, HB, r]),
                                    ALU.mult).then_inc(S("q_decayed"), 1)
                drained(pool, ("xn", i))
                x = xnat[0:r, 0:2 * P].rearrange("p (h c) -> p h c", h=HC)

                def scaled(dst, col):
                    return g.tensor_tensor(dst[0:r, :, :], x,
                                           small[0:r, col:col + HC].unsqueeze(2).broadcast_to([r, HC, PC]), ALU.mult)

                if i:
                    filled(pool, ("ya", i - 1))
                scaled(xdt, A_DT + i * HC).then_inc(S("x_dt"), 1)
                if i:
                    pool.wait_ge(S("ssd_sum"), i)
                scaled(xD, A_D).then_inc(S("x_skip"), 1)
                pool.wait_ge(S("ssd_w"), i + 1)
                scaled(xw, A_W).then_inc(S("x_w"), 1)
                if i == bias_tile:
                    filled(pool, ("v", NT - 1))
                    src = bass.AP(tensor=relpos_d.tensor, offset=0, ap=[[1, P], [384, HA], [1, 2 * P]])
                    g.dma_start(bias[:, :, :], src).then_inc(S("bias_in"), 16)
                inv_rms(A_GS, A_GR, HB, r, "gla_mean", i + 1, "gla_rms")
                inv_rms(A_YS, A_YR, 2, r, "ssd_mean", i + 1, "ssd_rms")
            for i in range(NT):
                inv_rms(A_MS + i, A_RS + i, 1, ROWS[i], "norm2_mean", i + 1, "norm2_rms")

            pool.wait_ge(S("h2_out0"), 16 * ((NT + 1) // 2))
            pool.wait_ge(S("h2_out1"), 16 * (NT // 2))
            for e in range(NE):
                if e >= 2:
                    filled(pool, ("xgT", e - 2, 1))
                drained(pool, ("ids", e))
                g.indirect_dma_start(out=xg[:, e % 2, :], out_offset=None, in_=h2_d,
                                     in_offset=bass.IndirectOffsetOnAxis(ap=ri[:, 16 + e:17 + e].bitcast(U32), axis=0)
                                     ).then_inc(S(f"xg{e % 2}_in"), 16)
            def combine(slots):
                for i in range(NT):
                    r = ROWS[i]
                    for k in range(2):
                        index = ri[0:r, k * NT + i:k * NT + i + 1].bitcast(U32)
                        g.indirect_dma_start(out=chosen(i, k), out_offset=None, in_=slots,
                                             in_offset=bass.IndirectOffsetOnAxis(ap=index, axis=0)
                                             ).then_inc(S(f"chosen{i}_in"), 16)
                for i in range(NT):
                    inv_rms(A_MS + i, A_RS + i, 1, ROWS[i], "final_mean", i + 1, "final_rms")

            pool.wait_ge(S("max_count"), 1)
            fullest = pool.value_load(ri[0:1, 60:61], min_val=0, max_val=TOK)
            filled(pool, ("ye", NE - 1, 1))
            pool.wait_ge(S("y_out0"), 16 * (NE // 2))
            pool.wait_ge(S("y_out1"), 16 * (NE // 2))
            with pool.If(fullest > CAP):
                pool.wait_ge(S("slots"), 1)
                pool.wait_ge(S("map_zero"), 16)
                for k in range(2):
                    for i in range(NT):
                        r = ROWS[i]
                        index = ri[0:r, k * NT + i:k * NT + i + 1].bitcast(U32)
                        g.indirect_dma_start(out=map_d, out_offset=bass.IndirectOffsetOnAxis(ap=index, axis=0),
                                             in_=ri[0:r, 32 + i:33 + i], in_offset=None).then_inc(S("map_written"), 16)
                pool.wait_ge(S("map_written"), 16 * 2 * NT)
                with pool.Fori(0, MORE) as t:
                    g.dma_start(ri[:, 61:62], map_d[bass.ds(t * CAP + SPAN, CAP), :]).then_inc(S("more_ids"), 16)
                    pool.wait_ge(S("more_ids"), (t + 1) * 16)
                    pool.sem_inc(S("more_ids_seen"), 1)
                    g.indirect_dma_start(out=xg[:, 0, :], out_offset=None, in_=h2_d,
                                         in_offset=bass.IndirectOffsetOnAxis(ap=ri[:, 61:62].bitcast(U32), axis=0)
                                         ).then_inc(S("more_x"), 16)
                    pool.wait_ge(S("more_turned"), t + 1)
                pool.wait_ge(S("more_out"), 16 * MORE)
                combine(y_d)
            with pool.Else():
                combine(y_d[0:SPAN, :])
            pool.nop()

        @block.scalar
        def _(act):
            a = nc.scalar.activation
            own = [0]

            def link(ins):
                own[0] += 1
                ins.then_inc(S("act_chain"), 1)
                act.wait_ge(S("act_chain"), own[0])

            def store(dst, src, sem):
                act.dma_start(dst, src).then_inc(S(sem), 16)

            def squares(i, rows, src, dump, sem):
                if i:
                    act.wait_ge(S(sem), i)
                a(dump, src, ACT.Square, accum_out=small[0:rows, A_SSQ + i:A_SSQ + i + 1]).then_inc(S(sem), 1)

            full(act, "par")
            free(a(par[:, 0:NPAR], bank[4][:, 0:NPAR], ACT.Copy), "par")
            for i in range(NT + 2):
                if i < NT:
                    act.wait_ge(S(f"x{i}_in"), 16)
                    squares(i, ROWS[i], x_in(i).rearrange("p (a b) -> p a b", a=2), mixT[0:ROWS[i], 0:2, 0:512], "norm1_sq")
                if i >= 2:
                    j = i - 2
                    act.wait_ge(S("norm1_rms"), j + 1)
                    a(x_in(j), x_in(j), ACT.Copy, scale=small[0:ROWS[j], A_RS + j:A_RS + j + 1]).then_inc(S("x_normed"), 1)
            act.wait_ge(S("ssd_params_in"), 48)
            a(small[:, A_NA:A_NA + HC], small[:, A_AL:A_AL + HC], ACT.Exp).then_inc(S("a_exp"), 1)
            full(act, "s0T")
            free(a(hst[:, 1, :, :], bank[4][:, 0:2 * PC].rearrange("p (j c) -> p j c", j=2), ACT.Copy), "s0T")
            for n, half in enumerate(HALVES):
                full(act, ("bq", n))
                free(a(qB[:, half], bank[n][:, 0:HALF], ACT.Copy, scale=DK ** -0.5), ("bq", n))
            act.wait_ge(S("zeroed"), 1)
            for i in range(NT):
                r = ROWS[i]
                o = full(act, ("bv", i))
                a(dtw[0:r, 0, i * HC:(i + 1) * HC], o[0:r, HB * DV:HB * DV + HC], ACT.Copy)
                free(a(bv[0:r, i, :], o[0:r, 0:HB * DV], ACT.Copy), ("bv", i))
            for n, half in enumerate(HALVES):
                full(act, ("lr", n))
                free(a(lrT[:, half], bank[2 + n][0:RANK, 0:HALF], ACT.Copy), ("lr", n))
            act.wait_ge(S("dt_u"), 1)
            link(a(dtw[:, 1, :], dtw[:, 0, :], ACT.Abs))
            a(dtw[:, 2, :], dtw[:, 1, :], ACT.Exp, scale=-1.0).then_inc(S("dt_e"), 1)
            act.wait_ge(S("dt_w"), 1)
            a(dtw[:, 4, :], dtw[:, 3, :], ACT.Ln).then_inc(S("dt_ln"), 1)
            for i in range(NT):
                r = ROWS[i]
                full(act, ("ogz", i))
                free(a(ogz[0:r, i, :], bank[i % 2][0:r, :], ACT.Copy, scale=0.5), ("ogz", i))
                drained(act, ("ogz", i))
                if i >= 2:
                    act.wait_ge(S("gates"), i - 1)
                a(gth[0:r, i % 2, :], ogz[0:r, i, :], ACT.Tanh).then_inc(S("gates_tanh"), 1)
            drained(act, ("gate", 0))
            drained(act, ("gate", 1))
            link(a(gtmp[:, 1, :], gtmp[:, 0, :], ACT.Abs))
            link(a(gtmp[:, 1, :], gtmp[:, 1, :], ACT.Exp, scale=-1.0))
            a(gtmp[:, 1, :], gtmp[:, 1, :], ACT.Ln, bias=1.0).then_inc(S("gate_log"), 1)
            drained(act, "par")
            a(xpre[:, :, SEQ + 3:SEQ + 6], par[:, GCS:GCS + 12].rearrange("p (t j) -> p j t", j=4),
              ACT.Copy).then_inc(S("conv_state_placed"), 1)
            moved = [0]

            def move(key):
                nm, n = key
                full(act, key)
                o = bank[fills[key][0]]
                if key == ("q", 0):
                    act.wait_ge(S("rev_out"), 16)
                if nm in ("q", "k"):
                    dst, sc = (qT, DH ** -0.5) if nm == "q" else (kT, 1.0)
                    free(a(dst[:, n // 2, HALVES[n % 2]], o[:, 0:HALF], ACT.Copy, scale=sc), key)
                    return
                r = ROWS[n]
                at = slice(T0[n], T0[n] + r)
                if nm == "v":
                    dst = o_pv[0, 0, at] if n < NT - 1 else o_sv[0, 0]
                    src, sem = V[0:r, n, :], "v_out"
                else:
                    dst = o_pk[0, 0, at] if n < NT - 1 else o_sk[0, 0]
                    src, sem = stage[0:r, n % 2, WA:2 * WA], f"k_out{n % 2}"
                    if n >= 2:
                        act.wait_ge(S(sem), 16 * (n // 2))
                free(a(src, o[0:r, :], ACT.Copy), key)
                drained(act, key)
                store(dst.rearrange("t h d -> t (h d)"), src, sem)

            began = {key: n for n, key in enumerate(fills)}

            def catch_up(key):
                while moved[0] < len(behind) and behind[moved[0]][1] <= began[key]:
                    move(behind[moved[0]][0])
                    moved[0] += 1

            def full_mix(key):
                catch_up(key)
                full(act, key)

            def tanh(j):
                act.wait_ge(S("conv_sum"), j + 1)
                if j:
                    act.wait_ge(S("conv_out"), j)
                a(thx[:, 0:TOK + 3], ctmp[:, j % 2, 0:TOK + 3], ACT.Tanh).then_inc(S("conv_tanh"), 1)

            for j in range(4):
                full(act, ("xbc", j, 0))
                free(a(xpre[:, j, 3:HALF + 3], bank[0][:, 0:HALF], ACT.Copy), ("xbc", j, 0))
                full(act, ("xbc", j, 1))
                a(xpre[:, j, HALF + 3:SEQ + 3], bank[1][:, 0:SEQ - HALF], ACT.Copy)
                free(a(xpre[:, j, SEQ + 6:TOK + 6], bank[1][:, SEQ - HALF:HALF], ACT.Copy), ("xbc", j, 1))
                if j:
                    tanh(j - 1)
            for s, dst in ((0, o_pc), (1, o_sc)):
                full_mix(("cst", s))
                free(a(cso[0:3, s, :], bank[3][0:3, :], ACT.Copy), ("cst", s))
                drained(act, ("cst", s))
                store(dst[0, 0], cso[0:3, s, :], "states_out")
            tanh(3)

            for i in range(NT):
                r = ROWS[i]
                t0, t1 = T0[i], T0[i] + r
                if i == 0:
                    drained(act, ("bq", 0))
                    drained(act, ("bq", 1))
                else:
                    filled(act, ("lev", i - 1, len(levels(i - 1)) - 1))
                for h in range(HB):
                    last = a(qbd[h * DK:(h + 1) * DK, h, 0:r], qB[h * DK:(h + 1) * DK, t0:t1], ACT.Copy)
                last.then_inc(S("q_blocks"), 1)
                act.wait_ge(S("gla_b"), i + 1)
                a(qs[:, 0:r], bcum[:, t0:t1], ACT.Exp).then_inc(S("gla_exps"), 1)
                a(kd[:, 0:r], bcum[:, t0:t1], ACT.Exp, scale=-1.0, bias=bcum[:, t1 - 1:t1]).then_inc(S("gla_exps"), 1)
                a(small[:, A_EBL:A_EBL + 1], bcum[:, t1 - 1:t1], ACT.Exp).then_inc(S("gla_exps"), 1)
                for n, m in enumerate(levels(i)[:-1]):
                    c = n_lev[i] - i + n
                    if n >= 2:
                        catch_up(("lev", i, n - 2))
                    act.wait_ge(S("dif"), c + 1)
                    a(dif[:, c % 2, 0:r], dif[:, c % 2, 0:r], ACT.Exp).then_inc(S("E"), 1)
                full_mix(("xn", i))
                free(a(xnat[0:r, :], bank[2][0:r, 0:3 * P], ACT.Copy), ("xn", i))
                act.wait_ge(S("cs_last"), i + 1)
                a(small[0:r, A_W:A_W + HC], small[0:r, A_W:A_W + HC], ACT.Exp)
                a(small[:, A_ECL:A_ECL + HC], small[:, A_CSL:A_CSL + HC], ACT.Exp)
                a(small[0:r, A_ECS:A_ECS + HC], small[0:r, A_CS + i * HC:A_CS + (i + 1) * HC],
                  ACT.Exp).then_inc(S("ssd_exps"), 1)
                drained(act, ("csrow", i))
                a(dec[0:r, :, 0:r], dec[0:r, :, 0:r], ACT.Exp).then_inc(S("decay"), 1)
                full_mix(("kdT", i))
                free(a(kdn[0:r, :], bank[1][0:r, 0:P], ACT.Copy), ("kdT", i))
                full_mix(("go", i))
                free(a(gv[0:r, :], bank[7][0:r, 0:HB * DV], ACT.Copy), ("go", i))
                for key, b, c, kt in ((("goT", i), 7, (GGN, GGN), WA // P), (("syT", i), 2, (GSN, GSN + 1), WA // P + 2)):
                    full_mix(key)
                    a(mixT[:, kt, t0:t1], bank[b][:, 0:r], ACT.Copy, scale=par[:, c[0]:c[0] + 1])
                    free(a(mixT[:, kt + 1, t0:t1], bank[b][:, r:2 * r], ACT.Copy, scale=par[:, c[1]:c[1] + 1]), key)
                if i >= NT - 2:
                    s = seq(i)
                    drained(act, ("gkv", i))
                    for h in range(HB):
                        store((o_pg, o_sg)[s][0, 0, h], Sg[h * DK:(h + 1) * DK, s, h, :], "states_out")
            for s in range(2):
                full_mix(("stT", s))
                free(a(sto[:, s, :], bank[2][0:PC, 0:2 * P], ACT.Copy), ("stT", s))
                drained(act, ("stT", s))
                o = (o_ps, o_ss)[s][0, 0].rearrange("(g j) p n -> j p g n", j=2)
                for j in range(2):
                    store(o[j], sto[:, s, j * P:(j + 1) * P].rearrange("p (g n) -> p g n", g=2), "states_out")
            filled(act, ("stT", 1))
            act.dma_start(cv[:, :, :], cache_v[0, 0].rearrange("(c p) h d -> p c (h d)", p=P)).then_inc(S("cached_v_in"), 16)
            for c in range(PAST // P):
                full_mix(("ckT", c))
                free(a(ckT[:, :, c * P:(c + 1) * P], bank[(0, 6)[c]][:, :].rearrange("p (j t) -> p j t", j=4), ACT.Copy),
                     ("ckT", c))
            for n in range(HEADS):
                if n < NA:
                    i, h = divmod(n, HA)
                    r, nk = ROWS[i], nkeys(i)
                    act.wait_ge(S("negmax"), n + 1)
                    if n >= 2:
                        filled(act, ("PT", n - 2))
                    c = A_SUM + (i % 2) * HA + h
                    free(a(Pm[0:r, n % 2, 0:nk], bank[4 + h % 2][0:r, 0:nk], ACT.Exp,
                           bias=small[0:r, A_NM + n % 4:A_NM + n % 4 + 1], accum_out=small[0:r, c:c + 1]), ("S", n))
                if 1 <= n <= NA:
                    m = n - 1
                    i, h = divmod(m, HA)
                    r, nk = ROWS[i], nkeys(i)
                    full(act, ("PT", m))
                    if m >= 2:
                        act.wait_ge(S("pv"), m - 1)
                    src, nb, rest = bank[6 + m % 2], nk // P, nk % P
                    if rest:
                        a(PT[0:rest, m % 2, nb * r:(nb + 1) * r], src[0:rest, nb * r:(nb + 1) * r], ACT.Copy)
                    free(a(PT[:, m % 2, 0:nb * r], src[:, 0:nb * r], ACT.Copy), ("PT", m))
                for i, step in steps_behind(n):
                    r = ROWS[i]
                    if step == 10:
                        drained(act, ("wo", i, 0))
                        drained(act, ("wo", i, 1))
                        squares(i, r, x1[0:r, i, :], dump[0:r, :], "norm2_sq")
                    if step == 12:
                        act.wait_ge(S("h2"), i + 1)
                        store(h2_d[T0[i]:T0[i] + r, :], h2[0:r, i % 2, :], f"h2_out{i % 2}")
                    if step == 13:
                        full(act, ("h2T", i, 0))
                        if i >= 2:
                            filled(act, ("lg", i - 2))
                        free(a(h2T[:, i % 2, 0:4, 0:r], bank[2][:, 0:4 * r].rearrange("p (k t) -> p k t", k=4), ACT.Copy),
                             ("h2T", i, 0))
            act.wait_ge(S("router_sub"), 1)
            a(rt[:, R_SUB, :, 0:4], rt[:, R_SUB, :, 0:4], ACT.Exp).then_inc(S("router_exp"), 1)
            act.wait_ge(S("router_sub"), 2)
            a(rt[:, R_V, :, 0:1], rt[:, R_V, :, 0:1], ACT.Exp).then_inc(S("router_exp"), 1)
            for e in range(-1, NE + 1):
                if 0 <= e < NE:
                    full(act, ("gu", e))
                    if e >= 2:
                        drained(act, ("gu", e - 2))
                    a(sg[:, e % 2, :], bank[2 + e % 2][:, 0:FE], ACT.Silu).then_inc(S("silu"), 1)
                if e >= 1:
                    d = e - 1
                    full(act, ("hT", d))
                    free(a(hidT[:, d % 2, :, :],
                           bank[4 + d % 2][:, 0:FE // P * CAP].rearrange("p (j c) -> p j c", j=FE // P), ACT.Copy),
                         ("hT", d))
                if e + 1 < NE:
                    full(act, ("xgT", e + 1, 0))
                    free(a(xgT[:, (e + 1) % 2, 0:4, :], bank[0][:, :].rearrange("p (k c) -> p k c", k=4), ACT.Copy),
                         ("xgT", e + 1, 0))
                if e >= 1:
                    if d >= 2:
                        act.wait_ge(S(f"y_out{d % 2}"), 16 * (d // 2))
                    full(act, ("ye", d, 0))
                    free(a(ye[:, d % 2, 0:512], bank[6][:, :], ACT.Copy), ("ye", d, 0))
                    drained(act, ("ye", d, 0))
                    drained(act, ("ye", d, 1))
                    store(y_d[d * CAP:(d + 1) * CAP, :], ye[:, d % 2, :], f"y_out{d % 2}")
            act.wait_ge(S("max_count"), 1)
            fullest = act.value_load(ri[0:1, 60:61], min_val=0, max_val=TOK)
            act.wait_ge(S("y_out0"), 16 * (NE // 2))
            act.wait_ge(S("y_out1"), 16 * (NE // 2))
            with act.If(fullest > CAP):
                with act.Fori(0, MORE) as t:
                    act.wait_ge(S("more_turned"), t + 1)
                    a(xgT[:, 0, 0:4, :], bank[0][:, :].rearrange("p (k c) -> p k c", k=4), ACT.Copy)
                    a(xgT[:, 0, 4:8, :], bank[1][:, :].rearrange("p (k c) -> p k c", k=4), ACT.Copy).then_inc(S("more_xT"), 1)
                    act.wait_ge(S("more_up"), t + 1)
                    a(sg[:, 0, :], bank[2][:, 0:FE], ACT.Silu).then_inc(S("more_silu"), 1)
                    act.wait_ge(S("more_hidden_turned"), t + 1)
                    a(hidT[:, 0, :, :], bank[4][:, 0:FE // P * CAP].rearrange("p (j c) -> p j c", j=FE // P),
                      ACT.Copy).then_inc(S("more_hiddenT"), 1)
                    act.wait_ge(S("more_down"), t + 1)
                    a(ye[:, 0, 0:512], bank[6][:, :], ACT.Copy)
                    a(ye[:, 0, 512:1024], bank[7][:, :], ACT.Copy).then_inc(S("more_y"), 1)
                    act.wait_ge(S("more_y"), t + 1)
                    act.dma_start(y_d[bass.ds(t * CAP + SPAN, CAP), :], ye[:, 0, :]).then_inc(S("more_out"), 16)
                    act.wait_ge(S("more_out"), (t + 1) * 16)
            act.nop()
            for i in range(NT + 1):
                if i < NT:
                    r = ROWS[i]
                    act.wait_ge(S("combined"), i + 1)
                    squares(i, r, x1[0:r, i, :].rearrange("p (a b) -> p a b", a=2), mixT[0:r, 0:2, 0:512], "final_sq")
                if i >= 1:
                    n = i - 1
                    r = ROWS[n]
                    act.wait_ge(S("y_normed"), n + 1)
                    dst = y_prompt[0, T0[n]:T0[n] + r, :] if n < NT - 1 else y_sample[0]
                    store(dst, ye[0:r, n % 2, :], f"y_final{n % 2}")
            act.wait_ge(S("states_out"), 16 * (2 + 2 * HB + 4))
            act.wait_ge(S("v_out"), 16 * NT)
            for i in range(2):
                n = (NT + 1 - i) // 2
                act.wait_ge(S(f"k_out{i}"), 16 * n)
                act.wait_ge(S(f"y_final{i}"), 16 * n)

        @block.vector
        def _(dve):
            v = nc.vector
            chain = [0]

            def link(ins):
                chain[0] += 1
                ins.then_inc(S("dve_chain"), 1)
                dve.wait_ge(S("dve_chain"), chain[0])

            def col(c, n=1, rows=P):
                return small[0:rows, c:c + n]

            def mean(ssq, ms, n, rows, over, sem):
                v.tensor_scalar(col(ms, n, rows), col(ssq, n, rows), 1.0 / over, EPS, ALU.mult, ALU.add).then_inc(S(sem), 1)

            for n in range(NT + 2):
                if n < NT:
                    dve.wait_ge(S("norm1_sq"), n + 1)
                    mean(A_SSQ + n, A_MS + n, 1, ROWS[n], D, "norm1_mean")
                if n == 0:
                    drained(dve, "par")
                i = n - 2
                if i >= 0:
                    r = ROWS[i]
                    for hf in range(2):
                        o = full(dve, ("xT", i, hf))
                        free(v.tensor_tensor(hT[:, 4 * hf:4 * hf + 4, T0[i]:T0[i] + r],
                                             o[:, 0:4 * r].rearrange("p (k t) -> p k t", k=4),
                                             par[:, G1 + 4 * hf:G1 + 4 * hf + 4].unsqueeze(2).broadcast_to([P, 4, r]),
                                             ALU.mult), ("xT", i, hf))
            dve.wait_ge(S("iotas"), 1)
            dve.wait_ge(S("consts"), 1)
            link(v.tensor_tensor(iot[:, 0, :], iot[:, 0, :], iot[:, 1, :], ALU.bitwise_xor))
            link(v.tensor_copy(lvf[:, 0, :], iot[:, 0, :]))
            link(v.tensor_tensor(lvf[:, 0, :], lvf[:, 0, :], striu[:, :], ALU.mult))
            for n, m in enumerate(LEV):
                link(v.tensor_scalar(lvf[:, 1 + n % 2, :], lvf[:, 0, :], float(m), None, ALU.is_ge))
                if n:
                    link(v.tensor_tensor(lmask[:, n, :], lvf[:, 1 + n % 2, :], lvf[:, 2 - n % 2, :], ALU.subtract))
                else:
                    link(v.tensor_copy(lmask[:, n, :], lvf[:, 1, :]))
            link(v.tensor_copy(lmask[:, 7, :], ident[:, :]))
            dve.wait_ge(S("table_in"), 16)
            link(v.tensor_copy(xrel[:, 0:2 * CLIP], rtab[:, 1:2 * CLIP + 1]))
            link(v.tensor_copy(xrel[:, 2 * CLIP:383], rtab[:, 2 * CLIP:2 * CLIP + 1].broadcast_to([HA, 127])))
            v.tensor_scalar(xrel[:, 0:383], xrel[:, 0:383], rtab[:, 2 * CLIP:2 * CLIP + 1], None,
                            ALU.subtract).then_inc(S("rev_ready"), 1)
            dve.wait_ge(S("a_exp"), 1)
            link(v.tensor_scalar(col(A_NA, HC), col(A_NA, HC), -1.0, None, ALU.mult))
            link(v.tensor_scalar(par[:, GCW:GCW + 20], par[:, GCW:GCW + 20], 0.5, None, ALU.mult))
            for n, half in enumerate(HALVES):
                o = full(dve, ("bk", n))
                free(v.tensor_copy(kB[:, half], o[:, 0:HALF]), ("bk", n))
            drained(dve, ("bv", NT - 2))
            drained(dve, ("bv", NT - 1))
            dt_u = dtw[:, 0, :].rearrange("p (i h) -> p i h", i=NT)
            link(v.tensor_tensor(dt_u, dt_u, col(A_DTB, HC).unsqueeze(1).broadcast_to([P, NT, HC]), ALU.add))
            v.tensor_scalar(dtw[:, 8, :], dtw[:, 0, :], 0.0, None, ALU.max).then_inc(S("dt_u"), 1)
            dve.wait_ge(S("dt_e"), 1)
            v.tensor_scalar(dtw[:, 3, :], dtw[:, 2, :], 1.0, None, ALU.add).then_inc(S("dt_w"), 1)
            dve.wait_ge(S("dt_w"), 1)
            link(v.tensor_scalar(dtw[:, 5, :], dtw[:, 3, :], -1.0, None, ALU.add))
            link(v.tensor_scalar(dtw[:, 6, :], dtw[:, 5, :], 0.0, None, ALU.is_equal))
            link(v.tensor_tensor(dtw[:, 5, :], dtw[:, 5, :], dtw[:, 6, :], ALU.add))
            link(v.reciprocal(dtw[:, 7, :], dtw[:, 5, :]))
            link(v.tensor_tensor(dtw[:, 7, :], dtw[:, 7, :], dtw[:, 2, :], ALU.mult))
            link(v.tensor_tensor(dtw[:, 6, :], dtw[:, 6, :], dtw[:, 2, :], ALU.mult))
            dve.wait_ge(S("dt_ln"), 1)
            link(v.tensor_tensor(dtw[:, 7, :], dtw[:, 7, :], dtw[:, 4, :], ALU.mult))
            link(v.tensor_tensor(dtw[:, 7, :], dtw[:, 7, :], dtw[:, 6, :], ALU.add))
            link(v.tensor_tensor(col(A_DT, NT * HC), dtw[:, 7, :], dtw[:, 8, :], ALU.add))
            v.tensor_tensor(col(A_A, NT * HC).rearrange("p (i h) -> p i h", i=NT),
                            col(A_DT, NT * HC).rearrange("p (i h) -> p i h", i=NT),
                            col(A_NA, HC).unsqueeze(1).broadcast_to([P, NT, HC]), ALU.mult).then_inc(S("a_ready"), 1)
            for i in range(NT):
                r = ROWS[i]
                dve.wait_ge(S("gates_tanh"), i + 1)
                v.scalar_tensor_tensor(out=ogz[0:r, i, :], in0=gth[0:r, i % 2, :], scalar=1.0, in1=ogz[0:r, i, :],
                                       op0=ALU.add, op1=ALU.mult).then_inc(S("gates"), 1)
            for n, half in enumerate(HALVES):
                o = full(dve, ("gate", n))
                free(v.tensor_scalar(gtmp[:, 0, half], o[:, 0:HALF], par[:, GBG:GBG + 1], None, ALU.add), ("gate", n))
            dve.wait_ge(S("gate_log"), 1)
            link(v.scalar_tensor_tensor(out=gtmp[:, 0, :], in0=gtmp[:, 0, :], scalar=0.0, in1=gtmp[:, 1, :],
                                        op0=ALU.min, op1=ALU.subtract))
            link(v.tensor_scalar(gtmp[:, 0, :], gtmp[:, 0, :], 1.0 / 16.0, None, ALU.mult))
            for i in range(NT):
                r = ROWS[i]
                v.tensor_tensor_scan(bcum[:, T0[i]:T0[i] + r], ones[:, 0:r], gtmp[:, 0, T0[i]:T0[i] + r], 0.0,
                                     ALU.mult, ALU.add).then_inc(S("gla_b"), 1)
            nb = NT - 1
            dve.wait_ge(S("conv_state_placed"), 1)
            L = TOK + 3

            def conv_silu(j):
                dve.wait_ge(S("conv_tanh"), j + 1)
                v.scalar_tensor_tensor(out=xc[:, j, 0:L], in0=thx[:, 0:L], scalar=1.0, in1=ctmp[:, j % 2, 0:L],
                                       op0=ALU.add, op1=ALU.mult).then_inc(S("conv_out"), 1)

            for j in range(4):
                acc = ctmp[:, j % 2, 0:L]

                def tap(t):
                    return par[:, GCW + 4 * t + j:GCW + 4 * t + j + 1]

                drained(dve, ("xbc", j, 0))
                drained(dve, ("xbc", j, 1))
                if j >= 2:
                    dve.wait_ge(S("conv_out"), j - 1)
                link(v.tensor_scalar(acc, xpre[:, j, 0:L], tap(0), par[:, GCB + j:GCB + j + 1], ALU.mult, ALU.add))
                for t in range(1, TAPS):
                    ins = v.scalar_tensor_tensor(out=acc, in0=xpre[:, j, t:t + L], scalar=tap(t), in1=acc,
                                                 op0=ALU.mult, op1=ALU.add)
                    if t < TAPS - 1:
                        link(ins)
                ins.then_inc(S("conv_sum"), 1)
                if j:
                    conv_silu(j - 1)
            conv_silu(3)
            o = full(dve, "cs")
            v.tensor_copy(col(A_CS, nb * HC), o[:, 0:nb * HC])
            free(v.tensor_copy(col(A_CS + nb * HC, HC, DEC), o[0:DEC, nb * HC:NT * HC]), "cs")
            drained(dve, "cs")

            for i in range(NT):
                r = ROWS[i]
                t0 = T0[i]
                base_c = n_lev[i] - i
                lev = levels(i)
                first = LEV.index(lev[0])
                dve.wait_ge(S("gla_exps"), 3 * (i + 1))
                drained(dve, ("bq", 0))
                drained(dve, ("bq", 1))
                v.tensor_tensor(qs[:, 0:r], qs[:, 0:r], qB[:, t0:t0 + r], ALU.mult).then_inc(S("q_from_start"), 1)
                v.tensor_tensor(kd[:, 0:r], kd[:, 0:r], kB[:, t0:t0 + r], ALU.mult).then_inc(S("k_to_end"), 1)

                def exponents(n):
                    m, c = lev[n], base_c + n
                    if c >= 2:
                        dve.wait_ge(S("q_decayed"), c - 1)
                        dve.wait_ge(S("k_decayed"), c - 1)
                    b = bcum[:, t0:t0 + r].rearrange("p (n two m) -> p n two m", two=2, m=m)
                    d = dif[:, c % 2, 0:r].rearrange("p (n two m) -> p n two m", two=2, m=m)
                    ref = b[:, :, 0, m - 1:m].broadcast_to([P, r // (2 * m), m])
                    v.tensor_tensor(d[:, :, 1, :], b[:, :, 1, :], ref, ALU.subtract)
                    v.tensor_tensor(d[:, :, 0, :], ref, b[:, :, 0, :], ALU.subtract).then_inc(S("dif"), 1)

                def decay_k(n):
                    c = base_c + n
                    dve.wait_ge(S("E"), c + 1)
                    if c >= 2:
                        filled(dve, lev_key[c - 2])
                    v.tensor_tensor(kE[:, c % 2, 0:r], kB[:, t0:t0 + r], dif[:, c % 2, 0:r],
                                    ALU.mult).then_inc(S("k_decayed"), 1)

                def select(n):
                    o = full(dve, ("lev", i, n))
                    if n:
                        drained(dve, ("lev", i, n - 1))
                    which = 7 if lev[n] == 0 else first + n
                    free(v.copy_predicated(att[0:r, :, 0:r],
                                           lmask[0:r, which, 0:r].unsqueeze(1).broadcast_to([r, HB, r]),
                                           o[0:r, 0:HB * r].rearrange("p (h t) -> p h t", h=HB)), ("lev", i, n))

                for n in range(len(lev) + 1):
                    if n < len(lev) - 1:
                        exponents(n)
                    if 1 <= n < len(lev):
                        decay_k(n - 1)
                    if n >= 2:
                        select(n - 2)
                select(len(lev) - 1)
                o = full(dve, ("csrow", i))
                link(v.tensor_copy(col(A_CSL, HC), o[:, :].rearrange("p (h t) -> p h t", h=HC)[:, :, r - 1]))
                v.tensor_tensor(col(A_W, HC, r), col(A_CSL, HC, r), col(A_CS + i * HC, HC, r),
                                ALU.subtract).then_inc(S("cs_last"), 1)
                for h in range(HC):
                    ins = v.tensor_scalar(dec[0:r, h, 0:r], o[0:r, h * P:h * P + r], col(A_CS + i * HC + h, 1, r), 0.0,
                                          ALU.subtract, ALU.min)
                free(ins, ("csrow", i))
                if i:
                    dve.wait_ge(S("ssd_scores"), i)
                for g in range(2):
                    o = full(dve, ("cby", i, g))
                    v.tensor_tensor(cbm[0:r, g, 0:r], o[0:r, 0:r], triu[0:r, 0:r], ALU.mult).then_inc(S("ssd_cb"), 1)
                dve.wait_ge(S("ssd_exps"), i + 1)
                v.tensor_tensor(col(A_W, HC, r), col(A_W, HC, r), col(A_DT + i * HC, HC, r), ALU.mult).then_inc(S("ssd_w"), 1)
                dve.wait_ge(S("decay"), i + 1)
                dve.wait_ge(S("ssd_cb"), 2 * (i + 1))
                for g in range(2):
                    ins = v.tensor_tensor(dec[0:r, 2 * g:2 * g + 2, 0:r], dec[0:r, 2 * g:2 * g + 2, 0:r],
                                          cbm[0:r, g, 0:r].unsqueeze(1).broadcast_to([r, 2, r]), ALU.mult)
                ins.then_inc(S("ssd_scores"), 1)
                for g in range(2):
                    o = bank[fills["cby", i, g][0]]
                    free(v.tensor_tensor(yt[0:r, g * 2 * PC:(g + 1) * 2 * PC].rearrange("p (j c) -> p j c", j=2),
                                         o[0:r, P:2 * P].rearrange("p (j c) -> p j c", j=2),
                                         col(A_ECS + 2 * g, 2, r).unsqueeze(2).broadcast_to([r, 2, PC]), ALU.mult),
                         ("cby", i, g))
                o = full(dve, ("st", i))
                for h in range(HC):
                    g, j = divmod(h, 2)
                    new, old = hst[g * NS:(g + 1) * NS, seq(i), j, :], hst[g * NS:(g + 1) * NS, seq(i), j, :]
                    ins = v.scalar_tensor_tensor(out=new, in0=old, scalar=small[g * NS:(g + 1) * NS, A_ECL + h:A_ECL + h + 1],
                                                 in1=o[g * NS:(g + 1) * NS, h * PC:(h + 1) * PC], op0=ALU.mult, op1=ALU.add)
                free(ins, ("st", i))
                drained(dve, ("st", i))
                drained(dve, ("cby", i, 1))
                dve.wait_ge(S("x_skip"), i + 1)
                v.tensor_tensor(yt[0:r, :], yt[0:r, :], xD[0:r, :, :].rearrange("p h c -> p (h c)"),
                                ALU.add).then_inc(S("ssd_sum"), 1)
                o = full(dve, ("ya", i))
                dve.wait_ge(S("ssd_sum"), i + 1)
                free(v.tensor_tensor(yv[0:r, :], o[0:r, 0:HC * PC], yt[0:r, :], ALU.add), ("ya", i))
                drained(dve, ("ya", i))
                link(v.tensor_tensor(yv[0:r, :], yv[0:r, :], ogz[0:r, i, HB * DV:], ALU.mult))
                link(v.tensor_tensor(yt[0:r, :], yv[0:r, :], yv[0:r, :], ALU.mult))
                link(v.tensor_reduce(col(A_YS, 2, r), yt[0:r, :].rearrange("p (g c) -> p g c", g=2), AX.X, ALU.add))
                mean(A_YS, A_YS, 2, r, HC * PC // 2, "ssd_mean")
                drained(dve, ("go", i))
                link(v.tensor_tensor(gt[0:r, :], gv[0:r, :], gv[0:r, :], ALU.mult))
                link(v.tensor_reduce(col(A_GS, HB, r), gt[0:r, :].rearrange("p (h c) -> p h c", h=HB), AX.X, ALU.add))
                mean(A_GS, A_GS, HB, r, DV, "gla_mean")
                o = full(dve, ("gkv", i))
                for h in range(HB):
                    p0, p1 = h * DK, (h + 1) * DK
                    ins = v.scalar_tensor_tensor(out=Sg[p0:p1, seq(i), h, :], in0=Sg[p0:p1, seq(i), h, :],
                                                 scalar=small[p0:p1, A_EBL:A_EBL + 1], in1=o[p0:p1, h * DV:(h + 1) * DV],
                                                 op0=ALU.mult, op1=ALU.add)
                free(ins, ("gkv", i))
                dve.wait_ge(S("gla_rms"), i + 1)
                link(v.tensor_tensor(gv[0:r, :].rearrange("p (h c) -> p h c", h=HB),
                                     gv[0:r, :].rearrange("p (h c) -> p h c", h=HB),
                                     col(A_GR, HB, r).unsqueeze(2).broadcast_to([r, HB, DV]), ALU.mult))
                v.tensor_tensor(gv[0:r, :], gv[0:r, :], ogz[0:r, i, 0:HB * DV], ALU.mult).then_inc(S("gla_gated"), 1)
                dve.wait_ge(S("ssd_rms"), i + 1)
                v.tensor_tensor(yv[0:r, :].rearrange("p (g c) -> p g c", g=2),
                                yv[0:r, :].rearrange("p (g c) -> p g c", g=2),
                                col(A_YR, 2, r).unsqueeze(2).broadcast_to([r, 2, HC * PC // 2]),
                                ALU.mult).then_inc(S("ssd_gated"), 1)

            dve.wait_ge(S("bias_in"), 16)
            link(v.memset(bias[0:P // 2, :, 0:P // 2], NEG))

            def att_norm(i):
                r = ROWS[i]
                if i == 0:
                    dve.wait_ge(S("states_out"), 16 * (2 + 2 * HB + 4))
                dve.wait_ge(S("pv"), HA * (i + 1))
                c = A_SUM + (i % 2) * HA
                link(v.reciprocal(col(A_RSUM + (i % 2) * HA, HA, r), col(c, HA, r)))
                o = bank[i % 2]
                free(v.tensor_tensor(attn[0:r, i % 2, :].rearrange("p (h d) -> p h d", h=HA),
                                     o[0:r, :].rearrange("p (h d) -> p h d", h=HA),
                                     col(A_RSUM + (i % 2) * HA, HA, r).unsqueeze(2).broadcast_to([r, HA, DH]), ALU.mult),
                     ("ao", i))

            def att_out(i):
                r = ROWS[i]
                o = full(dve, ("aoT", i))
                free(v.tensor_copy(mixT[:, 0:4, T0[i]:T0[i] + r], o[:, 0:4 * r].rearrange("p (k t) -> p k t", k=4)),
                     ("aoT", i))

            dve.wait_ge(S("zeroed"), 1)
            v.tensor_copy(ones_b[:, :], ones[:, :])
            v.tensor_copy(before_b[:, :], striu[:, :])
            v.tensor_copy(slot_f[:, :], slot_i[:, :])
            v.tensor_copy(tokid[:, :, 0], ri[:, 32:33].broadcast_to([P, NT]))
            for i in range(NT):
                v.memset(tokid[:, i, 1:2], float(i))
            v.tensor_copy(desc[:, :], ri[:, 40:44])
            v.tensor_copy(ebase[:, :], ri[:, 48:48 + NE])
            link(v.memset(lgt[:, :, :], 0.0))

            def residual(i, hf):
                if i == 0 and hf == 0:
                    dve.wait_ge(S("x1_in_residual"), 16 * NT)
                    dve.wait_ge(S("norm_rows_in"), 32)
                    dve.wait_ge(S("router_b_in"), 32)
                r = ROWS[i]
                o = full(dve, ("wo", i, hf))
                x = x1[0:r, i, hf * 512:(hf + 1) * 512]
                free(v.tensor_tensor(x, x, o[0:r, :], ALU.add), ("wo", i, hf))

            def norm2(i):
                r = ROWS[i]
                dve.wait_ge(S("norm2_sq"), i + 1)
                mean(A_SSQ + i, A_MS + i, 1, r, D, "norm2_mean")
                dve.wait_ge(S("norm2_rms"), i + 1)
                if i >= 2:
                    dve.wait_ge(S(f"h2_out{i % 2}"), 16 * (i // 2))
                v.scalar_tensor_tensor(out=h2[0:r, i % 2, :], in0=x1[0:r, i, :], scalar=col(A_RS + i, 1, r),
                                       in1=w2b[0:r, :], op0=ALU.mult, op1=ALU.mult).then_inc(S("h2"), 1)

            for n in range(HEADS):
                if n < NA:
                    i, h = divmod(n, HA)
                    r, nk = ROWS[i], nkeys(i)
                    o = full(dve, ("S", n))
                    if i == NT - 1:
                        link(v.tensor_tensor(o[0:r, P:nk], o[0:r, P:nk], bias[0:r, h, 2 * P - 1:P // 2 - 1:-1], ALU.add))
                    else:
                        w = min(nk, 2 * P)
                        link(v.tensor_tensor(o[0:r, nk - w:nk], o[0:r, nk - w:nk], bias[:, h, w - 1::-1], ALU.add))
                    v.tensor_reduce(col(A_NM + n % 4, 1, r), o[0:r, 0:nk], AX.X, ALU.max, negate=True).then_inc(S("negmax"), 1)
                for i, step in steps_behind(n):
                    r = ROWS[i]
                    if step == 0:
                        att_norm(i)
                        att_out(i)
                    if step in WO_ADD:
                        residual(i, WO_ADD[step])
                    if step == 11:
                        norm2(i)
                    if step == 15:
                        o = full(dve, ("h2T", i, 1))
                        free(v.tensor_copy(h2T[:, i % 2, 4:8, 0:r], o[:, 0:4 * r].rearrange("p (k t) -> p k t", k=4)),
                             ("h2T", i, 1))
                    if step == 17:
                        o = full(dve, ("lg", i))
                        free(v.tensor_tensor(lgt[0:r, i, :], o[0:r, 0:NG + NE], rb[0:r, :], ALU.add), ("lg", i))
            drained(dve, ("lg", NT - 1))

            def R(k, n=4):
                return rt[:, k, :, 0:n]

            def over(x, n):
                return x.broadcast_to([P, NT, n])


            def first_max(x, m, one_hot):
                link(v.tensor_reduce(m, x, AX.X, ALU.max))
                link(v.tensor_tensor(R(R_EQ), x, over(m, 4), ALU.is_equal))
                link(v.tensor_tensor(R(R_EQ), R(R_EQ), desc[:, :].unsqueeze(1).broadcast_to([P, NT, 4]), ALU.mult))
                link(v.tensor_reduce(rt[:, R_X, :, 0:1], R(R_EQ), AX.X, ALU.max))
                link(v.tensor_tensor(one_hot, R(R_EQ), over(rt[:, R_X, :, 0:1], 4), ALU.is_equal))

            G = lgt[:, :, 0:NG]
            VMG, VS, VP, VM1, VM2 = (rt[:, R_X, :, c:c + 1] for c in (1, 2, 3, 4, 5))
            VE, VD, VW1, VW2 = (rt[:, R_V, :, c:c + 1] for c in (0, 1, 2, 3))
            first_max(G, VMG, R(R_OHG))
            v.tensor_tensor(R(R_SUB), G, over(VMG, 4), ALU.subtract).then_inc(S("router_sub"), 1)
            link(v.tensor_tensor(rt[:, R_TMP, :, :].rearrange("p i (g j) -> p i g j", g=NG),
                                 lgt[:, :, NG:].rearrange("p i (g j) -> p i g j", g=NG),
                                 R(R_OHG).unsqueeze(3).broadcast_to([P, NT, NG, EG]), ALU.mult))
            link(v.tensor_reduce(R(R_SEL), rt[:, R_TMP, :, :].rearrange("p i (g j) -> p i j g", g=NG), AX.X, ALU.add))
            first_max(R(R_SEL), VM1, R(R_K1))
            link(v.scalar_tensor_tensor(out=R(R_L2), in0=R(R_K1), scalar=NEG, in1=R(R_SEL), op0=ALU.mult, op1=ALU.add))
            first_max(R(R_L2), VM2, R(R_K2))
            dve.wait_ge(S("router_exp"), 1)
            v.tensor_tensor(VE, VM2, VM1, ALU.subtract).then_inc(S("router_sub"), 1)
            for k, a_ in ((R_K1, R_A1), (R_K2, R_A2)):
                ins = v.tensor_tensor(rt[:, a_, :, :].rearrange("p i (g j) -> p i g j", g=NG),
                                      R(R_OHG).unsqueeze(3).broadcast_to([P, NT, NG, EG]),
                                      R(k).unsqueeze(2).broadcast_to([P, NT, NG, EG]), ALU.mult)
            link(ins)
            v.tensor_tensor(picked[:, :, :], R(R_A1, NE), R(R_A2, NE), ALU.add).then_inc(S("picks"), 1)
            dve.wait_ge(S("picks"), 1)
            o = full(dve, "pos")
            link(v.memset(rt[:, R_POS, NT - 1, :], 0.0))
            v.tensor_copy(R(R_POS, NE)[:, 0:nb, :], o[:, 0:nb * NE].rearrange("p (i e) -> p i e", i=nb))
            free(v.tensor_copy(rt[0:DEC, R_POS, NT - 1, :], o[0:DEC, nb * NE:NT * NE]), "pos")
            drained(dve, "pos")
            link(v.scalar_tensor_tensor(out=place_e[:, :, :], in0=R(R_POS, NE), scalar=1.0, in1=picked[:, :, :],
                                        op0=ALU.add, op1=ALU.mult))
            link(v.tensor_scalar(place_e[:, :, :], place_e[:, :, :], -1.0, None, ALU.add))

            def mark_slots(e):
                if e >= NE:
                    return
                if e >= 2:
                    filled(dve, ("ids", e - 2))
                v.tensor_tensor(onehot[:, e % 2, :, :], slot_f[:, :].unsqueeze(1).broadcast_to([P, NT, CAP]),
                                place_e[:, :, e:e + 1].broadcast_to([P, NT, CAP]), ALU.is_equal).then_inc(S("slot_one_hot"), 1)

            def slot_tokens(e):
                if e >= NE:
                    return
                o = full(dve, ("ids", e))
                if e >= 2:
                    drained(dve, ("ids", e - 2))
                link(v.tensor_scalar(idp[:, e % 2, :], o[:, 1:2], float(P), None, ALU.mult))
                free(v.tensor_tensor(ri[:, 16 + e:17 + e], idp[:, e % 2, :], o[:, 0:1], ALU.add), ("ids", e))

            for n in range(AHEAD):
                mark_slots(n)
                if n:
                    slot_tokens(n - 1)
            slot_tokens(AHEAD - 1)
            mark_slots(AHEAD)

            link(v.tensor_reduce(VS, R(R_SUB), AX.X, ALU.add))
            dve.wait_ge(S("router_exp"), 2)
            link(v.tensor_scalar(VD, VE, 1.0, None, ALU.add))
            link(v.tensor_tensor(VD, VD, VS, ALU.mult))
            link(v.reciprocal(VW1, VD))
            link(v.tensor_tensor(VW2, VW1, VE, ALU.mult))
            link(v.tensor_tensor(R(R_SLOT, NE), R(R_POS, NE), ebase[:, :].unsqueeze(1).broadcast_to([P, NT, NE]), ALU.add))
            for k, a_ in ((0, R_A1), (1, R_A2)):
                for n, src in ((6, R_POS), (8, R_SLOT)):
                    link(v.tensor_tensor(R(R_TMP, NE), R(a_, NE), R(src, NE), ALU.mult))
                    link(v.tensor_reduce(rt[:, R_X, :, n + k:n + k + 1], R(R_TMP, NE), AX.X, ALU.add))
            place_, slot = rt[:, R_X, :, 6:8], rt[:, R_X, :, 8:10]
            for n in range(1, ROUNDS):
                link(v.tensor_scalar(rt[:, R_X, :, 10:12], place_, float(n * CAP), float(SPAN - CAP), ALU.is_ge, ALU.mult))
                link(v.tensor_tensor(slot, slot, rt[:, R_X, :, 10:12], ALU.add))
            for k in range(2):
                ins = v.tensor_copy(ri[:, k * NT:(k + 1) * NT], rt[:, R_X, :, 8 + k])
            ins.then_inc(S("slots"), 1)
            o = full(dve, "tot")
            free(v.tensor_reduce(col(A_MAX), o[:, 0:NE], AX.X, ALU.max), "tot")
            drained(dve, "tot")
            v.tensor_copy(ri[:, 60:61], col(A_MAX)).then_inc(S("max_count"), 1)

            for e in range(-1, NE + 1):
                if e >= 0:
                    slot_tokens(e + AHEAD)
                    mark_slots(e + AHEAD + 1)
                if 0 <= e < NE:
                    dve.wait_ge(S("silu"), e + 1)
                    if e >= 2:
                        filled(dve, ("hT", e - 2))
                    free(v.tensor_tensor(hid[:, e % 2, :], bank[2 + e % 2][:, FE:2 * FE], sg[:, e % 2, :], ALU.mult),
                         ("gu", e))
                if e + 1 < NE:
                    o = full(dve, ("xgT", e + 1, 1))
                    free(v.tensor_copy(xgT[:, (e + 1) % 2, 4:8, :], o[:, :].rearrange("p (k c) -> p k c", k=4)),
                         ("xgT", e + 1, 1))
                if e >= 1:
                    d = e - 1
                    if d >= 2:
                        dve.wait_ge(S(f"y_out{d % 2}"), 16 * (d // 2))
                    o = full(dve, ("ye", d, 1))
                    free(v.tensor_copy(ye[:, d % 2, 512:1024], o[:, :]), ("ye", d, 1))

            dve.wait_ge(S("max_count"), 1)
            fullest = dve.value_load(ri[0:1, 60:61], min_val=0, max_val=TOK)
            with dve.If(fullest > CAP):
                with dve.Fori(0, MORE) as t:
                    dve.wait_ge(S("more_silu"), t + 1)
                    v.tensor_tensor(hid[:, 0, :], bank[2][:, FE:2 * FE], sg[:, 0, :], ALU.mult).then_inc(S("more_hidden"), 1)
            dve.nop()

            def final(i):
                r = ROWS[i]
                dve.wait_ge(S("final_sq"), i + 1)
                mean(A_SSQ + i, A_MS + i, 1, r, D, "final_mean")
                dve.wait_ge(S("final_rms"), i + 1)
                if i >= 2:
                    dve.wait_ge(S(f"y_final{i % 2}"), 16 * (i // 2))
                v.scalar_tensor_tensor(out=ye[0:r, i % 2, :], in0=x1[0:r, i, :], scalar=col(A_RS + i, 1, r),
                                       in1=wfb[0:r, :], op0=ALU.mult, op1=ALU.mult).then_inc(S("y_normed"), 1)

            for i in range(NT):
                r = ROWS[i]
                dve.wait_ge(S(f"chosen{i}_in"), 32)
                link(v.scalar_tensor_tensor(out=x1[0:r, i, :], in0=chosen(i, 0), scalar=rt[0:r, R_V, i, 2:3],
                                            in1=x1[0:r, i, :], op0=ALU.mult, op1=ALU.add))
                v.scalar_tensor_tensor(out=x1[0:r, i, :], in0=chosen(i, 1),
                                       scalar=rt[0:r, R_V, i, 3:4], in1=x1[0:r, i, :], op0=ALU.mult,
                                       op1=ALU.add).then_inc(S("combined"), 1)
                if i >= 1:
                    final(i - 1)
            final(NT - 1)


_INS = ['x_prompt', 'x_sample', 'cache_k_a', 'cache_v_a', 'state_gla', 'state_conv', 'state_ssm', 'norm1_w', 'w_in',
        'rel_bias_table', 'gla_w_gate_up', 'gla_b_gate', 'gla_norm_w', 'ssm_conv_w', 'ssm_conv_b', 'ssm_dt_bias',
        'ssm_a_log', 'ssm_d', 'ssm_norm_w', 'w_out', 'norm2_w', 'router_group_w', 'router_group_b',
        'router_expert_w', 'router_expert_b', 'exp_w_gate', 'exp_w_up', 'exp_w_down', 'final_norm_w']


def kernel(**inputs):
    import numpy as _np
    import concourse.bacc as _bacc
    from concourse import mybir as _mybir
    from concourse.bass_utils import run_bass_kernel_spmd as _run

    nc = _bacc.Bacc("TRN2", target_bir_lowering=False, num_devices=1)
    arrays, ins = {}, []
    for name in _INS:
        a = _np.ascontiguousarray(inputs[name])
        arrays[f"in_{name}"] = a
        ins.append(nc.dram_tensor(f"in_{name}", a.shape, _mybir.dt.from_np(a.dtype), kind="ExternalInput").ap())
    sh = {k: v.shape for k, v in inputs.items()}
    b, seq, d = sh['x_prompt']
    db, dec, _ = sh['x_sample']
    depth, _, _, ha, dh = sh['cache_k_a']
    window = 512
    shapes = [(b, seq, d), (db, dec, d),
              (depth, b, min(window, seq), ha, dh), (depth, b, min(window, seq), ha, dh),
              (depth, b) + sh['state_gla'][2:], (depth, b) + sh['state_conv'][2:], (depth, b) + sh['state_ssm'][2:],
              (depth, db, dec, ha, dh), (depth, db, dec, ha, dh),
              sh['state_gla'], sh['state_conv'], sh['state_ssm']]
    outs = [nc.dram_tensor(f"out_{i}", s, _mybir.dt.float32, kind="ExternalOutput").ap() for i, s in enumerate(shapes)]
    encoder_layer(nc, ins, outs)
    r = _run(nc, [arrays], core_ids=[0])
    return tuple(r.results[0][f"out_{i}"] for i in range(len(shapes)))
```
